# Optimizing a Trainium2 kernel written in Bass

```python
import jax, jax.numpy as jnp
from jax import lax
import numpy as np

D_MODEL = 1024
BATCH = 1
SEQ = 256
DEPTH = 2

GRID_W = 64
CTX_LEN = 256
EPS = 1e-6
ROPE_BASE = 10000.0
BLOCK = 128
A_HEADS = 8
A_KV_HEADS = 2
A_HEAD_DIM = 64
A_GROUP = A_HEADS // A_KV_HEADS
WINDOW = 128
A_Q_W = A_HEADS * A_HEAD_DIM
A_KV_W = A_KV_HEADS * A_HEAD_DIM
B_HEADS = 8
B_NOPE_DIM = 64
B_ROPE_DIM = 32
B_V_DIM = 64
B_Q_RANK = 256
B_KV_RANK = 128
B_OUT_W = B_HEADS * B_V_DIM
N_EXPERTS = 16
N_GROUPS = 4
EXPERTS_PER_GROUP = N_EXPERTS // N_GROUPS
TOP_K = 2
D_EXPERT = 512
IN_WIDTHS = (A_Q_W, A_KV_W, A_KV_W, B_Q_RANK, B_KV_RANK, B_ROPE_DIM, D_MODEL, D_MODEL)
IN_OFFSETS = tuple(int(v) for v in np.cumsum(IN_WIDTHS)[:-1])
D_IN = sum(IN_WIDTHS)

kernel_name = 'hybrid_swa_mla_grouped_moe_diffusion_trunk'

def rmsnorm(x, g):
    xf = x.astype(jnp.float32)
    y = xf * lax.rsqrt(jnp.mean(xf * xf, axis=-1, keepdims=True) + EPS)
    return (y * g.astype(jnp.float32)).astype(x.dtype)

def modulate(h, shift, scale):
    return h * (1 + scale) + shift

def rope_tables(pos, dim):
    inv = ROPE_BASE ** (-jnp.arange(0, dim, 2, dtype=jnp.float32) / dim)
    ang = pos.astype(jnp.float32)[:, None] * inv[None, :]
    return jnp.cos(ang), jnp.sin(ang)

def rope_1d(x, cos, sin):
    half = x.shape[-1] // 2
    x1, x2 = x[..., :half], x[..., half:]
    c = cos[:, None, :].astype(x.dtype)
    s = sin[:, None, :].astype(x.dtype)
    return jnp.concatenate([x1 * c - x2 * s, x1 * s + x2 * c], axis=-1)

def rope_2d(x, rows, cols):
    d = x.shape[-1] // 2
    cr, sr = rope_tables(rows, d)
    cc, sc = rope_tables(cols, d)
    return jnp.concatenate([rope_1d(x[..., :d], cr, sr), rope_1d(x[..., d:], cc, sc)], axis=-1)

def softmax_with_sink(logits, sink):
    m = jnp.maximum(jnp.max(logits, axis=-1, keepdims=True), sink)
    e = jnp.exp(logits - m)
    return e / (jnp.sum(e, axis=-1, keepdims=True) + jnp.exp(sink - m))

def project(h, w_in, q_norm, w_uq, kv_norm, w_ukv):
    B, L, _ = h.shape
    q_a, k_a, v_a, c_q, c_kv, k_r, g_a, g_b = jnp.split(h @ w_in, IN_OFFSETS, axis=-1)
    q_a = q_a.reshape(B, L, A_HEADS, A_HEAD_DIM)
    k_a = k_a.reshape(B, L, A_KV_HEADS, A_HEAD_DIM)
    v_a = v_a.reshape(B, L, A_KV_HEADS, A_HEAD_DIM)
    q_b = (rmsnorm(c_q, q_norm) @ w_uq).reshape(B, L, B_HEADS, B_NOPE_DIM + B_ROPE_DIM)
    kv_b = (rmsnorm(c_kv, kv_norm) @ w_ukv).reshape(B, L, B_HEADS, B_NOPE_DIM + B_V_DIM)
    q_n, q_r = q_b[..., :B_NOPE_DIM], q_b[..., B_NOPE_DIM:]
    k_n, v_b = kv_b[..., :B_NOPE_DIM], kv_b[..., B_NOPE_DIM:]
    return q_a, k_a, v_a, q_n, q_r, k_n, k_r, v_b, g_a, g_b

def window_gqa_latent(q, k, v, k_ctx, v_ctx, sink):
    B, S = q.shape[:2]
    nb = S // BLOCK
    scale = A_HEAD_DIM ** -0.5
    pad = ((0, 0), (BLOCK, BLOCK), (0, 0), (0, 0))
    kp, vp = jnp.pad(k, pad), jnp.pad(v, pad)
    s_sink = sink.astype(jnp.float32).reshape(A_KV_HEADS, A_GROUP)[None, :, :, None, None]
    qb = jnp.moveaxis(q.reshape(B, nb, BLOCK, A_KV_HEADS, A_GROUP, A_HEAD_DIM), 1, 0)

    def one_block(args):
        n, q_n = args
        k_b = lax.dynamic_slice_in_dim(kp, n * BLOCK, 3 * BLOCK, axis=1)
        v_b = lax.dynamic_slice_in_dim(vp, n * BLOCK, 3 * BLOCK, axis=1)
        qi = n * BLOCK + jnp.arange(BLOCK)
        kj = (n - 1) * BLOCK + jnp.arange(3 * BLOCK)
        valid = (kj[None, :] >= 0) & (kj[None, :] < S) & (jnp.abs(qi[:, None] - kj[None, :]) <= WINDOW)
        s_b = jnp.einsum('bqkgd,bjkd->bkgqj', q_n, k_b).astype(jnp.float32) * scale
        s_b = jnp.where(valid, s_b, -jnp.inf)
        s_c = jnp.einsum('bqkgd,bckd->bkgqc', q_n, k_ctx).astype(jnp.float32) * scale
        p = softmax_with_sink(jnp.concatenate([s_b, s_c], axis=-1), s_sink).astype(v.dtype)
        return (jnp.einsum('bkgqj,bjkd->bqkgd', p[..., :3 * BLOCK], v_b)
                + jnp.einsum('bkgqc,bckd->bqkgd', p[..., 3 * BLOCK:], v_ctx))

    o = lax.map(one_block, (jnp.arange(nb), qb))
    return jnp.moveaxis(o, 0, 1).reshape(B, S, A_Q_W)

def gqa_context(q, k, v, sink):
    B, C = q.shape[:2]
    qg = q.reshape(B, C, A_KV_HEADS, A_GROUP, A_HEAD_DIM)
    s = jnp.einsum('bqkgd,bckd->bkgqc', qg, k).astype(jnp.float32) * (A_HEAD_DIM ** -0.5)
    s_sink = sink.astype(jnp.float32).reshape(A_KV_HEADS, A_GROUP)[None, :, :, None, None]
    p = softmax_with_sink(s, s_sink).astype(v.dtype)
    return jnp.einsum('bkgqc,bckd->bqkgd', p, v).reshape(B, C, A_Q_W)

def mla_scores(q_n, q_r, k_n, k_r):
    s = jnp.einsum('bqhd,bkhd->bhqk', q_n, k_n) + jnp.einsum('bqhr,bkr->bhqk', q_r, k_r)
    return s.astype(jnp.float32) * ((B_NOPE_DIM + B_ROPE_DIM) ** -0.5)

def mla_latent(q_n, q_r, k_n, k_r, v, k_n_ctx, k_r_ctx, v_ctx):
    B, S = q_n.shape[:2]
    nb = S // BLOCK
    kn_all = jnp.concatenate([k_n_ctx, k_n], axis=1)
    kr_all = jnp.concatenate([k_r_ctx, k_r], axis=1)
    v_all = jnp.concatenate([v_ctx, v], axis=1)

    def blocks(t):
        return jnp.moveaxis(t.reshape(B, nb, BLOCK, *t.shape[2:]), 1, 0)

    def one_block(args):
        qn_b, qr_b = args
        p = jax.nn.softmax(mla_scores(qn_b, qr_b, kn_all, kr_all), axis=-1).astype(v_all.dtype)
        return jnp.einsum('bhqk,bkhd->bqhd', p, v_all)

    o = lax.map(one_block, (blocks(q_n), blocks(q_r)))
    return jnp.moveaxis(o, 0, 1).reshape(B, S, B_OUT_W)

def mla_context(q_n, q_r, k_n, k_r, v):
    B, C = q_n.shape[:2]
    p = jax.nn.softmax(mla_scores(q_n, q_r, k_n, k_r), axis=-1).astype(v.dtype)
    return jnp.einsum('bhqk,bkhd->bqhd', p, v).reshape(B, C, B_OUT_W)

def merge(y_a, y_b, g_a, g_b, w_o_a, w_o_b, w_out):
    return (jax.nn.sigmoid(g_a) * (y_a @ w_o_a) + jax.nn.sigmoid(g_b) * (y_b @ w_o_b)) @ w_out

def mixer(h_lat, h_ctx, rows, cols, need_ctx, w_in, sink, q_norm, w_uq, kv_norm, w_ukv, w_o_a, w_o_b, w_out):
    qa, ka, va, qn, qr, kn, kr, vb, ga, gb = project(h_lat, w_in, q_norm, w_uq, kv_norm, w_ukv)
    qa_c, ka_c, va_c, qn_c, qr_c, kn_c, kr_c, vb_c, ga_c, gb_c = project(h_ctx, w_in, q_norm, w_uq, kv_norm, w_ukv)
    qa = rope_2d(qa, rows, cols)
    ka = rope_2d(ka, rows, cols)
    qr = rope_2d(qr, rows, cols)
    kr = rope_2d(kr[:, :, None, :], rows, cols)[:, :, 0, :]
    y_a = window_gqa_latent(qa, ka, va, ka_c, va_c, sink)
    y_b = mla_latent(qn, qr, kn, kr, vb, kn_c, kr_c, vb_c)
    out_lat = merge(y_a, y_b, ga, gb, w_o_a, w_o_b, w_out)
    if not need_ctx:
        return out_lat, None
    y_a_c = gqa_context(qa_c, ka_c, va_c, sink)
    y_b_c = mla_context(qn_c, qr_c, kn_c, kr_c, vb_c)
    out_ctx = merge(y_a_c, y_b_c, ga_c, gb_c, w_o_a, w_o_b, w_out)
    return out_lat, out_ctx

def grouped_moe(h, w_router, router_bias, w_gate, w_up, w_down):
    T = h.shape[0]
    scores = jax.nn.sigmoid(h.astype(jnp.float32) @ w_router.astype(jnp.float32))
    sel = scores + router_bias.astype(jnp.float32)
    grp_score = lax.top_k(sel.reshape(T, N_GROUPS, EXPERTS_PER_GROUP), TOP_K)[0].sum(-1)
    best = jnp.argmax(grp_score, axis=-1)
    in_group = (jnp.arange(N_EXPERTS) // EXPERTS_PER_GROUP)[None, :] == best[:, None]
    _, idx = lax.top_k(jnp.where(in_group, sel, -jnp.inf), TOP_K)
    w = jnp.take_along_axis(scores, idx, axis=-1)
    w = w / jnp.sum(w, axis=-1, keepdims=True)
    gates = jnp.sum(jax.nn.one_hot(idx, N_EXPERTS, dtype=jnp.float32) * w[..., None], axis=1)

    def expert(acc, xs):
        wg, wu, wd, g = xs
        y = (jax.nn.silu(h @ wg) * (h @ wu)) @ wd
        return acc + g[:, None].astype(h.dtype) * y, None

    out, _ = lax.scan(expert, jnp.zeros_like(h), (w_gate, w_up, w_down, gates.T))
    return out

def setup_inputs(seed: int = 0) -> dict:
    key = jax.random.key(seed)
    ks = jax.random.split(key, 24)
    D = D_MODEL

    def nrm(k, shape, scale):
        return jax.random.normal(k, shape, jnp.float32) * scale

    return {
        'x': nrm(ks[0], (BATCH, SEQ, D), 1.0),
        'c': nrm(ks[1], (BATCH, D), 1.0),
        'ctx': nrm(ks[2], (BATCH, CTX_LEN, D), 1.0),
        'c_ctx': nrm(ks[3], (D,), 1.0),
        'w_mod': nrm(ks[4], (DEPTH, D, 6 * D), 0.5 * D ** -0.5),
        'b_mod': nrm(ks[5], (DEPTH, 6 * D), 0.01),
        'norm_mix': 1.0 + nrm(ks[6], (DEPTH, D), 0.02),
        'norm_ffn': 1.0 + nrm(ks[7], (DEPTH, D), 0.02),
        'w_in': nrm(ks[8], (DEPTH, D, D_IN), D ** -0.5),
        'attn_sink': nrm(ks[9], (DEPTH, A_HEADS), 0.5),
        'mla_q_norm': 1.0 + nrm(ks[10], (DEPTH, B_Q_RANK), 0.02),
        'w_uq': nrm(ks[11], (DEPTH, B_Q_RANK, B_HEADS * (B_NOPE_DIM + B_ROPE_DIM)), B_Q_RANK ** -0.5),
        'mla_kv_norm': 1.0 + nrm(ks[12], (DEPTH, B_KV_RANK), 0.02),
        'w_ukv': nrm(ks[13], (DEPTH, B_KV_RANK, B_HEADS * (B_NOPE_DIM + B_V_DIM)), B_KV_RANK ** -0.5),
        'w_o_a': nrm(ks[14], (DEPTH, A_Q_W, D), A_Q_W ** -0.5),
        'w_o_b': nrm(ks[15], (DEPTH, B_OUT_W, D), B_OUT_W ** -0.5),
        'w_out': nrm(ks[16], (DEPTH, D, D), D ** -0.5),
        'w_router': nrm(ks[17], (D, N_EXPERTS), D ** -0.5),
        'router_bias': nrm(ks[18], (N_EXPERTS,), 0.01),
        'w_expert_gate': nrm(ks[19], (DEPTH, N_EXPERTS, D, D_EXPERT), D ** -0.5),
        'w_expert_up': nrm(ks[20], (DEPTH, N_EXPERTS, D, D_EXPERT), D ** -0.5),
        'w_expert_down': nrm(ks[21], (DEPTH, N_EXPERTS, D_EXPERT, D), D_EXPERT ** -0.5),
        'final_norm': 1.0 + nrm(ks[22], (D,), 0.02),
    }

def reference(x, c, ctx, c_ctx, w_mod, b_mod, norm_mix, norm_ffn, w_in, attn_sink, mla_q_norm, w_uq,
              mla_kv_norm, w_ukv, w_o_a, w_o_b, w_out, w_router, router_bias, w_expert_gate, w_expert_up,
              w_expert_down, final_norm):
    B, S, D = x.shape
    ROWS = S // GRID_W
    rows = jnp.repeat(jnp.arange(ROWS), GRID_W)
    cols = jnp.tile(jnp.arange(GRID_W), ROWS)
    silu_c = jax.nn.silu(c)
    silu_c_ctx = jax.nn.silu(c_ctx)
    xc = ctx
    for l in range(DEPTH):
        need_ctx = l < DEPTH - 1
        sh1, sc1, g1, sh2, sc2, g2 = [m[:, None, :] for m in jnp.split(silu_c @ w_mod[l] + b_mod[l], 6, axis=-1)]
        sh1c, sc1c, g1c, sh2c, sc2c, g2c = jnp.split(silu_c_ctx @ w_mod[l] + b_mod[l], 6, axis=-1)
        h_lat = modulate(rmsnorm(x, norm_mix[l]), sh1, sc1)
        h_ctx = modulate(rmsnorm(xc, norm_mix[l]), sh1c, sc1c)
        y_lat, y_ctx = mixer(h_lat, h_ctx, rows, cols, need_ctx, w_in[l], attn_sink[l], mla_q_norm[l], w_uq[l],
                             mla_kv_norm[l], w_ukv[l], w_o_a[l], w_o_b[l], w_out[l])
        x = x + g1 * y_lat
        h_lat = modulate(rmsnorm(x, norm_ffn[l]), sh2, sc2).reshape(B * S, D)
        if need_ctx:
            xc = xc + g1c * y_ctx
            h_ctx = modulate(rmsnorm(xc, norm_ffn[l]), sh2c, sc2c).reshape(-1, D)
            f = grouped_moe(jnp.concatenate([h_lat, h_ctx], axis=0), w_router, router_bias,
                            w_expert_gate[l], w_expert_up[l], w_expert_down[l])
            x = x + g2 * f[:B * S].reshape(B, S, D)
            xc = xc + g2c * f[B * S:].reshape(xc.shape)
        else:
            f = grouped_moe(h_lat, w_router, router_bias, w_expert_gate[l], w_expert_up[l], w_expert_down[l])
            x = x + g2 * f.reshape(B, S, D)
    return rmsnorm(x, final_norm)


_drawn_inputs = setup_inputs


def setup_inputs(seed=0):
    import zlib

    import numpy as np

    out = dict(_drawn_inputs(seed))
    spreads = {}
    factors = {'norm_mix': 5.035,
     'attn_sink': 8.0,
     'mla_q_norm': 8.0,
     'mla_kv_norm': 6.508,
     'final_norm': 2.834}
    for name, (base, spread) in spreads.items():
        noise = np.random.default_rng([zlib.crc32(name.encode()), seed]).standard_normal(out[name].shape)
        drawn = base * np.exp(spread * noise) if base else spread * noise
        out[name] = __import__('jax').numpy.asarray(drawn.astype(out[name].dtype))
    for name, factor in factors.items():
        out[name] = (out[name] * factor).astype(out[name].dtype)
    return out
```

```python
from contextlib import ExitStack

import numpy as np

import concourse.bass as bass
from concourse import mybir

F32 = mybir.dt.float32
BF16 = mybir.dt.bfloat16
U32 = mybir.dt.uint32
I32 = mybir.dt.int32
ALU = mybir.AluOpType
ACT = mybir.ActivationFunctionType
AX = mybir.AxisListType

P = 128
D = 1024
KD = D // P
SEQ = 256
CTX = 256
NT = (SEQ + CTX) // P
NL = SEQ // P
DEPTH = 2
GRID_W = 64
ROPE_BASE = 10000.0
EPS = 1e-6
HEADS = 8
HD = 64
KV_A = 2
WINDOW = 128
QR, KVR, RD = 256, 128, 32
HB = HD + RD
E = 16
GROUPS = 4
F = 512
KF = F // P
CAP = P
ROUNDS = NT
BLK = 512
Z_QA, Z_KA, Z_VA, Z_CQ, Z_CKV, Z_KR, Z_END = 0, 512, 640, 768, 1024, 1152, 1184
Z_YA, Z_YB, Z_W = 0, 768, 1280
BIG = 1e30
MOD = 3 * D


def constants():
    cols, at = [], {}

    def put(name, a):
        at[name] = (sum(c.shape[1] for c in cols), a.shape[1])
        cols.append(np.asarray(a, np.float32))

    p = np.arange(P)
    put("ident", np.eye(P))
    put("tri", (p[:, None] < p[None, :]))
    put("iota", np.broadcast_to(p[None, :], (P, P)))
    for i in range(NL):
        q, k = i * P + p[:, None], (1 - i) * P + p[None, :]
        put(f"mask{i}", np.where(np.abs(q - k) <= WINDOW, 0.0, -BIG))
    for name, dim in (("a", HD // 2), ("b", RD // 2)):
        inv = (np.float32(ROPE_BASE) ** (-np.arange(0, dim, 2, dtype=np.float32) / np.float32(dim))).astype(np.float32)
        for i in range(NL):
            t = i * P + p
            parts_c, parts_s = [], []
            for pos in (t // GRID_W, t % GRID_W):
                ang = pos.astype(np.float32)[:, None] * inv[None, :]
                parts_c += [np.cos(ang), np.cos(ang)]
                parts_s += [np.sin(ang), np.sin(ang)]
            put(f"cos_{name}{i}", np.concatenate(parts_c, 1))
            put(f"sin_{name}{i}", np.concatenate(parts_s, 1))
    put("rank_g", np.broadcast_to(GROUPS - np.arange(GROUPS)[None], (P, GROUPS)))
    put("rank_e", np.broadcast_to(E - np.arange(E)[None], (P, E)))
    put("eid", np.broadcast_to(np.arange(E)[None] * CAP, (P, E)))
    for i in range(NT):
        put(f"tok{i}", np.stack([p, np.full(P, i * P)], 1))
    put("minus_half", np.full((P, 8), -0.5))
    return np.concatenate(cols, 1), at


CONST, AT = constants()
NCONST = CONST.shape[1]


def trunk(nc, a, const_in, out):
    with ExitStack() as ctx:
        def sb(name, shape, dt=F32):
            return ctx.enter_context(nc.sbuf_tensor(name, shape, dt))

        def sem(name):
            return ctx.enter_context(nc.semaphore(name))

        def dram(name, shape, dt=F32):
            return nc.dram_tensor(name, shape, dt).ap()

        mod_dram = dram("mod_rows", (DEPTH, 2, 2, MOD))
        h_dram = dram("h_rows", (NT * P, D))
        y_dram = dram("y_rows", (E * CAP, D))

        const = sb("const", [P, NCONST])

        def cst(name):
            o, n = AT[name]
            return const[:, o:o + n]

        ident = cst("ident")
        x = sb("x_tok", [P, NT, D])
        hT = sb("hT", [P, KD, NT * P])
        wslot = [sb(f"wslot{s}", [P, KD * BLK]) for s in range(3)]
        modbc = sb("modbc", [P, 2, MOD])
        z = sb("z", [P, NT, Z_W])
        arena = sb("arena", [P, 17408])

        def carve(o, n, dt=F32):
            return arena[:, o:o + n]

        qaT = carve(0, 2048).rearrange("p (c t) -> p c t", c=4)
        kaT = carve(2048, 1024).rearrange("p (c t) -> p c t", c=2)
        vb = carve(3072, 2048).rearrange("p (i n) -> p i n", i=NT)
        qbT = carve(5120, 4096).rearrange("p (h t) -> p h t", h=HEADS)
        kbT = carve(9216, 4096).rearrange("p (h t) -> p h t", h=HEADS)
        rope_c = carve(13312, 640)
        rope_s = carve(13952, 640)
        zq = carve(14592, 768)
        kcat = carve(15360, 768)
        kdup = carve(16128, 256)
        cn = carve(16384, 384)
        cT = carve(16768, 384).rearrange("p (c t) -> p c t", c=3)
        prob = [carve(13312 + 512 * j, 512) for j in range(3)]
        pT = [carve(14848 + 512 * j, 512).rearrange("p (c t) -> p c t", c=4) for j in range(2)]
        yT = carve(5120, 4096).rearrange("p (b c t) -> p b c t", b=2, c=4)
        mix = carve(9216, 4096).rearrange("p (i n) -> p i n", i=NT)
        sg = [carve(13312 + 512 * j, 512) for j in range(2)]
        pg = [carve(14336 + 512 * j, 512) for j in range(2)]
        htok = [carve(1024 * j, 1024) for j in range(2)]
        junk = carve(2048, 1024)
        xg = carve(4096, 1024)
        xgT = carve(5120, 1024).rearrange("p (k t) -> p k t", k=KD)
        tg = carve(6144, 512)
        au = carve(6656, 512)
        auT = carve(7168, 512).rearrange("p (k t) -> p k t", k=KF)
        ysb = carve(7680, 1024)
        y1 = [carve(8704 + 2048 * j, 1024) for j in range(2)]
        y2 = [carve(9728 + 2048 * j, 1024) for j in range(2)]
        rt = sb("rt", [P, 1600])
        oh = carve(13312, E * CAP).rearrange("p (j n) -> p j n", j=2)
        ohb = [oh[:, j].bitcast(BF16).rearrange("p (e s) -> p e s", e=E) for j in range(2)]
        small = sb("small", [P, 96])
        bf = sb("bf", [P, 2 * P + NT * E + 2 * NT], BF16)
        tri_b, ones_b = bf[:, 0:P], bf[:, P:2 * P]
        m_b = bf[:, 2 * P:2 * P + NT * E].rearrange("p (i e) -> p i e", e=E)
        tok_b = bf[:, 2 * P + NT * E:].rearrange("p (i c) -> p i c", c=2)
        idx = sb("idx", [P, E], U32)
        row = sb("row", [P, 2, NT], U32)
        idxc = sb("idxc", [P, 1], U32)
        more = sb("more", [1, 1], I32)
        sinks = sb("sinks", [P, 2 * HEADS])
        lora = sb("lora", [P, QR + KVR])
        wr = sb("wr", [P, KD, E])
        rbias = sb("rbias", [P, E])
        cvec = sb("cvec", [P, 2, KD])
        cth = sb("cth", [P, 2, KD])
        mrow = z[0:2, :, :].rearrange("p i n -> p (i n)")[:, 0:MOD]
        brow = hT[0:2, :, :].rearrange("p i n -> p (i n)")[:, 0:MOD]
        grow = arena[0:2, 0:D]
        trow = arena[0:2, D:D + BLK]

        bank = [ctx.enter_context(nc.psum_tensor(f"bank{j}", [P, BLK], F32)) for j in range(8)]

        s_stage = sem("stage_end")
        w_full = [sem(f"w_full{s}") for s in range(3)]
        w_used = [sem(f"w_used{s}") for s in range(3)]
        s_const = sem("const_in")
        s_c = sem("c_in")
        s_x = sem("x_in")
        s_cs = sem("silu_c")
        s_brow = sem("bias_row_in")
        s_mevac = sem("mod_evac")
        s_mrow = sem("mod_row_out")
        s_link = sem("dve_link")
        counts = dict(
            modbc=32, ss=2 * NT, var=2, rstd=2, h=2 * NT, tr=4 * NT, hev=4 * NT, lorain=64, p=3 * NT, pev=3 * NT,
            rz=NT, rcv=NT, rcr=NT, rcn=NT, rt1=NT, rt2=NT, rp=NT, rpev=NT, rq=NT, rqT=NT, rqe=NT,
            sc=2 * NT * HEADS, nm=2 * NT * HEADS, ex=2 * NT * HEADS, pt=2 * NT * HEADS, pte=2 * NT * HEADS,
            pv=2 * NT * HEADS, nms=NT, es=NT, yev=2 * NT, yt=2 * NT, yte=2 * NT, o=6 * NT, sg=4 * NT, m=2 * NT,
            mt=2 * NT, mte=2 * NT, wo=2 * NT, xup=2 * NT, hst0=8 * NT, hst1=8 * NT, lg=1, lge=1, rb=1, pos=1,
            ohr=NT, ix=NT, gat=16 * E, xt=E, xte=2 * E, th=E, aug=E, au=E, at=E, ate=E, ye=2 * E, yst=16 * E,
            g00=8 * NT, g01=8 * NT, g10=8 * NT, g11=8 * NT, f=NT)
        signals = {n: sem(n) for n in counts}

        class Layer:

            def __init__(self, l):
                self.l = l

            def __getitem__(self, name):
                return signals[name]

            def at(self, name, n):
                return signals[name], n + self.l * counts[name]

        L = [Layer(l) for l in range(DEPTH)]
        s_out = sem("out_dma")
        s_fin = sem("final")

        s_cs2 = sem("tanh_c")
        s_mt = sem("scale_row")
        s_wr = sem("router_in")
        s_x2 = sem("ctx_in")
        s_lora_w = [sem(f"w_ukv_in_{l}") for l in range(DEPTH)]
        s_ob_w = [sem(f"w_o_b_in_{l}") for l in range(DEPTH)]
        s_passed = sem("step_passed")
        s_more = [sem(f"more_step_{l}") for l in range(DEPTH)]
        s_xw = [sem(f"more_weights_in_{l}") for l in range(DEPTH)]
        s_xg = [sem(f"more_rows_in_{l}") for l in range(DEPTH)]
        s_xy = [sem(f"more_results_out_{l}") for l in range(DEPTH)]
        s_xc = [sem(f"more_results_in_{l}") for l in range(DEPTH)]
        s_fvar, s_frs, s_fn, s_fout = sem("final_var"), sem("final_rstd"), sem("final_norm_in"), sem("final_out")

        block = ctx.enter_context(nc.Block())
        stages = {}

        def barrier(name, eng):
            n = stages[name] = stages.get(name, 0) + 1
            eng.drain().then_inc(s_stage, 1)
            eng.wait_ge(s_stage, 4 * n)

        links = [0]

        def link(dve, ins):
            links[0] += 1
            ins.then_inc(s_link, 1)
            dve.wait_ge(s_link, links[0])

        def tiles(l):
            return range(NT) if l < DEPTH - 1 else range(NL)

        def kind(i):
            return 0 if i < NL else 1

        MOD_PER_SLOT = DEPTH * 12 // 3
        BLOCKS = 12

        def slot_of(l, b):
            return b % 3, MOD_PER_SLOT + l * (BLOCKS // 3 + E) + b // 3 + 1

        def moe_base(l):
            return MOD_PER_SLOT + l * (BLOCKS // 3 + E) + BLOCKS // 3

        def used_base(l):
            return MOD_PER_SLOT + l * E

        def w_view(s, n=BLK):
            return wslot[s][:, 0:KD * n].rearrange("p (k n) -> p k n", k=KD)

        wd_view = wslot[2][:, :].rearrange("p (k n) -> p k n", k=KF)

        def in_jobs(l):
            T = tiles(l)
            jobs = [(0, i, 0, 512) for i in T]
            jobs += [(1, i, 512, 512 if i in T else 256) for i in range(NT)]
            return jobs + [(2, i, 1024, 160) for i in range(NT)]

        def attention_units(l):
            groups = [(br, i) for br in range(2) for i in tiles(l)]
            return [(g, br, i, h, 0 if i < NL else NL, NT if i < NL else NT - NL)
                    for g, (br, i) in enumerate(groups) for h in range(HEADS)]

        def att_scale(br):
            return (HD if br == 0 else HB) ** -0.5

        def nm_at(g):
            return 24 + (g % 2) * 8

        def read_pT(act, S, units, u):
            g, br, i, h, k0, nk = units[u]
            act.wait_ge(*S.at("pt", u + 1))
            if u >= 2:
                act.wait_ge(*S.at("pv", u - 1))
            act.copy(pT[u % 2][:, 0:nk, :], bank[3 + u % 2][:, 0:nk * P].rearrange("p (c t) -> p c t", c=nk)
                     ).then_inc(S["pte"], 1)

        def rcol(o, n):
            return rt[:, o:o + n]

        r_sc = rcol(0, NT * E)
        r_w = rcol(1500, 2 * NT).rearrange("p (c i) -> p c i", c=2)
        r_wm = rcol(1508, 2 * NT).rearrange("p (c i) -> p c i", c=2)

        def route(dve, lk, S, T):
            n = len(T)
            ne = n * E

            def by_tile(v, m=E):
                return v.rearrange("p (i e) -> p i e", i=n)

            def over(v, m):
                return v.unsqueeze(2).to_broadcast([P, v.shape[1], m])

            sc, sel, ms, w, t = (rcol(64 * j, ne) for j in (0, 1, 2, 3, 4))
            o1, o2 = rcol(320, ne), rcol(384, ne)
            mf, posm, pos = rcol(448, ne), rcol(512, ne), rcol(576, ne)
            pair = rcol(640, n * GROUPS * 6).rearrange("p (g c) -> p g c", c=6)
            gs, w4, pen = rcol(740, n * GROUPS), rcol(756, n * GROUPS), rcol(772, n * GROUPS)
            gm = rcol(788, n)
            m1 = rcol(792, n)
            ssum = rcol(796, 2 * n)
            den = rcol(804, n)
            bE = [P, n, E]
            dve.wait_ge(*S.at("lge", 1))
            dve.wait_ge(s_wr, 32)
            lk(dve.tensor_scalar(sc, sc, 0.5, 0.5, ALU.mult, ALU.add))
            lk(dve.tensor_tensor(by_tile(sel), by_tile(sc), rbias[:, :].unsqueeze(1).to_broadcast(bE), ALU.add))
            g4 = sel.rearrange("p (g c) -> p g c", c=4)
            dve.tensor_tensor(pair[:, :, 0:3], g4[:, :, 0:3], g4[:, :, 1:4], ALU.add)
            dve.tensor_tensor(pair[:, :, 3:5], g4[:, :, 0:2], g4[:, :, 2:4], ALU.add)
            lk(dve.tensor_tensor(pair[:, :, 5:6], g4[:, :, 0:1], g4[:, :, 3:4], ALU.add))
            lk(dve.tensor_reduce(gs, pair, AX.X, ALU.max))
            lk(dve.tensor_reduce(gm, by_tile(gs), AX.X, ALU.max))
            lk(dve.tensor_tensor(by_tile(w4), by_tile(gs), over(gm, GROUPS), ALU.is_equal))
            lk(dve.tensor_tensor(by_tile(w4), by_tile(w4),
                                 cst("rank_g").unsqueeze(1).to_broadcast([P, n, GROUPS]), ALU.mult))
            lk(dve.tensor_reduce(gm, by_tile(w4), AX.X, ALU.max))
            lk(dve.tensor_tensor(by_tile(w4), by_tile(w4), over(gm, GROUPS), ALU.is_equal))
            lk(dve.tensor_scalar(pen, w4, -1.0, BIG, ALU.add, ALU.mult))
            lk(dve.tensor_tensor(ms.rearrange("p (g c) -> p g c", c=4), g4, over(pen, 4), ALU.add))
            for c, o in enumerate((o1, o2)):
                lk(dve.tensor_reduce(m1, by_tile(ms), AX.X, ALU.max))
                lk(dve.tensor_tensor(by_tile(w), by_tile(ms), over(m1, E), ALU.is_equal))
                lk(dve.tensor_tensor(by_tile(w), by_tile(w), cst("rank_e").unsqueeze(1).to_broadcast(bE), ALU.mult))
                lk(dve.tensor_reduce(m1, by_tile(w), AX.X, ALU.max))
                lk(dve.tensor_tensor(by_tile(o), by_tile(w), over(m1, E), ALU.is_equal))
                lk(dve.tensor_tensor(t, o, sc, ALU.mult))
                lk(dve.tensor_reduce(ssum[:, c * n:(c + 1) * n], by_tile(t), AX.X, ALU.add))
                if c == 0:
                    lk(dve.scalar_tensor_tensor(out=ms, in0=o, scalar=-3 * BIG, in1=ms, op0=ALU.mult, op1=ALU.add))
            lk(dve.tensor_tensor(mf, o1, o2, ALU.add))
            dve.tensor_copy(m_b[:, 0:n, :], by_tile(mf)).then_inc(S["rb"], 1)
            lk(dve.tensor_tensor(den, ssum[:, 0:n], ssum[:, n:2 * n], ALU.add))
            lk(dve.reciprocal(den, den))
            for c in range(2):
                dve.scalar_tensor_tensor(out=r_w[:, c, 0:n], in0=ssum[:, c * n:(c + 1) * n], scalar=0.5,
                                         in1=den, op0=ALU.mult, op1=ALU.mult)
            dve.wait_ge(*S.at("pos", 1))
            lk(dve.tensor_copy(pos, bank[1][:, 0:ne]))
            lk(dve.scalar_tensor_tensor(out=posm, in0=pos, scalar=1.0, in1=mf, op0=ALU.add, op1=ALU.mult))
            lk(dve.tensor_scalar(posm, posm, -1.0, None, ALU.add))
            for c, o in enumerate((o1, o2)):
                lk(dve.tensor_tensor(t, o, pos, ALU.mult))
                lk(dve.tensor_reduce(r_place[:, c, 0:n], by_tile(t), AX.X, ALU.add))
                lk(dve.tensor_tensor(by_tile(t), by_tile(o), cst("eid").unsqueeze(1).to_broadcast(bE), ALU.mult))
                lk(dve.tensor_reduce(r_first[:, c, 0:n], by_tile(t), AX.X, ALU.add))
            lk(dve.tensor_reduce(r_more[:, 0:1], bank[1][:, ne:ne + E], AX.X, ALU.max))
            lk(dve.tensor_scalar(r_more[:, 1:2], r_more[:, 0:1], CAP + 0.5, None, ALU.is_gt))
            for r in range(2, ROUNDS):
                lk(dve.scalar_tensor_tensor(out=r_more[:, 1:2], in0=r_more[:, 0:1], scalar=r * CAP + 0.5,
                                            in1=r_more[:, 1:2], op0=ALU.is_gt, op1=ALU.add))
            dve.tensor_copy(more[:, :], r_more[0:1, 1:2])
            for j in range(n):
                if j >= 2:
                    dve.wait_ge(*S.at("ix", j - 1))
                one_hots(dve, n, j).then_inc(S["ohr"], 1)
            places(dve, lk, n)
            dve.wait_ge(*S.at("ix", n))
            lists(dve, lk, n)

        r_posm = rcol(512, NT * E)
        r_place = rcol(900, 2 * NT).rearrange("p (c i) -> p c i", c=2)
        r_first = rcol(908, 2 * NT).rearrange("p (c i) -> p c i", c=2)
        r_more = rcol(920, 2)

        def one_hots(dve, n, j):
            return dve.tensor_tensor(ohb[j % 2], cst("iota").unsqueeze(1).to_broadcast([P, E, P]),
                                     r_posm[:, j * E:(j + 1) * E].unsqueeze(2).to_broadcast([P, E, P]), ALU.is_equal)

        def places(dve, lk, n):
            for c in range(2):
                place, clamped = r_place[:, c, 0:n], rcol(930, n)
                lk(dve.tensor_scalar(clamped, place, 0.0, CAP - 1.0, ALU.max, ALU.min))
                lk(dve.tensor_tensor(rcol(936, n), clamped, place, ALU.is_equal))
                lk(dve.tensor_tensor(r_wm[:, c, 0:n], r_w[:, c, 0:n], rcol(936, n), ALU.mult))
                lk(dve.tensor_tensor(clamped, clamped, r_first[:, c, 0:n], ALU.add))
                lk(dve.tensor_copy(row[:, c, 0:n], clamped))

        def lists(dve, lk, n):
            acc, acc2 = rcol(824, E), rcol(840, E)
            for j in range(n):
                lk(dve.tensor_reduce(acc2 if j else acc, bank[2 + j][:, 0:2 * E].rearrange("p (e c) -> p e c", c=2),
                                     AX.X, ALU.add))
                if j:
                    lk(dve.tensor_tensor(acc, acc, acc2, ALU.add))
            lk(dve.tensor_copy(idx[:, :], acc))

        def combine(dve, lk, l, n, i):
            a1, a2 = y1[n % 2], y2[n % 2]
            lk(dve.tensor_scalar(a1, a1, r_wm[:, 0, n:n + 1], None, ALU.mult))
            lk(dve.scalar_tensor_tensor(out=a1, in0=a2, scalar=r_wm[:, 1, n:n + 1], in1=a1,
                                        op0=ALU.mult, op1=ALU.add))
            lk(dve.tensor_tensor(a1, a1, modbc[:, kind(i), 2 * D:3 * D], ALU.mult))
            return dve.tensor_tensor(x[:, i, :], x[:, i, :], a1, ALU.add)

        xw_gate = hT
        xw_up = z[:, :, :].rearrange("p i n -> p (i n)")[:, 0:KD * BLK].rearrange("p (k n) -> p k n", k=KD)
        xw_down = carve(12800, KF * D).rearrange("p (k n) -> p k n", k=KF)
        EXPERT_STEPS = 12

        def more_rounds(name, eng, l):
            T = tiles(l)
            n = len(T)
            steps = 2 * n + 1 + E * EXPERT_STEPS + 2 * n
            count = eng.value_load(more[0:1, 0:1], min_val=0, max_val=ROUNDS - 1)
            with eng.If(count > 0):
                with eng.Fori(0, count) as r:
                    done = [0]

                    def step(e=None):
                        done[0] += 1
                        eng.drain().then_inc(s_more[l], 1)
                        if e is None:
                            eng.wait_ge(s_more[l], r * (4 * steps) + 4 * done[0])
                        else:
                            eng.wait_ge(s_more[l], r * (4 * steps) + e * (4 * EXPERT_STEPS) + 4 * done[0])
                        eng.sem_inc(s_passed, 1)

                    for j in range(n):
                        if name == "dve":
                            if j == 0:
                                eng.tensor_scalar(r_posm[:, 0:n * E], r_posm[:, 0:n * E], -float(CAP), None, ALU.add)
                                eng.tensor_scalar(r_place[:, :, 0:n], r_place[:, :, 0:n], -float(CAP), None, ALU.add)
                                eng.drain()
                            one_hots(eng, n, j)
                        step()
                        if name == "pe":
                            for e in range(E):
                                eng.matmul(bank[2 + j][:, 2 * e:2 * e + 2], ohb[j % 2][:, e, :], tok_b[:, T[j], :],
                                           start=True, stop=True)
                        step()
                    if name == "dve":
                        drained = lambda ins: eng.drain()
                        places(eng, drained, n)
                        lists(eng, drained, n)
                    step()
                    before = done[0]
                    with eng.Fori(0, E) as e:
                        if name == "dve":
                            eng.tensor_copy(idxc[:, :], idx[:, bass.ds(e, 1)])
                        if name == "pool":
                            for dst, w in ((xw_gate, "w_expert_gate"), (xw_up, "w_expert_up"),
                                           (xw_down, "w_expert_down")):
                                eng.dma_start(dst[:, :, :], a[w][l].rearrange("e (k p) n -> e p k n", p=P)[
                                    bass.ds(e, 1)].rearrange("e p k n -> p (e k) n")).then_inc(s_xw[l], 16)
                        step(e)
                        if name == "pool":
                            eng.indirect_dma_start(out=xg, out_offset=None, in_=h_dram,
                                                   in_offset=bass.IndirectOffsetOnAxis(ap=idxc[:, :], axis=0)
                                                   ).then_inc(s_xg[l], 16)
                            eng.wait_ge(s_xg[l], r * (16 * E) + e * 16 + 16)
                            eng.wait_ge(s_xw[l], r * (48 * E) + e * 48 + 48)
                            eng.sem_inc(s_passed, 1)
                        step(e)
                        if name == "pe":
                            for k in range(KD):
                                eng.transpose(bank[k // 4][:, (k % 4) * P:(k % 4 + 1) * P],
                                              xg[:, k * P:(k + 1) * P], ident)
                        step(e)
                        for c, who in enumerate(("act", "dve")):
                            if name == who:
                                (eng.copy if c == 0 else eng.tensor_copy)(
                                    xgT[:, 4 * c:4 * c + 4, :], bank[c][:, :].rearrange("p (k t) -> p k t", k=4))
                        step(e)
                        if name == "pe":
                            for c, w in enumerate((xw_gate, xw_up)):
                                for k in range(KD):
                                    eng.matmul(bank[2 + c][:, :], xgT[:, k, :], w[:, k, :], start=k == 0,
                                               stop=k == KD - 1)
                        step(e)
                        if name == "act":
                            eng.activation(tg, bank[2][:, :], ACT.Tanh, scale=0.5)
                        step(e)
                        if name == "dve":
                            eng.scalar_tensor_tensor(out=au, in0=tg, scalar=1.0, in1=bank[2][:, :],
                                                     op0=ALU.add, op1=ALU.mult)
                            eng.drain()
                            eng.tensor_tensor(au, au, bank[3][:, :], ALU.mult)
                        step(e)
                        if name == "pe":
                            for k in range(KF):
                                eng.transpose(bank[4][:, k * P:(k + 1) * P], au[:, k * P:(k + 1) * P], ident)
                        step(e)
                        if name == "act":
                            eng.copy(auT[:, :, :], bank[4][:, :].rearrange("p (k t) -> p k t", k=4))
                        step(e)
                        if name == "pe":
                            for c in range(2):
                                for k in range(KF):
                                    eng.matmul(bank[5 + c][:, :], auT[:, k, :], xw_down[:, k, c * BLK:(c + 1) * BLK],
                                               start=k == 0, stop=k == KF - 1)
                        step(e)
                        if name == "act":
                            eng.copy(ysb[:, 0:BLK], bank[5][:, :])
                        if name == "dve":
                            eng.tensor_copy(ysb[:, BLK:D], bank[6][:, :])
                        step(e)
                        if name == "pool":
                            eng.dma_start(y_dram[bass.ds(e * CAP, CAP), :], ysb).then_inc(s_xy[l], 16)
                            eng.wait_ge(s_xy[l], r * (16 * E) + e * 16 + 16)
                            eng.sem_inc(s_passed, 1)
                        step(e)
                    assert done[0] - before == EXPERT_STEPS
                    done[0] = before + E * EXPERT_STEPS
                    for j, i in enumerate(T):
                        if name == "pool":
                            for c, dst in enumerate((y1[j % 2], y2[j % 2])):
                                eng.indirect_dma_start(out=dst, out_offset=None, in_=y_dram,
                                                       in_offset=bass.IndirectOffsetOnAxis(ap=row[:, c, j:j + 1],
                                                                                           axis=0)
                                                       ).then_inc(s_xc[l], 16)
                            eng.wait_ge(s_xc[l], r * (32 * n) + 32 * (j + 1))
                            eng.sem_inc(s_passed, 1)
                        step()
                        if name == "dve":
                            combine(eng, lambda ins: eng.drain(), l, j, i)
                        step()

        B_IN, B_LORA, B_GA, B_GB, B_O, B_OUT = (0, 1, 2), 3, (4, 7), (5, 8), (6, 9), (10, 11)
        IN_COLS = ((0, 512), (512, 512), (1024, 160))
        uq_w = wslot[0][:, 0:2 * 768].rearrange("p (k n) -> p k n", k=2)
        ukv_w = wslot[0][:, 1536:1536 + D]

        @block.sync
        def _(sp):
            for l in range(DEPTH):
                for b in range(12):
                    s = b % 3
                    if l or b >= 3:
                        sp.wait_ge(w_used[s], l * 4 + b // 3)
                    sp.dma_start(w_view(s), a["w_mod"][l].rearrange("(p k) n -> p k n", k=KD)[
                        :, :, b * BLK:(b + 1) * BLK]
                    ).then_inc(w_full[s], 16)

            def wait_block_used(l, b):
                prev, s = b - 3, b % 3
                if prev < 0:
                    sp.wait_ge(w_used[s], used_base(l))
                    return
                S, n = L[l], len(tiles(l))
                if prev in B_IN:
                    sp.wait_ge(*S.at("p", sum(j[0] <= prev for j in in_jobs(l))))
                elif prev == B_LORA:
                    sp.wait_ge(*S.at("rp", NT))
                elif prev in B_OUT:
                    sp.wait_ge(*S.at("wo", n * (B_OUT.index(prev) + 1)))
                else:
                    half, part = divmod(prev - 4, 3)
                    sp.wait_ge(*S.at("o", 3 * (n * (half + 1) - 1) + part + 1))

            def cols(w, o, n):
                return w.rearrange("(k p) n -> p k n", p=P)[:, :, o:o + n]

            for l in range(DEPTH):
                w_in = a["w_in"][l]
                for b in range(BLOCKS):
                    s, n = slot_of(l, b)
                    wait_block_used(l, b)
                    if b in B_IN:
                        o, w = IN_COLS[b]
                        sp.dma_start(w_view(s, w), cols(w_in, o, w)).then_inc(w_full[s], 16)
                    elif b == B_LORA:
                        sp.dma_start(uq_w, a["w_uq"][l].rearrange("(k p) n -> p k n", p=P)).then_inc(w_full[s], 16)
                        sp.dma_start(ukv_w, a["w_ukv"][l]).then_inc(s_lora_w[l], 16)
                    elif b in B_GA or b in B_GB:
                        half = 0 if b < 7 else 1
                        o = Z_END + (0 if b in B_GA else D) + half * BLK
                        sp.dma_start(w_view(s), cols(w_in, o, BLK)).then_inc(w_full[s], 16)
                    elif b in B_O:
                        half = B_O.index(b)
                        v = w_view(s)
                        sp.dma_start(v[:, 0:4], cols(a["w_o_a"][l], half * BLK, BLK)).then_inc(w_full[s], 16)
                        sp.dma_start(v[:, 4:8], cols(a["w_o_b"][l], half * BLK, BLK)).then_inc(s_ob_w[l], 16)
                    else:
                        sp.dma_start(w_view(s), cols(a["w_out"][l], B_OUT.index(b) * BLK, BLK)).then_inc(w_full[s], 16)

                def load_expert(s, e):
                    w = a[("w_expert_gate", "w_expert_up", "w_expert_down")[s]][l]
                    src = w.rearrange("e (k p) n -> e p k n", p=P)[bass.ds(e, 1)].rearrange("e p k n -> p (e k) n")
                    sp.dma_start(w_view(s) if s < 2 else wd_view, src).then_inc(w_full[s], 16)

                def next_expert(s, e):
                    sp.wait_ge(w_used[s], e + used_base(l))
                    load_expert(s, e)

                for s in range(3):
                    wait_block_used(l, BLOCKS + s)
                    load_expert(s, 0)
                next_expert(0, 1)
                next_expert(1, 1)
                with sp.Fori(2, E) as e:
                    next_expert(0, e)
                    next_expert(1, e)
                    next_expert(2, e - 1)
                next_expert(2, E - 1)

        @block.tensor
        def _(pe):
            def product(dst, lhs, rhs, n, first=True, last=True):
                for k in range(n):
                    ins = pe.matmul(dst, lhs(k), rhs(k), start=first and k == 0, stop=last and k == n - 1)
                return ins

            pe.wait_ge(s_cs, 1)
            for l in range(DEPTH):
                for b in range(12):
                    s = b % 3
                    pe.wait_ge(w_full[s], (l * 4 + b // 3 + 1) * 16)
                    if l or b >= 6:
                        pe.wait_ge(s_mevac, l * 12 + b - 5)
                    w = w_view(s)
                    product(bank[b % 6][0:2, :], lambda k: cvec[:, :, k], lambda k: w[:, k, :], KD
                            ).then_inc(w_used[s], 1)
            barrier("pe", pe)

            def transposes_of_h(S, ts, base):
                for j, i in enumerate(ts):
                    pe.wait_ge(*S.at("h", base + j + 1))
                    if base + j >= 2:
                        pe.wait_ge(*S.at("hev", 2 * (base + j - 1)))
                    for k in range(KD):
                        ins = pe.transpose(bank[2 * (j % 2) + k // 4][:, (k % 4) * P:(k % 4 + 1) * P],
                                           htok[j % 2][:, k * P:(k + 1) * P], ident)
                        if k % 4 == 3:
                            ins.then_inc(S["tr"], 1)

            for l in range(DEPTH):
                S = L[l]
                T = tiles(l)
                transposes_of_h(S, range(NT), 0)
                barrier("pe", pe)
                jobs = in_jobs(l)
                for n, (b, i, o, w) in enumerate(jobs):
                    s, full = slot_of(l, B_IN[b])
                    pe.wait_ge(w_full[s], 16 * full)
                    if n >= 8:
                        pe.wait_ge(*S.at("pev", n - 7))
                    wv = w_view(s, IN_COLS[b][1])
                    ins = product(bank[n % 8][:, 0:w], lambda k: hT[:, k, i * P:(i + 1) * P],
                                  lambda k: wv[:, k, 0:w], KD)
                    ins.then_inc(S["p"], 1)
                barrier("pe", pe)
                s, full = slot_of(l, B_LORA)
                for i in range(NT):
                    q = i in T
                    pe.wait_ge(*S.at("rcn", i + 1))
                    if i:
                        pe.wait_ge(*S.at("rqe", i))
                    for c in range(3):
                        ins = pe.transpose(bank[0][:, c * P:(c + 1) * P], cn[:, c * P:(c + 1) * P], ident)
                    ins.then_inc(S["rt1"], 1)
                    pe.wait_ge(*S.at("rt2", i + 1))
                    if i == 0:
                        pe.wait_ge(w_full[s], 16 * full)
                        pe.wait_ge(s_lora_w[l], 16)
                    if q:
                        product(bank[1][:, :], lambda k: cT[:, k, :], lambda k: uq_w[:, k, 0:512], 2)
                        product(bank[2][:, 0:256], lambda k: cT[:, k, :], lambda k: uq_w[:, k, 512:768], 2)
                    product(bank[3][:, :], lambda k: cT[:, 2, :], lambda k: ukv_w[:, 0:512], 1)
                    ins = product(bank[4][:, :], lambda k: cT[:, 2, :], lambda k: ukv_w[:, 512:1024], 1)
                    ins.then_inc(S["rp"], 1)
                    pe.wait_ge(*S.at("rq", i + 1))
                    if q:
                        for c in range(4):
                            pe.transpose(bank[5][:, c * P:(c + 1) * P], z[:, i, c * P:(c + 1) * P], ident)
                        for h in range(HEADS):
                            pe.transpose(bank[6 + h // 4][0:HB, (h % 4) * P:(h % 4 + 1) * P],
                                         zq[:, h * HB:(h + 1) * HB], ident)
                    for c in range(2):
                        pe.transpose(bank[0][:, c * P:(c + 1) * P], kdup[:, c * P:(c + 1) * P], ident)
                    for h in range(HEADS):
                        ins = pe.transpose(bank[1 + h // 4][0:HB, (h % 4) * P:(h % 4 + 1) * P],
                                           kcat[:, h * HB:(h + 1) * HB], ident)
                    ins.then_inc(S["rqT"], 1)
                barrier("pe", pe)
                units = attention_units(l)

                def scores(u):
                    g, br, i, h, k0, nk = units[u]
                    if u >= 3:
                        pe.wait_ge(*S.at("ex", u - 2))
                    sl = slice(k0 * P, NT * P)
                    if br == 0:
                        r = slice((h % 2) * HD, (h % 2 + 1) * HD)
                        lhs, rhs = qaT[r, h // 2, i * P:(i + 1) * P], kaT[r, h // 4, sl]
                    else:
                        lhs, rhs = qbT[0:HB, h, i * P:(i + 1) * P], kbT[0:HB, h, sl]
                    pe.matmul(bank[u % 3][:, 0:nk * P], lhs, rhs, start=True, stop=True).then_inc(S["sc"], 1)

                def turn(u):
                    g, br, i, h, k0, nk = units[u]
                    pe.wait_ge(*S.at("ex", u + 1))
                    if u >= 2:
                        pe.wait_ge(*S.at("pte", u - 1))
                    for c in range(nk):
                        ins = pe.transpose(bank[3 + u % 2][:, c * P:(c + 1) * P],
                                           prob[u % 3][:, c * P:(c + 1) * P], ident)
                    ins.then_inc(S["pt"], 1)

                def values(u):
                    g, br, i, h, k0, nk = units[u]
                    pe.wait_ge(*S.at("pte", u + 1))
                    if h == 0 and g >= 2:
                        pe.wait_ge(*S.at("yev", g - 1))
                    for c in range(nk):
                        v = (z[:, k0 + c, Z_VA + (h // 4) * HD:Z_VA + (h // 4 + 1) * HD] if br == 0
                             else vb[:, k0 + c, h * HD:(h + 1) * HD])
                        ins = pe.matmul(bank[5 + g % 2][:, h * HD:(h + 1) * HD], pT[u % 2][:, c, :], v,
                                        start=c == 0, stop=c == nk - 1)
                    ins.then_inc(S["pv"], 1)

                for u in range(len(units) + 3):
                    if u < len(units):
                        scores(u)
                    if 2 <= u < len(units) + 2:
                        turn(u - 2)
                    if u >= 3:
                        values(u - 3)
                barrier("pe", pe)
                for n, i in enumerate(T):
                    if n >= 2:
                        pe.wait_ge(*S.at("yte", 2 * (n - 1)))
                    for br, o in ((0, Z_YA), (1, Z_YB)):
                        for c in range(4):
                            ins = pe.transpose(bank[2 * (n % 2) + br][:, c * P:(c + 1) * P],
                                               z[:, i, o + c * P:o + (c + 1) * P], ident)
                        ins.then_inc(S["yt"], 1)
                barrier("pe", pe)
                n = 0
                for half in range(2):
                    for i in T:
                        sa, fa = slot_of(l, B_GA[half])
                        sb_, fb = slot_of(l, B_GB[half])
                        so, fo = slot_of(l, B_O[half])
                        h_at = lambda k: hT[:, k, i * P:(i + 1) * P]
                        wa, wb, wo = w_view(sa), w_view(sb_), w_view(so)
                        q = 4 * (n % 2)
                        if n >= 2:
                            pe.wait_ge(*S.at("m", n - 1))
                        pe.wait_ge(w_full[sa], 16 * fa)
                        ins = product(bank[q][:, :], h_at, lambda k: wa[:, k, :], KD)
                        ins.then_inc(S["o"], 1)
                        pe.wait_ge(w_full[sb_], 16 * fb)
                        ins = product(bank[q + 1][:, :], h_at, lambda k: wb[:, k, :], KD)
                        ins.then_inc(S["o"], 1)
                        pe.wait_ge(w_full[so], 16 * fo)
                        pe.wait_ge(s_ob_w[l], 16 * (half + 1))
                        product(bank[q + 2][:, :], lambda k: yT[:, 0, k, i * P:(i + 1) * P],
                                lambda k: wo[:, k, :], 4)
                        ins = product(bank[q + 3][:, :], lambda k: yT[:, 1, k, i * P:(i + 1) * P],
                                      lambda k: wo[:, 4 + k, :], 4)
                        ins.then_inc(S["o"], 1)
                        n += 1
                barrier("pe", pe)
                for n, i in enumerate(T):
                    if n >= 2:
                        pe.wait_ge(*S.at("mte", 2 * (n - 1)))
                    for k in range(KD):
                        ins = pe.transpose(bank[2 * (n % 2) + k // 4][:, (k % 4) * P:(k % 4 + 1) * P],
                                           mix[:, i, k * P:(k + 1) * P], ident)
                        if k % 4 == 3:
                            ins.then_inc(S["mt"], 1)
                barrier("pe", pe)
                n = 0
                for half in range(2):
                    s, full = slot_of(l, B_OUT[half])
                    wv = w_view(s)
                    for i in T:
                        pe.wait_ge(w_full[s], 16 * full)
                        if n >= 8:
                            pe.wait_ge(*S.at("xup", n - 7))
                        ins = product(bank[n % 8][:, :], lambda k: hT[:, k, i * P:(i + 1) * P],
                                      lambda k: wv[:, k, :], KD)
                        ins.then_inc(S["wo"], 1)
                        n += 1
                barrier("pe", pe)
                transposes_of_h(S, T, NT)
                barrier("pe", pe)
                for n, i in enumerate(T):
                    ins = product(bank[0][:, n * E:(n + 1) * E], lambda k: hT[:, k, i * P:(i + 1) * P],
                                  lambda k: wr[:, k, :], KD)
                ins.then_inc(S["lg"], 1)
                pe.wait_ge(*S.at("rb", 1))
                for n, i in enumerate(T):
                    for j in range(n):
                        pe.matmul(bank[1][:, n * E:(n + 1) * E], ones_b, m_b[:, j, :], start=j == 0, stop=False)
                    ins = pe.matmul(bank[1][:, n * E:(n + 1) * E], tri_b, m_b[:, n, :], start=n == 0, stop=True)
                for n, i in enumerate(T):
                    ins = pe.matmul(bank[1][:, len(T) * E:(len(T) + 1) * E], ones_b, m_b[:, n, :], start=n == 0,
                                    stop=n == len(T) - 1)
                ins.then_inc(S["pos"], 1)
                for n, i in enumerate(T):
                    pe.wait_ge(*S.at("ohr", n + 1))
                    for e in range(E):
                        ins = pe.matmul(bank[2 + n][:, 2 * e:2 * e + 2], ohb[n % 2][:, e, :], tok_b[:, i, :],
                                        start=True, stop=True)
                    ins.then_inc(S["ix"], 1)
                barrier("pe", pe)

                base = moe_base(l)
                wg, wu = w_view(0), w_view(1)

                def turn_rows(e):
                    pe.wait_ge(*S.at("gat", (e + 1) * 16))
                    for k in range(KD):
                        ins = pe.transpose(bank[k // 4][:, (k % 4) * P:(k % 4 + 1) * P],
                                           xg[:, k * P:(k + 1) * P], ident)
                    ins.then_inc(S["xt"], 1)

                def gate_up(e):
                    pe.wait_ge(*S.at("xte", (e + 1) * 2))
                    pe.wait_ge(w_full[0], (e + base + 1) * 16)
                    product(bank[2][:, :], lambda k: xgT[:, k, :], lambda k: wg[:, k, :], KD).then_inc(w_used[0], 1)
                    pe.wait_ge(w_full[1], (e + base + 1) * 16)
                    product(bank[3][:, :], lambda k: xgT[:, k, :], lambda k: wu[:, k, :], KD).then_inc(w_used[1], 1)

                def down(e):
                    pe.wait_ge(*S.at("ate", e + 1))
                    if not isinstance(e, int) or e:
                        pe.wait_ge(*S.at("ye", e * 2))
                    pe.wait_ge(w_full[2], (e + base + 1) * 16)
                    product(bank[5][:, :], lambda k: auT[:, k, :], lambda k: wd_view[:, k, 0:BLK], KF)
                    product(bank[6][:, :], lambda k: auT[:, k, :], lambda k: wd_view[:, k, BLK:D], KF
                            ).then_inc(w_used[2], 1)

                def turn_act(e):
                    pe.wait_ge(*S.at("au", e + 1))
                    for k in range(KF):
                        ins = pe.transpose(bank[4][:, k * P:(k + 1) * P], au[:, k * P:(k + 1) * P], ident)
                    ins.then_inc(S["at"], 1)

                turn_rows(0)
                gate_up(0)
                turn_rows(1)
                turn_act(0)

                def turn(e):
                    gate_up(e)
                    down(e - 1)
                    turn_rows(e + 1)
                    turn_act(e)

                turn(1)
                with pe.Fori(2, E - 1) as e:
                    turn(e)
                gate_up(E - 1)
                down(E - 2)
                turn_act(E - 1)
                down(E - 1)
                barrier("pe", pe)
                barrier("pe", pe)
                more_rounds("pe", pe, l)
            barrier("pe", pe)

        @block.scalar
        def _(act):
            act.wait_ge(s_c, 32)
            act.activation(cth[:, :, :], cvec[:, :, :], ACT.Tanh, scale=0.5).then_inc(s_cs2, 1)
            barrier("act", act)

            def squares(S, ts, ncol):
                for j, i in enumerate(ts):
                    if ncol + j:
                        act.wait_ge(*S.at("ss", ncol + j))
                    act.activation(junk, x[:, i, :], ACT.Square, accum_out=small[:, j:j + 1]).then_inc(S["ss"], 1)

            def read_out_h(S, ts, base):
                for j, i in enumerate(ts):
                    for c in range(2):
                        act.wait_ge(*S.at("tr", 2 * (base + j) + c + 1))
                        act.copy(hT[:, 4 * c:4 * c + 4, i * P:(i + 1) * P],
                                 bank[2 * (j % 2) + c][:, :].rearrange("p (k t) -> p k t", k=4)
                                 ).then_inc(S["hev"], 1)

            for l in range(DEPTH):
                S = L[l]
                T = tiles(l)
                if l == 0:
                    act.wait_ge(s_x, 16)
                    act.wait_ge(s_x2, 16)
                else:
                    act.wait_ge(*L[l - 1].at("f", NT))
                squares(S, range(NT), 0)
                read_out_h(S, range(NT), 0)
                barrier("act", act)
                for n, (b, i, o, w) in enumerate(in_jobs(l)):
                    act.wait_ge(*S.at("p", n + 1))
                    act.copy(z[:, i, o:o + w], bank[n % 8][:, 0:w]).then_inc(S["pev"], 1)
                barrier("act", act)
                for i in range(NT):
                    q = i in T
                    if q:
                        act.activation(rope_c[:, 0:QR], z[:, i, Z_CQ:Z_CKV], ACT.Square,
                                       accum_out=small[:, 16:17])
                    act.activation(rope_c[:, QR:QR + KVR], z[:, i, Z_CKV:Z_KR], ACT.Square,
                                   accum_out=small[:, 17:18]).then_inc(S["rz"], 1)
                    act.wait_ge(*S.at("rt1", i + 1))
                    act.copy(cT[:, :, :], bank[0][:, 0:384].rearrange("p (c t) -> p c t", c=3)
                             ).then_inc(S["rt2"], 1)
                    act.wait_ge(*S.at("rp", i + 1))
                    if q:
                        act.copy(zq[:, 0:512], bank[1][:, :])
                        act.copy(zq[:, 512:768], bank[2][:, 0:256])
                    for c in range(2):
                        kv = bank[3 + c][:, :].rearrange("p (h c d) -> p h c d", h=4, c=2)
                        act.copy(kcat.rearrange("p (h d) -> p h d", d=HB)[:, 4 * c:4 * c + 4, 0:HD], kv[:, :, 0, :])
                        ins = act.copy(vb[:, i, c * 256:(c + 1) * 256].rearrange("p (h d) -> p h d", h=4),
                                       kv[:, :, 1, :])
                    ins.then_inc(S["rpev"], 1)
                    act.wait_ge(*S.at("rqT", i + 1))
                    t = slice(i * P, (i + 1) * P)
                    if q:
                        act.copy(qaT[:, :, t], bank[5][:, :].rearrange("p (c t) -> p c t", c=4))
                        for c in range(2):
                            act.copy(qbT[0:HB, 4 * c:4 * c + 4, t],
                                     bank[6 + c][0:HB, :].rearrange("p (c t) -> p c t", c=4))
                    act.copy(kaT[:, :, t], bank[0][:, 0:256].rearrange("p (c t) -> p c t", c=2))
                    for c in range(2):
                        ins = act.copy(kbT[0:HB, 4 * c:4 * c + 4, t],
                                       bank[1 + c][0:HB, :].rearrange("p (c t) -> p c t", c=4))
                    ins.then_inc(S["rqe"], 1)
                barrier("act", act)
                units = attention_units(l)
                for u, (g, br, i, h, k0, nk) in enumerate(units):
                    act.wait_ge(*S.at("nm", u + 1))
                    if u >= 3:
                        act.wait_ge(*S.at("pt", u - 2))
                    act.activation(prob[u % 3][:, 0:nk * P], bank[u % 3][:, 0:nk * P], ACT.Exp,
                                   bias=small[:, nm_at(g) + h:nm_at(g) + h + 1], scale=att_scale(br),
                                   accum_out=small[:, 48 + (g % 2) * 8 + h:49 + (g % 2) * 8 + h]
                                   ).then_inc(S["ex"], 1)
                    if u >= 1:
                        read_pT(act, S, units, u - 1)
                    if h == HEADS - 1 and br == 0:
                        act.wait_ge(*S.at("nms", g + 1))
                        act.activation(small[:, 64:64 + HEADS], small[:, 64:64 + HEADS], ACT.Exp
                                       ).then_inc(S["es"], 1)
                read_pT(act, S, units, len(units) - 1)
                barrier("act", act)
                for n, i in enumerate(T):
                    for br in range(2):
                        act.wait_ge(*S.at("yt", 2 * n + br + 1))
                        act.copy(yT[:, br, :, i * P:(i + 1) * P],
                                 bank[2 * (n % 2) + br][:, :].rearrange("p (c t) -> p c t", c=4)
                                 ).then_inc(S["yte"], 1)
                barrier("act", act)
                for n in range(2 * len(T)):
                    q = 4 * (n % 2)
                    if n >= 1:
                        act.wait_ge(*S.at("m", n))
                    for c in range(2):
                        act.wait_ge(*S.at("o", 3 * n + c + 1))
                        act.activation(sg[c], bank[q + c][:, :], ACT.Tanh, scale=0.5).then_inc(S["sg"], 1)
                barrier("act", act)
                for n, i in enumerate(T):
                    for c in range(2):
                        act.wait_ge(*S.at("mt", 2 * n + c + 1))
                        act.copy(hT[:, 4 * c:4 * c + 4, i * P:(i + 1) * P],
                                 bank[2 * (n % 2) + c][:, :].rearrange("p (k t) -> p k t", k=4)
                                 ).then_inc(S["mte"], 1)
                barrier("act", act)
                barrier("act", act)
                squares(S, T, NT)
                read_out_h(S, T, NT)
                barrier("act", act)
                act.wait_ge(*S.at("lg", 1))
                act.activation(r_sc[:, 0:len(T) * E], bank[0][:, 0:len(T) * E], ACT.Tanh, scale=0.5
                               ).then_inc(S["lge"], 1)
                barrier("act", act)
                base = moe_base(l)

                def read_rows(e):
                    act.wait_ge(*S.at("xt", e + 1))
                    act.copy(xgT[:, 0:4, :], bank[0][:, :].rearrange("p (k t) -> p k t", k=4)).then_inc(S["xte"], 1)

                def tanh_gate(e):
                    act.wait_ge(w_used[0], e + used_base(l) + 1)
                    act.activation(tg, bank[2][:, :], ACT.Tanh, scale=0.5).then_inc(S["th"], 1)

                def read_act(e):
                    act.wait_ge(*S.at("at", e + 1))
                    act.copy(auT[:, :, :], bank[4][:, :].rearrange("p (k t) -> p k t", k=4)).then_inc(S["ate"], 1)

                def read_y(e):
                    act.wait_ge(w_used[2], e + used_base(l) + 1)
                    if not isinstance(e, int) or e:
                        act.wait_ge(*S.at("yst", e * 16))
                    act.copy(ysb[:, 0:BLK], bank[5][:, :]).then_inc(S["ye"], 1)

                read_rows(0)
                tanh_gate(0)
                read_rows(1)
                read_act(0)

                def turn(e):
                    tanh_gate(e)
                    read_y(e - 1)
                    read_rows(e + 1)
                    read_act(e)

                turn(1)
                with act.Fori(2, E - 1) as e:
                    turn(e)
                tanh_gate(E - 1)
                read_y(E - 2)
                read_act(E - 1)
                read_y(E - 1)
                barrier("act", act)
                barrier("act", act)
                more_rounds("act", act, l)
            for n, i in enumerate(range(NL)):
                act.wait_ge(*L[DEPTH - 1].at("f", n + 1))
                if n:
                    act.wait_ge(s_fin, n)
                act.activation(junk, x[:, i, :], ACT.Square, accum_out=small[:, n:n + 1]).then_inc(s_fin, 1)
            barrier("act", act)

        @block.vector
        def _(dve):
            def lk(ins):
                link(dve, ins)

            dve.wait_ge(s_cs2, 1)
            lk(dve.scalar_tensor_tensor(out=cth[:, :, :], in0=cth[:, :, :], scalar=1.0, in1=cvec[:, :, :],
                                        op0=ALU.add, op1=ALU.mult))
            dve.tensor_scalar(cvec[:, :, :], cth[:, :, :], 0.5, None, ALU.mult).then_inc(s_cs, 1)
            dve.wait_ge(s_const, 16)
            dve.tensor_copy(tri_b, cst("tri"))
            dve.memset(ones_b, 1.0)
            for i in range(NT):
                dve.tensor_copy(tok_b[:, i, :], cst(f"tok{i}"))
            for l in range(DEPTH):
                for b in range(12):
                    c = b % 6
                    if c == 0:
                        dve.wait_ge(s_brow, l * 64 + 32 * (b // 6 + 1))
                        if l or b:
                            dve.wait_ge(s_mrow, l * 32 + 16 * (b // 6))
                    dve.wait_ge(w_used[b % 3], l * 4 + b // 3 + 1)
                    cs = slice(c * BLK, (c + 1) * BLK)
                    if c // 2 != 1:
                        dve.tensor_tensor(mrow[:, cs], bank[c][0:2, :], brow[:, cs], ALU.add).then_inc(s_mevac, 1)
                    else:
                        dve.wait_ge(s_mevac, l * 12 + b)
                        dve.tensor_tensor(trow, bank[c][0:2, :], brow[:, cs], ALU.add).then_inc(s_mt, 1)
                        dve.wait_ge(s_mt, l * 4 + (b // 6) * 2 + c - 1)
                        dve.scalar_tensor_tensor(out=mrow[:, cs], in0=trow, scalar=1.0,
                                                 in1=grow[:, (c - 2) * BLK:(c - 1) * BLK],
                                                 op0=ALU.add, op1=ALU.mult).then_inc(s_mevac, 1)
            barrier("dve", dve)

            def norm_tiles(S, ts, base):
                dve.wait_ge(*S.at("ss", base + len(ts)))
                dve.tensor_scalar(small[:, 8:8 + len(ts)], small[:, 0:len(ts)], 1.0 / D, EPS, ALU.mult, ALU.add
                                  ).then_inc(S["var"], 1)
                dve.wait_ge(*S.at("rstd", 1 if base == 0 else 2))
                dve.wait_ge(*S.at("modbc", 16 if base == 0 else 32))
                for j, i in enumerate(ts):
                    if j >= 2:
                        dve.wait_ge(*S.at("tr", 2 * (base + j - 1)))
                        if base:
                            dve.wait_ge(*S.at(f"hst{j % 2}", 16 * (j // 2)))
                    lk(dve.scalar_tensor_tensor(out=htok[j % 2], in0=x[:, i, :], scalar=small[:, 12 + j:13 + j],
                                                in1=modbc[:, kind(i), D:2 * D], op0=ALU.mult, op1=ALU.mult))
                    dve.tensor_tensor(htok[j % 2], htok[j % 2], modbc[:, kind(i), 0:D], ALU.add
                                      ).then_inc(S["h"], 1)

            def rope(v, dim, heads, name, i):
                n = heads * dim
                d4 = dim // 4
                cos = cst(f"cos_{name}{i}").unsqueeze(1).to_broadcast([P, heads, dim])
                sin = cst(f"sin_{name}{i}").unsqueeze(1).to_broadcast([P, heads, dim])
                vc = rope_c[:, 0:n].rearrange("p (h d) -> p h d", d=dim)
                vs = rope_s[:, 0:n].rearrange("p (h d) -> p h d", d=dim)
                dve.tensor_tensor(vc, v, cos, ALU.mult)
                lk(dve.tensor_tensor(vs, v, sin, ALU.mult))
                for rc in range(2):
                    lo = slice(rc * dim // 2, rc * dim // 2 + d4)
                    hi = slice(rc * dim // 2 + d4, (rc + 1) * dim // 2)
                    dve.tensor_tensor(v[:, :, lo], vc[:, :, lo], vs[:, :, hi], ALU.subtract)
                    ins = dve.tensor_tensor(v[:, :, hi], vc[:, :, hi], vs[:, :, lo], ALU.add)
                return ins

            for l in range(DEPTH):
                S = L[l]
                T = tiles(l)
                norm_tiles(S, range(NT), 0)
                barrier("dve", dve)
                barrier("dve", dve)
                for i in range(NT):
                    q = i in T
                    dve.wait_ge(*S.at("rz", i + 1))
                    if i == 0:
                        dve.wait_ge(*S.at("lorain", 64))
                    if q:
                        dve.tensor_scalar(small[:, 18:19], small[:, 16:17], 1.0 / QR, EPS, ALU.mult, ALU.add)
                    else:
                        dve.memset(small[:, 18:19], 1.0)
                    dve.tensor_scalar(small[:, 19:20], small[:, 17:18], 1.0 / KVR, EPS, ALU.mult, ALU.add
                                      ).then_inc(S["rcv"], 1)
                    dve.wait_ge(*S.at("rcr", i + 1))
                    if q:
                        dve.scalar_tensor_tensor(out=cn[:, 0:QR], in0=z[:, i, Z_CQ:Z_CKV], scalar=small[:, 20:21],
                                                 in1=lora[:, 0:QR], op0=ALU.mult, op1=ALU.mult)
                    elif i == NL:
                        dve.memset(cn[:, 0:QR], 0.0)
                    dve.scalar_tensor_tensor(out=cn[:, QR:], in0=z[:, i, Z_CKV:Z_KR], scalar=small[:, 21:22],
                                             in1=lora[:, QR:], op0=ALU.mult, op1=ALU.mult).then_inc(S["rcn"], 1)
                    if i < NL:
                        lk(rope(z[:, i, 0:10 * HD].rearrange("p (h d) -> p h d", d=HD), HD, 10, "a", i))
                        lk(rope(z[:, i, Z_KR:Z_END].rearrange("p (h d) -> p h d", d=RD), RD, 1, "b", i))
                    kd = kdup.rearrange("p (g c d) -> p g c d", g=KV_A, c=2)
                    ka = z[:, i, Z_KA:Z_VA].rearrange("p (g d) -> p g d", g=KV_A)
                    if i:
                        dve.wait_ge(*S.at("rqT", i))
                    for c in range(2):
                        dve.tensor_copy(kd[:, :, c, :], ka)
                    dve.wait_ge(*S.at("rpev", i + 1))
                    ins = dve.tensor_copy(kcat.rearrange("p (h d) -> p h d", d=HB)[:, :, HD:HB],
                                          z[:, i, Z_KR:Z_END].unsqueeze(1).to_broadcast([P, HEADS, RD]))
                    if i < NL:
                        lk(ins)
                        ins = rope(zq.rearrange("p (h d) -> p h d", d=HB)[:, :, HD:HB], RD, HEADS, "b", i)
                    ins.then_inc(S["rq"], 1)
                barrier("dve", dve)
                units = attention_units(l)

                def finish(g):
                    u_last = 8 * g + 7
                    _, br, i, _, _, _ = units[u_last]
                    dve.wait_ge(*S.at("ex", u_last + 1))
                    ls = small[:, 48 + (g % 2) * 8:56 + (g % 2) * 8]
                    if br == 0:
                        dve.wait_ge(*S.at("es", g + 1))
                        lk(dve.tensor_tensor(small[:, 72:80], ls, small[:, 64:72], ALU.add))
                        lk(dve.reciprocal(small[:, 80:88], small[:, 72:80]))
                    else:
                        lk(dve.reciprocal(small[:, 80:88], ls))
                    dve.wait_ge(*S.at("pv", u_last + 1))
                    o = Z_YA if br == 0 else Z_YB
                    dve.tensor_tensor(z[:, i, o:o + 512].rearrange("p (h d) -> p h d", d=HD),
                                      bank[5 + g % 2][:, :].rearrange("p (h d) -> p h d", d=HD),
                                      small[:, 80:88].unsqueeze(2).to_broadcast([P, HEADS, HD]), ALU.mult
                                      ).then_inc(S["yev"], 1)

                for u, (g, br, i, h, k0, nk) in enumerate(units):
                    dve.wait_ge(*S.at("sc", u + 1))
                    b = bank[u % 3]
                    if br == 0 and i < NL:
                        cut = b[:, (1 - i) * P:(2 - i) * P]
                        lk(dve.tensor_tensor(cut, cut, cst(f"mask{i}"), ALU.add))
                    lk(dve.tensor_reduce(small[:, 88 + u % 2:89 + u % 2], b[:, 0:nk * P], AX.X, ALU.max))
                    nm = small[:, nm_at(g) + h:nm_at(g) + h + 1]
                    if br == 0:
                        ins = dve.tensor_scalar(nm, small[:, 88 + u % 2:89 + u % 2], -att_scale(br), sinks[:, 8 + h:9 + h],
                                                ALU.mult, ALU.min)
                    else:
                        ins = dve.tensor_scalar(nm, small[:, 88 + u % 2:89 + u % 2], -att_scale(br), None, ALU.mult)
                    ins.then_inc(S["nm"], 1)
                    if h == HEADS - 1 and br == 0:
                        dve.wait_ge(*S.at("nm", u + 1))
                        dve.tensor_tensor(small[:, 64:72], sinks[:, 0:8], small[:, nm_at(g):nm_at(g) + 8], ALU.add
                                          ).then_inc(S["nms"], 1)
                    if h == 3 and g >= 1:
                        finish(g - 1)
                finish(units[-1][0])
                barrier("dve", dve)
                barrier("dve", dve)
                n = 0
                for half in range(2):
                    for i in T:
                        q = 4 * (n % 2)
                        dve.wait_ge(*S.at("sg", 2 * n + 2))
                        dve.wait_ge(*S.at("o", 3 * n + 3))
                        for c in range(2):
                            ins = dve.scalar_tensor_tensor(out=pg[c], in0=sg[c], scalar=1.0, in1=bank[q + 2 + c][:, :],
                                                           op0=ALU.add, op1=ALU.mult)
                        lk(ins)
                        dve.tensor_tensor(mix[:, i, half * BLK:(half + 1) * BLK], pg[0], pg[1], ALU.add
                                          ).then_inc(S["m"], 1)
                        n += 1
                barrier("dve", dve)
                barrier("dve", dve)
                n = 0
                for half in range(2):
                    cs = slice(half * BLK, (half + 1) * BLK)
                    for i in T:
                        dve.wait_ge(*S.at("wo", n + 1))
                        lk(dve.scalar_tensor_tensor(out=pg[n % 2], in0=bank[n % 8][:, :], scalar=0.5,
                                                    in1=modbc[:, kind(i), 2 * D + half * BLK:2 * D + (half + 1) * BLK],
                                                    op0=ALU.mult, op1=ALU.mult))
                        dve.tensor_tensor(x[:, i, cs], x[:, i, cs], pg[n % 2], ALU.add).then_inc(S["xup"], 1)
                        n += 1
                barrier("dve", dve)
                norm_tiles(S, T, NT)
                barrier("dve", dve)
                route(dve, lk, S, T)
                barrier("dve", dve)
                base = moe_base(l)

                def read_rows_d(e):
                    dve.wait_ge(*S.at("xt", e + 1))
                    dve.tensor_copy(xgT[:, 4:8, :], bank[1][:, :].rearrange("p (k t) -> p k t", k=4)
                                    ).then_inc(S["xte"], 1)

                def activate(e):
                    dve.wait_ge(*S.at("th", e + 1))
                    dve.scalar_tensor_tensor(out=au, in0=tg, scalar=1.0, in1=bank[2][:, :],
                                             op0=ALU.add, op1=ALU.mult).then_inc(S["aug"], 1)
                    dve.wait_ge(*S.at("aug", e + 1))
                    dve.wait_ge(w_used[1], e + used_base(l) + 1)
                    dve.tensor_tensor(au, au, bank[3][:, :], ALU.mult).then_inc(S["au"], 1)

                def read_y_d(e):
                    dve.wait_ge(w_used[2], e + used_base(l) + 1)
                    if not isinstance(e, int) or e:
                        dve.wait_ge(*S.at("yst", e * 16))
                    dve.tensor_copy(ysb[:, BLK:D], bank[6][:, :]).then_inc(S["ye"], 1)

                read_rows_d(0)
                activate(0)
                read_rows_d(1)

                def turn(e):
                    activate(e)
                    read_y_d(e - 1)
                    read_rows_d(e + 1)

                turn(1)
                with dve.Fori(2, E - 1) as e:
                    turn(e)
                activate(E - 1)
                read_y_d(E - 2)
                read_y_d(E - 1)
                barrier("dve", dve)
                for n, i in enumerate(T):
                    for c in range(2):
                        dve.wait_ge(*S.at(f"g{c}{n % 2}", 16 * (n // 2 + 1)))
                    combine(dve, lk, l, n, i).then_inc(S["f"], 1)
                dve.wait_ge(*S.at("f", len(T)))
                barrier("dve", dve)
                more_rounds("dve", dve, l)
            dve.wait_ge(s_fin, NL)
            dve.tensor_scalar(small[:, 8:8 + NL], small[:, 0:NL], 1.0 / D, EPS, ALU.mult, ALU.add).then_inc(s_fvar, 1)
            dve.wait_ge(s_frs, 1)
            dve.wait_ge(s_fn, 16)
            for i in range(NL):
                dve.scalar_tensor_tensor(out=htok[i], in0=x[:, i, :], scalar=small[:, 12 + i:13 + i],
                                         in1=modbc[:, 0, 0:D], op0=ALU.mult, op1=ALU.mult).then_inc(s_fout, 1)
            barrier("dve", dve)

        @block.gpsimd
        def _(pool):
            pool.dma_start(cvec[:, 0, :], a["c"].rearrange("b (p k) -> p (b k)", k=KD)).then_inc(s_c, 16)
            pool.dma_start(cvec[:, 1, :], a["c_ctx"].rearrange("(p k) -> p k", k=KD)).then_inc(s_c, 16)
            pool.dma_start(const[:, :], const_in).then_inc(s_const, 16)
            pool.dma_start(wr[:, :, :], a["w_router"].rearrange("(k p) e -> p k e", p=P)).then_inc(s_wr, 16)
            pool.dma_start(rbias[:, :], a["router_bias"].rearrange("(a e) -> a e", a=1).to_broadcast([P, E])
                           ).then_inc(s_wr, 16)
            pool.dma_start(x[:, 0:NL, :], a["x"].rearrange("b (i p) d -> p (b i) d", p=P)).then_inc(s_x, 16)
            pool.dma_start(x[:, NL:NT, :], a["ctx"].rearrange("b (i p) d -> p (b i) d", p=P)).then_inc(s_x2, 16)
            for l in range(DEPTH):
                for sub, g in enumerate((a["norm_mix"], a["norm_ffn"])):
                    if l or sub:
                        pool.wait_ge(s_mevac, l * 12 + sub * 6)
                    pool.dma_start(brow, a["b_mod"][l:l + 1, sub * MOD:(sub + 1) * MOD].to_broadcast([2, MOD])
                                   ).then_inc(s_brow, 16)
                    pool.dma_start(grow, g[l:l + 1, :].to_broadcast([2, D])).then_inc(s_brow, 16)
                    pool.wait_ge(s_mevac, l * 12 + sub * 6 + 6)
                    pool.dma_start(mod_dram[l, sub], mrow
                                   ).then_inc(s_mrow, 16)
            pool.wait_ge(s_mrow, 16 * 2 * DEPTH)
            barrier("pool", pool)

            def load_mod(S, l, sub):
                pool.dma_start(modbc[:, :, :].rearrange("p t n -> p (t n)"),
                               mod_dram[l, sub].rearrange("(a t) n -> a (t n)", a=1).to_broadcast([P, 2 * MOD])
                               ).then_inc(S["modbc"], 16)

            def inverse_root(S, n, v):
                pool.wait_ge(*S.at("var", v))
                pool.tensor_tensor(small[:, 12:12 + n], small[:, 8:8 + n], cst("minus_half")[:, 0:n], ALU.pow
                                   ).then_inc(S["rstd"], 1)

            for l in range(DEPTH):
                S = L[l]
                T = tiles(l)
                load_mod(S, l, 0)
                pool.dma_start(lora[:, 0:QR], a["mla_q_norm"][l:l + 1, :].to_broadcast([P, QR])).then_inc(S["lorain"], 16)
                pool.dma_start(lora[:, QR:], a["mla_kv_norm"][l:l + 1, :].to_broadcast([P, KVR])
                               ).then_inc(S["lorain"], 16)
                pool.dma_start(sinks[:, 0:HEADS], a["attn_sink"][l:l + 1, :].to_broadcast([P, HEADS])
                               ).then_inc(S["lorain"], 16)
                pool.dma_start(sinks[:, HEADS:], a["attn_sink"][l:l + 1, :].to_broadcast([P, HEADS])
                               ).then_inc(S["lorain"], 16)
                inverse_root(S, NT, 1)
                barrier("pool", pool)
                pool.wait_ge(*S.at("lorain", 64))
                pool.tensor_scalar(sinks[:, HEADS:], sinks[:, HEADS:], -1.0, None, ALU.mult)
                barrier("pool", pool)
                for i in range(NT):
                    pool.wait_ge(*S.at("rcv", i + 1))
                    pool.tensor_tensor(small[:, 20:22], small[:, 18:20], cst("minus_half")[:, 0:2], ALU.pow
                                       ).then_inc(S["rcr"], 1)
                barrier("pool", pool)
                for _ in range(4):
                    barrier("pool", pool)
                barrier("pool", pool)
                load_mod(S, l, 1)
                inverse_root(S, len(T), 2)
                for n, i in enumerate(T):
                    pool.wait_ge(*S.at("h", NT + n + 1))
                    pool.dma_start(h_dram[i * P:(i + 1) * P, :], htok[n % 2]).then_inc(S[f"hst{n % 2}"], 16)
                for j in range(2):
                    pool.wait_ge(*S.at(f"hst{j}", 16 * len(T) // 2))
                barrier("pool", pool)
                barrier("pool", pool)

                def gather(e):
                    pool.indirect_dma_start(out=xg, out_offset=None, in_=h_dram,
                                            in_offset=bass.IndirectOffsetOnAxis(ap=idx[:, e:e + 1], axis=0)
                                            ).then_inc(S["gat"], 16)

                gather(0)
                for e in range(E):
                    if e + 1 < E:
                        pool.wait_ge(*S.at("xt", e + 1))
                        gather(e + 1)
                    if e:
                        pool.wait_ge(*S.at("ye", 2 * e))
                        pool.dma_start(y_dram[(e - 1) * CAP:e * CAP, :], ysb).then_inc(S["yst"], 16)
                pool.wait_ge(*S.at("ye", 2 * E))
                pool.dma_start(y_dram[(E - 1) * CAP:E * CAP, :], ysb).then_inc(S["yst"], 16)
                pool.wait_ge(*S.at("yst", 16 * E))
                barrier("pool", pool)
                for n, i in enumerate(T):
                    if n >= 2:
                        pool.wait_ge(*S.at("f", n - 1))
                    for c, (dst, s) in enumerate(((y1[n % 2], S[f"g0{n % 2}"]), (y2[n % 2], S[f"g1{n % 2}"]))):
                        pool.indirect_dma_start(out=dst, out_offset=None, in_=y_dram,
                                                in_offset=bass.IndirectOffsetOnAxis(ap=row[:, c, n:n + 1], axis=0)
                                                ).then_inc(s, 16)
                pool.wait_ge(*S.at("f", len(T)))
                barrier("pool", pool)
                more_rounds("pool", pool, l)
            pool.dma_start(modbc[:, 0, 0:D], a["final_norm"].rearrange("(a d) -> a d", a=1).to_broadcast([P, D])
                           ).then_inc(s_fn, 16)
            pool.wait_ge(s_fvar, 1)
            pool.tensor_tensor(small[:, 12:12 + NL], small[:, 8:8 + NL], cst("minus_half")[:, 0:NL], ALU.pow
                               ).then_inc(s_frs, 1)
            for i in range(NL):
                pool.wait_ge(s_fout, i + 1)
                pool.dma_start(out[0, i * P:(i + 1) * P, :], htok[i]).then_inc(s_out, 16)
            pool.wait_ge(s_out, 16 * NL)
            barrier("pool", pool)


_INS = ['x', 'c', 'ctx', 'c_ctx', 'w_mod', 'b_mod', 'norm_mix', 'norm_ffn', 'w_in', 'attn_sink', 'mla_q_norm', 'w_uq',
        'mla_kv_norm', 'w_ukv', 'w_o_a', 'w_o_b', 'w_out', 'w_router', 'router_bias', 'w_expert_gate', 'w_expert_up',
        'w_expert_down', 'final_norm']


def kernel(**inputs):
    import concourse.bacc as bacc
    from concourse.bass_utils import run_bass_kernel_spmd

    nc = bacc.Bacc("TRN2", target_bir_lowering=False, num_devices=1)
    arrays = {f"in_{n}": np.ascontiguousarray(inputs[n]) for n in _INS}
    args = {n: nc.dram_tensor(f"in_{n}", arrays[f"in_{n}"].shape, F32, kind="ExternalInput").ap() for n in _INS}
    arrays["tables"] = CONST
    tables = nc.dram_tensor("tables", CONST.shape, F32, kind="ExternalInput").ap()
    out = nc.dram_tensor("out", (1, SEQ, D), F32, kind="ExternalOutput").ap()
    trunk(nc, args, tables, out)
    r = run_bass_kernel_spmd(nc, [arrays], core_ids=[0])
    return r.results[0]["out"]
```

```python
from contextlib import ExitStack

import numpy as np

import concourse.bass as bass
from concourse import mybir

F32 = mybir.dt.float32
BF16 = mybir.dt.bfloat16
U32 = mybir.dt.uint32
I32 = mybir.dt.int32
ALU = mybir.AluOpType
ACT = mybir.ActivationFunctionType
AX = mybir.AxisListType

P = 128
D = 1024
KD = D // P
SEQ = 256
CTX = 256
NT = (SEQ + CTX) // P
NL = SEQ // P
DEPTH = 2
GRID_W = 64
ROPE_BASE = 10000.0
EPS = 1e-6
HEADS = 8
HD = 64
KV_A = 2
WINDOW = 128
QR, KVR, RD = 256, 128, 32
HB = HD + RD
E = 16
GROUPS = 4
F = 512
KF = F // P
CAP = P
ROUNDS = NT
BLK = 512
Z_QA, Z_KA, Z_VA, Z_CQ, Z_CKV, Z_KR, Z_END = 0, 512, 640, 768, 1024, 1152, 1184
Z_YA, Z_YB, Z_W = 0, 768, 1280
BIG = 1e30
MOD = 3 * D


def constants():
    cols, at = [], {}

    def put(name, a):
        at[name] = (sum(c.shape[1] for c in cols), a.shape[1])
        cols.append(np.asarray(a, np.float32))

    p = np.arange(P)
    put("ident", np.eye(P))
    put("tri", (p[:, None] < p[None, :]))
    put("iota", np.broadcast_to(p[None, :], (P, P)))
    for i in range(NL):
        q, k = i * P + p[:, None], (1 - i) * P + p[None, :]
        put(f"mask{i}", np.where(np.abs(q - k) <= WINDOW, 0.0, -BIG))
    for name, dim in (("a", HD // 2), ("b", RD // 2)):
        inv = (np.float32(ROPE_BASE) ** (-np.arange(0, dim, 2, dtype=np.float32) / np.float32(dim))).astype(np.float32)
        for i in range(NL):
            t = i * P + p
            parts_c, parts_s = [], []
            for pos in (t // GRID_W, t % GRID_W):
                ang = pos.astype(np.float32)[:, None] * inv[None, :]
                parts_c += [np.cos(ang), np.cos(ang)]
                parts_s += [np.sin(ang), np.sin(ang)]
            put(f"cos_{name}{i}", np.concatenate(parts_c, 1))
            put(f"sin_{name}{i}", np.concatenate(parts_s, 1))
    put("rank_g", np.broadcast_to(GROUPS - np.arange(GROUPS)[None], (P, GROUPS)))
    put("rank_e", np.broadcast_to(E - np.arange(E)[None], (P, E)))
    put("eid", np.broadcast_to(np.arange(E)[None] * CAP, (P, E)))
    for i in range(NT):
        put(f"tok{i}", np.stack([p, np.full(P, i * P)], 1))
    put("minus_half", np.full((P, 8), -0.5))
    return np.concatenate(cols, 1), at


CONST, AT = constants()
NCONST = CONST.shape[1]


def trunk(nc, a, const_in, out):
    with ExitStack() as ctx:
        def sb(name, shape, dt=F32):
            return ctx.enter_context(nc.sbuf_tensor(name, shape, dt))

        def sem(name):
            return ctx.enter_context(nc.semaphore(name))

        def dram(name, shape, dt=F32):
            return nc.dram_tensor(name, shape, dt).ap()

        mod_dram = dram("mod_rows", (DEPTH, 2, 2, MOD))
        h_dram = dram("h_rows", (NT * P, D))
        y_dram = dram("y_rows", (E * CAP, D))

        const = sb("const", [P, NCONST])

        def cst(name):
            o, n = AT[name]
            return const[:, o:o + n]

        ident = cst("ident")
        x = sb("x_tok", [P, NT, D])
        hT = sb("hT", [P, KD, NT * P])
        wslot = [sb(f"wslot{s}", [P, KD * BLK]) for s in range(3)]
        modbc = sb("modbc", [P, 2, MOD])
        z = sb("z", [P, NT, Z_W])
        rt = sb("rt", [P, 1600])
        arena = sb("arena", [P, 17408])

        def carve(o, n, dt=F32):
            return arena[:, o:o + n]

        qaT = carve(0, 2048).rearrange("p (c t) -> p c t", c=4)
        kaT = carve(2048, 1024).rearrange("p (c t) -> p c t", c=2)
        vb = carve(3072, 2048).rearrange("p (i n) -> p i n", i=NT)
        qbT = carve(5120, 4096).rearrange("p (h t) -> p h t", h=HEADS)
        kbT = carve(9216, 4096).rearrange("p (h t) -> p h t", h=HEADS)
        rope_c = carve(13312, 640)
        rope_s = carve(13952, 640)
        zq = [carve(14592, 768), modbc[:, 0, 0:768]]
        kcat = [carve(15360, 768), modbc[:, 0, 768:1536]]
        kdup = [carve(16128, 256), modbc[:, 0, 1536:1792]]
        lora_sum, lora_var, lora_rstd = (rt[:, o:o + 2 * NT] for o in (1520, 1528, 1536))
        lora_junk = carve(9216, 4096).rearrange("p (i n) -> p i n", i=NT)
        cn = carve(16384, 384)
        cT = carve(16768, 384).rearrange("p (c t) -> p c t", c=3)
        prob = [carve(13312 + 512 * j, 512) for j in range(3)]
        pT = [carve(14848 + 512 * j, 512).rearrange("p (c t) -> p c t", c=4) for j in range(2)]
        yT = carve(5120, 4096).rearrange("p (b c t) -> p b c t", b=2, c=4)
        mix = carve(9216, 4096).rearrange("p (i n) -> p i n", i=NT)
        sg = [carve(13312 + 512 * j, 512) for j in range(2)]
        pg = [carve(14336 + 512 * j, 512) for j in range(2)]
        htok = [carve(1024 * j, 1024) for j in range(2)]
        junk = carve(2048, 1024)
        xg = carve(4096, 1024)
        xgT = carve(5120, 1024).rearrange("p (k t) -> p k t", k=KD)
        tg = carve(6144, 512)
        au = carve(6656, 512)
        auT = carve(7168, 512).rearrange("p (k t) -> p k t", k=KF)
        ysb = carve(7680, 1024)
        ysb_last = carve(8704, 1024)
        y1 = [carve(8704 + 2048 * j, 1024) for j in range(2)]
        y2 = [carve(9728 + 2048 * j, 1024) for j in range(2)]
        oh = carve(13312, E * CAP).rearrange("p (j n) -> p j n", j=2)
        ohb = [oh[:, j].bitcast(BF16).rearrange("p (e s) -> p e s", e=E) for j in range(2)]
        small = sb("small", [P, 96])
        bf = sb("bf", [P, 2 * P + NT * E + 2 * NT], BF16)
        tri_b, ones_b = bf[:, 0:P], bf[:, P:2 * P]
        m_b = bf[:, 2 * P:2 * P + NT * E].rearrange("p (i e) -> p i e", e=E)
        tok_b = bf[:, 2 * P + NT * E:].rearrange("p (i c) -> p i c", c=2)
        idx = sb("idx", [P, E], U32)
        row = sb("row", [P, 2, NT], U32)
        idxc = sb("idxc", [P, 1], U32)
        more = sb("more", [1, 1], I32)
        sinks = sb("sinks", [P, 2 * HEADS])
        lora = sb("lora", [P, QR + KVR])
        wr = sb("wr", [P, KD, E])
        rbias = sb("rbias", [P, E])
        cvec = sb("cvec", [P, 2, KD])
        cth = sb("cth", [P, 2, KD])
        mrow = z[0:2, :, :].rearrange("p i n -> p (i n)")[:, 0:MOD]
        brow = arena[0:2, 4096:4096 + MOD]
        grow = arena[0:2, 4096 + MOD:4096 + MOD + D]
        trow = arena[0:2, 4096 + MOD + D:4096 + MOD + D + BLK]

        bank = [ctx.enter_context(nc.psum_tensor(f"bank{j}", [P, BLK], F32)) for j in range(8)]

        s_stage = sem("stage_end")
        w_full = [sem(f"w_full{s}") for s in range(3)]
        w_used = [sem(f"w_used{s}") for s in range(3)]
        s_const = sem("const_in")
        s_c = sem("c_in")
        s_x = sem("x_in")
        s_cs = sem("silu_c")
        s_brow = sem("bias_row_in")
        s_mevac = sem("mod_evac")
        s_mrow = sem("mod_row_out")
        s_link = sem("dve_link")
        counts = dict(
            modn=32, modg=32, ss=2 * NT, var=2, rstd=2, h=2 * NT, tr=4 * NT, hev=4 * NT, lorain=64, p=3 * NT, pev=3 * NT,
            rz=1, rcv=1, rcr=1, rcn=NT, rtq=NT, rqq=NT, rt1=NT, rt2=NT, rp=NT, rpev=NT, rq=NT, rqT=NT, rqe=NT,
            sc=2 * NT * HEADS, nm=2 * NT * HEADS, ex=2 * NT * HEADS, pt=2 * NT * HEADS, pte=2 * NT * HEADS,
            pv=2 * NT * HEADS, nms=NT, es=NT, yev=2 * NT, yt=2 * NT, yte=2 * NT, o=6 * NT, sg=4 * NT, m=2 * NT,
            mt=2 * NT, mte=2 * NT, wo=2 * NT, xup=2 * NT, hst0=8 * NT, hst1=8 * NT, lg=1, lge=1, rb=1, pos=1,
            ohr=NT, ix=NT, gat=16 * E, xt=E, xte=2 * E, th=E, aug=E, au=E, at=E, ate=E, ye=2 * E, yst=16 * E,
            g00=8 * NT, g01=8 * NT, g10=8 * NT, g11=8 * NT, f=NT, ym=NT)
        signals = {n: sem(n) for n in counts}

        class Layer:

            def __init__(self, l):
                self.l = l

            def __getitem__(self, name):
                return signals[name]

            def at(self, name, n):
                return signals[name], n + self.l * counts[name]

        L = [Layer(l) for l in range(DEPTH)]
        s_out = sem("out_dma")
        s_fin = sem("final")

        s_cs2 = sem("tanh_c")
        s_mt = sem("scale_row")
        s_wr = sem("router_in")
        s_x2 = sem("ctx_in")
        s_lora_w = [sem(f"w_ukv_in_{l}") for l in range(DEPTH)]
        s_ob_w = [sem(f"w_o_b_in_{l}") for l in range(DEPTH)]
        s_passed = sem("step_passed")
        s_more = [sem(f"more_step_{l}") for l in range(DEPTH)]
        s_xw = [sem(f"more_weights_in_{l}") for l in range(DEPTH)]
        s_xg = [sem(f"more_rows_in_{l}") for l in range(DEPTH)]
        s_xy = [sem(f"more_results_out_{l}") for l in range(DEPTH)]
        s_xc = [sem(f"more_results_in_{l}") for l in range(DEPTH)]
        s_fvar, s_frs, s_fn, s_fout = sem("final_var"), sem("final_rstd"), sem("final_norm_in"), sem("final_out")

        block = ctx.enter_context(nc.Block())
        stages = {}

        def barrier(name, eng):
            n = stages[name] = stages.get(name, 0) + 1
            eng.drain().then_inc(s_stage, 1)
            eng.wait_ge(s_stage, 4 * n)

        links = [0]

        def link(dve, ins):
            links[0] += 1
            ins.then_inc(s_link, 1)
            dve.wait_ge(s_link, links[0])

        def tiles(l):
            return range(NT) if l < DEPTH - 1 else range(NL)

        def kind(i):
            return 0 if i < NL else 1

        MOD_PER_SLOT = DEPTH * 12 // 3

        def first_norm_tile(b, late):
            j, odd = divmod(b - 12 - late, 2)
            return j if odd == 0 and 0 <= j < NT else None

        BLOCKS = 12

        def slot_of(l, b):
            return b % 3, MOD_PER_SLOT + l * (BLOCKS // 3 + E) + b // 3 + 1

        def moe_base(l):
            return MOD_PER_SLOT + l * (BLOCKS // 3 + E) + BLOCKS // 3

        def used_base(l):
            return MOD_PER_SLOT + l * E

        def w_view(s, n=BLK):
            return wslot[s][:, 0:KD * n].rearrange("p (k n) -> p k n", k=KD)

        wd_view = wslot[2][:, :].rearrange("p (k n) -> p k n", k=KF)

        def in_jobs(l):
            T = tiles(l)
            jobs = [(0, i, 0, 512) for i in T]
            jobs += [(1, i, 512, 512 if i in T else 256) for i in range(NT)]
            return jobs + [(2, i, 1024, 160) for i in range(NT)]

        def attention_units(l):
            groups = [(br, i) for br in range(2) for i in tiles(l)]
            return [(g, br, i, h, 0 if i < NL else NL, NT if i < NL else NT - NL)
                    for g, (br, i) in enumerate(groups) for h in range(HEADS)]

        def att_scale(br):
            return (HD if br == 0 else HB) ** -0.5

        def nm_at(g):
            return 24 + (g % 2) * 8

        def read_pT(act, S, units, u):
            g, br, i, h, k0, nk = units[u]
            act.wait_ge(*S.at("pt", u + 1))
            if u >= 2:
                act.wait_ge(*S.at("pv", u - 1))
            act.copy(pT[u % 2][:, 0:nk, :], bank[3 + u % 2][:, 0:nk * P].rearrange("p (c t) -> p c t", c=nk)
                     ).then_inc(S["pte"], 1)

        def rcol(o, n):
            return rt[:, o:o + n]

        r_sc = rcol(0, NT * E)
        r_w = rcol(1500, 2 * NT).rearrange("p (c i) -> p c i", c=2)
        r_wm = rcol(1508, 2 * NT).rearrange("p (c i) -> p c i", c=2)

        def route(dve, lk, S, T):
            n = len(T)
            ne = n * E

            def by_tile(v, m=E):
                return v.rearrange("p (i e) -> p i e", i=n)

            def over(v, m):
                return v.unsqueeze(2).to_broadcast([P, v.shape[1], m])

            sc, sel, ms, w, t = (rcol(64 * j, ne) for j in (0, 1, 2, 3, 4))
            o1, o2 = rcol(320, ne), rcol(384, ne)
            mf, posm, pos = rcol(448, ne), rcol(512, ne), rcol(576, ne)
            pair = rcol(640, n * GROUPS * 6).rearrange("p (g c) -> p g c", c=6)
            gs, w4, pen = rcol(740, n * GROUPS), rcol(756, n * GROUPS), rcol(772, n * GROUPS)
            gm = rcol(788, n)
            m1 = rcol(792, n)
            ssum = rcol(796, 2 * n)
            den = rcol(804, n)
            bE = [P, n, E]
            dve.wait_ge(*S.at("lge", 1))
            dve.wait_ge(s_wr, 32)
            lk(dve.tensor_scalar(sc, sc, 0.5, 0.5, ALU.mult, ALU.add))
            lk(dve.tensor_tensor(by_tile(sel), by_tile(sc), rbias[:, :].unsqueeze(1).to_broadcast(bE), ALU.add))
            g4 = sel.rearrange("p (g c) -> p g c", c=4)
            dve.tensor_tensor(pair[:, :, 0:3], g4[:, :, 0:3], g4[:, :, 1:4], ALU.add)
            dve.tensor_tensor(pair[:, :, 3:5], g4[:, :, 0:2], g4[:, :, 2:4], ALU.add)
            lk(dve.tensor_tensor(pair[:, :, 5:6], g4[:, :, 0:1], g4[:, :, 3:4], ALU.add))
            lk(dve.tensor_reduce(gs, pair, AX.X, ALU.max))
            lk(dve.tensor_reduce(gm, by_tile(gs), AX.X, ALU.max))
            lk(dve.tensor_tensor(by_tile(w4), by_tile(gs), over(gm, GROUPS), ALU.is_equal))
            lk(dve.tensor_tensor(by_tile(w4), by_tile(w4),
                                 cst("rank_g").unsqueeze(1).to_broadcast([P, n, GROUPS]), ALU.mult))
            lk(dve.tensor_reduce(gm, by_tile(w4), AX.X, ALU.max))
            lk(dve.tensor_tensor(by_tile(w4), by_tile(w4), over(gm, GROUPS), ALU.is_equal))
            lk(dve.tensor_scalar(pen, w4, -1.0, BIG, ALU.add, ALU.mult))
            lk(dve.tensor_tensor(ms.rearrange("p (g c) -> p g c", c=4), g4, over(pen, 4), ALU.add))
            for c, o in enumerate((o1, o2)):
                lk(dve.tensor_reduce(m1, by_tile(ms), AX.X, ALU.max))
                lk(dve.tensor_tensor(by_tile(w), by_tile(ms), over(m1, E), ALU.is_equal))
                lk(dve.tensor_tensor(by_tile(w), by_tile(w), cst("rank_e").unsqueeze(1).to_broadcast(bE), ALU.mult))
                lk(dve.tensor_reduce(m1, by_tile(w), AX.X, ALU.max))
                lk(dve.tensor_tensor(by_tile(o), by_tile(w), over(m1, E), ALU.is_equal))
                lk(dve.tensor_tensor(t, o, sc, ALU.mult))
                lk(dve.tensor_reduce(ssum[:, c * n:(c + 1) * n], by_tile(t), AX.X, ALU.add))
                if c == 0:
                    lk(dve.scalar_tensor_tensor(out=ms, in0=o, scalar=-3 * BIG, in1=ms, op0=ALU.mult, op1=ALU.add))
            lk(dve.tensor_tensor(mf, o1, o2, ALU.add))
            dve.tensor_copy(m_b[:, 0:n, :], by_tile(mf)).then_inc(S["rb"], 1)
            lk(dve.tensor_tensor(den, ssum[:, 0:n], ssum[:, n:2 * n], ALU.add))
            lk(dve.reciprocal(den, den))
            for c in range(2):
                dve.scalar_tensor_tensor(out=r_w[:, c, 0:n], in0=ssum[:, c * n:(c + 1) * n], scalar=0.5,
                                         in1=den, op0=ALU.mult, op1=ALU.mult)
            dve.wait_ge(*S.at("pos", 1))
            lk(dve.tensor_copy(pos, bank[1][:, 0:ne]))
            lk(dve.scalar_tensor_tensor(out=posm, in0=pos, scalar=1.0, in1=mf, op0=ALU.add, op1=ALU.mult))
            lk(dve.tensor_scalar(posm, posm, -1.0, None, ALU.add))
            for c, o in enumerate((o1, o2)):
                lk(dve.tensor_tensor(t, o, pos, ALU.mult))
                lk(dve.tensor_reduce(r_place[:, c, 0:n], by_tile(t), AX.X, ALU.add))
                lk(dve.tensor_tensor(by_tile(t), by_tile(o), cst("eid").unsqueeze(1).to_broadcast(bE), ALU.mult))
                lk(dve.tensor_reduce(r_first[:, c, 0:n], by_tile(t), AX.X, ALU.add))
            lk(dve.tensor_reduce(r_more[:, 0:1], bank[1][:, ne:ne + E], AX.X, ALU.max))
            lk(dve.tensor_scalar(r_more[:, 1:2], r_more[:, 0:1], CAP + 0.5, None, ALU.is_gt))
            for r in range(2, ROUNDS):
                lk(dve.scalar_tensor_tensor(out=r_more[:, 1:2], in0=r_more[:, 0:1], scalar=r * CAP + 0.5,
                                            in1=r_more[:, 1:2], op0=ALU.is_gt, op1=ALU.add))
            dve.tensor_copy(more[:, :], r_more[0:1, 1:2])
            for j in range(n):
                if j >= 2:
                    dve.wait_ge(*S.at("ix", j - 1))
                one_hots(dve, n, j).then_inc(S["ohr"], 1)
            places(dve, lk, n)
            dve.wait_ge(*S.at("ix", n))
            lists(dve, lk, n)

        r_posm = rcol(512, NT * E)
        r_place = rcol(900, 2 * NT).rearrange("p (c i) -> p c i", c=2)
        r_first = rcol(908, 2 * NT).rearrange("p (c i) -> p c i", c=2)
        r_more = rcol(920, 2)

        def one_hots(dve, n, j):
            return dve.tensor_tensor(ohb[j % 2], cst("iota").unsqueeze(1).to_broadcast([P, E, P]),
                                     r_posm[:, j * E:(j + 1) * E].unsqueeze(2).to_broadcast([P, E, P]), ALU.is_equal)

        def places(dve, lk, n):
            for c in range(2):
                place, clamped = r_place[:, c, 0:n], rcol(930, n)
                lk(dve.tensor_scalar(clamped, place, 0.0, CAP - 1.0, ALU.max, ALU.min))
                lk(dve.tensor_tensor(rcol(936, n), clamped, place, ALU.is_equal))
                lk(dve.tensor_tensor(r_wm[:, c, 0:n], r_w[:, c, 0:n], rcol(936, n), ALU.mult))
                lk(dve.tensor_tensor(clamped, clamped, r_first[:, c, 0:n], ALU.add))
                lk(dve.tensor_copy(row[:, c, 0:n], clamped))

        def lists(dve, lk, n):
            acc, acc2 = rcol(824, E), rcol(840, E)
            for j in range(n):
                lk(dve.tensor_reduce(acc2 if j else acc, bank[2 + j][:, 0:2 * E].rearrange("p (e c) -> p e c", c=2),
                                     AX.X, ALU.add))
                if j:
                    lk(dve.tensor_tensor(acc, acc, acc2, ALU.add))
            lk(dve.tensor_copy(idx[:, :], acc))

        def combine(dve, lk, l, n, i):
            a1, a2 = y1[n % 2], y2[n % 2]
            lk(dve.scalar_tensor_tensor(out=a1, in0=a2, scalar=r_wm[:, 1, n:n + 1], in1=a1,
                                        op0=ALU.mult, op1=ALU.add))
            lk(dve.tensor_tensor(a1, a1, modbc[:, kind(i), 2 * D:3 * D], ALU.mult))
            return dve.tensor_tensor(x[:, i, :], x[:, i, :], a1, ALU.add)

        xw_gate = hT
        xw_up = z[:, :, :].rearrange("p i n -> p (i n)")[:, 0:KD * BLK].rearrange("p (k n) -> p k n", k=KD)
        xw_down = carve(12800, KF * D).rearrange("p (k n) -> p k n", k=KF)
        EXPERT_STEPS = 12

        def more_rounds(name, eng, l):
            T = tiles(l)
            n = len(T)
            steps = 2 * n + 1 + E * EXPERT_STEPS + 2 * n + 1
            count = eng.value_load(more[0:1, 0:1], min_val=0, max_val=ROUNDS - 1)
            with eng.If(count > 0):
                with eng.Fori(0, count) as r:
                    done = [0]

                    def step(e=None):
                        done[0] += 1
                        eng.drain().then_inc(s_more[l], 1)
                        if e is None:
                            eng.wait_ge(s_more[l], r * (4 * steps) + 4 * done[0])
                        else:
                            eng.wait_ge(s_more[l], r * (4 * steps) + e * (4 * EXPERT_STEPS) + 4 * done[0])
                        eng.sem_inc(s_passed, 1)

                    for j in range(n):
                        if name == "dve":
                            if j == 0:
                                eng.tensor_scalar(r_posm[:, 0:n * E], r_posm[:, 0:n * E], -float(CAP), None, ALU.add)
                                eng.tensor_scalar(r_place[:, :, 0:n], r_place[:, :, 0:n], -float(CAP), None, ALU.add)
                                eng.drain()
                            one_hots(eng, n, j)
                        step()
                        if name == "pe":
                            for e in range(E):
                                eng.matmul(bank[2 + j][:, 2 * e:2 * e + 2], ohb[j % 2][:, e, :], tok_b[:, T[j], :],
                                           start=True, stop=True)
                        step()
                    if name == "dve":
                        drained = lambda ins: eng.drain()
                        places(eng, drained, n)
                        lists(eng, drained, n)
                    step()
                    before = done[0]
                    with eng.Fori(0, E) as e:
                        if name == "dve":
                            eng.tensor_copy(idxc[:, :], idx[:, bass.ds(e, 1)])
                        if name == "pool":
                            for dst, w in ((xw_gate, "w_expert_gate"), (xw_up, "w_expert_up"),
                                           (xw_down, "w_expert_down")):
                                eng.dma_start(dst[:, :, :], a[w][l].rearrange("e (k p) n -> e p k n", p=P)[
                                    bass.ds(e, 1)].rearrange("e p k n -> p (e k) n")).then_inc(s_xw[l], 16)
                        step(e)
                        if name == "pool":
                            eng.indirect_dma_start(out=xg, out_offset=None, in_=h_dram,
                                                   in_offset=bass.IndirectOffsetOnAxis(ap=idxc[:, :], axis=0)
                                                   ).then_inc(s_xg[l], 16)
                            eng.wait_ge(s_xg[l], r * (16 * E) + e * 16 + 16)
                            eng.wait_ge(s_xw[l], r * (48 * E) + e * 48 + 48)
                            eng.sem_inc(s_passed, 1)
                        step(e)
                        if name == "pe":
                            for k in range(KD):
                                eng.transpose(bank[k // 4][:, (k % 4) * P:(k % 4 + 1) * P],
                                              xg[:, k * P:(k + 1) * P], ident)
                        step(e)
                        for c, who in enumerate(("act", "dve")):
                            if name == who:
                                (eng.copy if c == 0 else eng.tensor_copy)(
                                    xgT[:, 4 * c:4 * c + 4, :], bank[c][:, :].rearrange("p (k t) -> p k t", k=4))
                        step(e)
                        if name == "pe":
                            for c, w in enumerate((xw_gate, xw_up)):
                                for k in range(KD):
                                    eng.matmul(bank[2 + c][:, :], xgT[:, k, :], w[:, k, :], start=k == 0,
                                               stop=k == KD - 1)
                        step(e)
                        if name == "act":
                            eng.activation(tg, bank[2][:, :], ACT.Tanh, scale=0.5)
                        step(e)
                        if name == "dve":
                            eng.scalar_tensor_tensor(out=au, in0=tg, scalar=1.0, in1=bank[2][:, :],
                                                     op0=ALU.add, op1=ALU.mult)
                            eng.drain()
                            eng.tensor_tensor(au, au, bank[3][:, :], ALU.mult)
                        step(e)
                        if name == "pe":
                            for k in range(KF):
                                eng.transpose(bank[4][:, k * P:(k + 1) * P], au[:, k * P:(k + 1) * P], ident)
                        step(e)
                        if name == "act":
                            eng.copy(auT[:, :, :], bank[4][:, :].rearrange("p (k t) -> p k t", k=4))
                        step(e)
                        if name == "pe":
                            for c in range(2):
                                for k in range(KF):
                                    eng.matmul(bank[5 + c][:, :], auT[:, k, :], xw_down[:, k, c * BLK:(c + 1) * BLK],
                                               start=k == 0, stop=k == KF - 1)
                        step(e)
                        if name == "act":
                            eng.copy(ysb[:, 0:BLK], bank[5][:, :])
                        if name == "dve":
                            eng.tensor_copy(ysb[:, BLK:D], bank[6][:, :])
                        step(e)
                        if name == "pool":
                            eng.dma_start(y_dram[bass.ds(e * CAP, CAP), :], ysb).then_inc(s_xy[l], 16)
                            eng.wait_ge(s_xy[l], r * (16 * E) + e * 16 + 16)
                            eng.sem_inc(s_passed, 1)
                        step(e)
                    assert done[0] - before == EXPERT_STEPS
                    done[0] = before + E * EXPERT_STEPS
                    for j, i in enumerate(T):
                        if name == "pool":
                            for c, dst in enumerate((y1[j % 2], y2[j % 2])):
                                eng.indirect_dma_start(out=dst, out_offset=None, in_=y_dram,
                                                       in_offset=bass.IndirectOffsetOnAxis(ap=row[:, c, j:j + 1],
                                                                                           axis=0)
                                                       ).then_inc(s_xc[l], 16)
                            eng.wait_ge(s_xc[l], r * (32 * n) + 32 * (j + 1))
                            eng.sem_inc(s_passed, 1)
                        step()
                        if name == "dve":
                            eng.tensor_scalar(y1[j % 2], y1[j % 2], r_wm[:, 0, j:j + 1], None, ALU.mult)
                            eng.drain()
                            combine(eng, lambda ins: eng.drain(), l, j, i)
                        step()
                        if name == "act":
                            eng.activation(junk, x[:, i, :], ACT.Square, accum_out=small[:, j:j + 1])
                    step()

        B_IN, B_LORA, B_GA, B_GB, B_O, B_OUT = (0, 1, 2), 3, (4, 7), (5, 8), (6, 9), (10, 11)
        IN_COLS = ((0, 512), (512, 512), (1024, 160))
        uq_w = wslot[0][:, 0:2 * 768].rearrange("p (k n) -> p k n", k=2)
        ukv_w = wslot[0][:, 1536:1536 + D]

        @block.sync
        def _(sp):
            sp.dma_start(cvec[:, 0, :], a["c"].rearrange("b (p k) -> p (b k)", k=KD)).then_inc(s_c, 16)
            sp.dma_start(cvec[:, 1, :], a["c_ctx"].rearrange("(p k) -> p k", k=KD)).then_inc(s_c, 16)
            for l in range(DEPTH):
                for b in range(12):
                    s = b % 3
                    if l or b >= 3:
                        sp.wait_ge(w_used[s], l * 4 + b // 3)
                    sp.dma_start(w_view(s), a["w_mod"][l].rearrange("(p k) n -> p k n", k=KD)[
                        :, :, b * BLK:(b + 1) * BLK]
                    ).then_inc(w_full[s], 16)

            def wait_block_used(l, b):
                prev, s = b - 3, b % 3
                if prev < 0:
                    sp.wait_ge(w_used[s], used_base(l))
                    return
                S, n = L[l], len(tiles(l))
                if prev in B_IN:
                    sp.wait_ge(*S.at("p", sum(j[0] <= prev for j in in_jobs(l))))
                elif prev == B_LORA:
                    sp.wait_ge(*S.at("rp", NT))
                elif prev in B_OUT:
                    sp.wait_ge(*S.at("wo", n * (B_OUT.index(prev) + 1)))
                else:
                    half, part = divmod(prev - 4, 3)
                    sp.wait_ge(*S.at("o", 3 * (n * (half + 1) - 1) + part + 1))

            def cols(w, o, n):
                return w.rearrange("(k p) n -> p k n", p=P)[:, :, o:o + n]

            for l in range(DEPTH):
                w_in = a["w_in"][l]
                for b in range(BLOCKS):
                    s, n = slot_of(l, b)
                    wait_block_used(l, b)
                    if b in B_IN:
                        o, w = IN_COLS[b]
                        sp.dma_start(w_view(s, w), cols(w_in, o, w)).then_inc(w_full[s], 16)
                    elif b == B_LORA:
                        sp.dma_start(uq_w, a["w_uq"][l].rearrange("(k p) n -> p k n", p=P)).then_inc(w_full[s], 16)
                        sp.dma_start(ukv_w, a["w_ukv"][l]).then_inc(s_lora_w[l], 16)
                    elif b in B_GA or b in B_GB:
                        half = 0 if b < 7 else 1
                        o = Z_END + (0 if b in B_GA else D) + half * BLK
                        sp.dma_start(w_view(s), cols(w_in, o, BLK)).then_inc(w_full[s], 16)
                    elif b in B_O:
                        half = B_O.index(b)
                        v = w_view(s)
                        sp.dma_start(v[:, 0:4], cols(a["w_o_a"][l], half * BLK, BLK)).then_inc(w_full[s], 16)
                        sp.dma_start(v[:, 4:8], cols(a["w_o_b"][l], half * BLK, BLK)).then_inc(s_ob_w[l], 16)
                    else:
                        sp.dma_start(w_view(s), cols(a["w_out"][l], B_OUT.index(b) * BLK, BLK)).then_inc(w_full[s], 16)

                def load_expert(s, e):
                    w = a[("w_expert_gate", "w_expert_up", "w_expert_down")[s]][l]
                    src = w.rearrange("e (k p) n -> e p k n", p=P)[bass.ds(e, 1)].rearrange("e p k n -> p (e k) n")
                    sp.dma_start(w_view(s) if s < 2 else wd_view, src).then_inc(w_full[s], 16)

                def next_expert(s, e):
                    sp.wait_ge(w_used[s], e + used_base(l))
                    load_expert(s, e)

                for s in range(3):
                    wait_block_used(l, BLOCKS + s)
                    load_expert(s, 0)
                next_expert(0, 1)
                next_expert(1, 1)
                with sp.Fori(2, E) as e:
                    next_expert(0, e)
                    next_expert(1, e)
                    next_expert(2, e - 1)
                next_expert(2, E - 1)

        @block.tensor
        def _(pe):
            def product(dst, lhs, rhs, n, first=True, last=True):
                for k in range(n):
                    ins = pe.matmul(dst, lhs(k), rhs(k), start=first and k == 0, stop=last and k == n - 1)
                return ins

            def transpose_of_h(S, base, j):
                pe.wait_ge(*S.at("h", base + j + 1))
                if base + j >= 2:
                    pe.wait_ge(*S.at("hev", 2 * (base + j - 1)))
                for k in range(KD):
                    ins = pe.transpose(bank[2 * (j % 2) + k // 4][:, (k % 4) * P:(k % 4 + 1) * P],
                                       htok[j % 2][:, k * P:(k + 1) * P], ident)
                    if k % 4 == 3:
                        ins.then_inc(S["tr"], 1)

            pe.wait_ge(s_const, 16)
            pe.wait_ge(s_cs, 1)
            for l in range(DEPTH):
                for b in range(12):
                    s = b % 3
                    pe.wait_ge(w_full[s], (l * 4 + b // 3 + 1) * 16)
                    g = l * 12 + b
                    if g >= 4:
                        pe.wait_ge(s_mevac, g - 3)
                    w = w_view(s)
                    product(bank[4 + g % 4][0:2, :], lambda k: cvec[:, :, k], lambda k: w[:, k, :], KD
                            ).then_inc(w_used[s], 1)
                    j = first_norm_tile(g, 1)
                    if j is not None:
                        transpose_of_h(L[0], 0, j)
            barrier("pe", pe)

            for l in range(DEPTH):
                S = L[l]
                T = tiles(l)
                jobs = in_jobs(l)
                if l:
                    transpose_of_h(S, 0, 0)
                for n, (b, i, o, w) in enumerate(jobs):
                    if l and n + 1 < NT:
                        transpose_of_h(S, 0, n + 1)
                    s, full = slot_of(l, B_IN[b])
                    if n < NT:
                        pe.wait_ge(*S.at("hev", 2 * (max(n, i) + 1)))
                    pe.wait_ge(w_full[s], 16 * full)
                    if n >= 8:
                        pe.wait_ge(*S.at("pev", n - 7))
                    wv = w_view(s, IN_COLS[b][1])
                    ins = product(bank[(n + 4) % 8][:, 0:w], lambda k: hT[:, k, i * P:(i + 1) * P],
                                  lambda k: wv[:, k, 0:w], KD)
                    ins.then_inc(S["p"], 1)
                barrier("pe", pe)
                s, full = slot_of(l, B_LORA)

                def turn_compressed(i):
                    pe.wait_ge(*S.at("rcn", i + 1))
                    if i:
                        pe.wait_ge(*S.at("rt2", i))
                    for c in range(3):
                        ins = pe.transpose(bank[0][:, c * P:(c + 1) * P], cn[:, c * P:(c + 1) * P], ident)
                    ins.then_inc(S["rt1"], 1)

                def expand(i):
                    pe.wait_ge(*S.at("rt2", i + 1))
                    if i == 0:
                        pe.wait_ge(w_full[s], 16 * full)
                        pe.wait_ge(s_lora_w[l], 16)
                    else:
                        pe.wait_ge(*S.at("rpev", i))
                    if i in T:
                        product(bank[1][:, :], lambda k: cT[:, k, :], lambda k: uq_w[:, k, 0:512], 2)
                        product(bank[2][:, 0:256], lambda k: cT[:, k, :], lambda k: uq_w[:, k, 512:768], 2)
                    product(bank[3][:, :], lambda k: cT[:, 2, :], lambda k: ukv_w[:, 0:512], 1)
                    ins = product(bank[4][:, :], lambda k: cT[:, 2, :], lambda k: ukv_w[:, 512:1024], 1)
                    ins.then_inc(S["rp"], 1)

                def turn_q(i):
                    pe.wait_ge(*S.at("rq", i + 1))
                    if i:
                        pe.wait_ge(*S.at("rqe", i))
                    for c in range(4):
                        pe.transpose(bank[5][:, c * P:(c + 1) * P], z[:, i, c * P:(c + 1) * P], ident)
                    for h in range(HEADS):
                        ins = pe.transpose(bank[6 + h // 4][0:HB, (h % 4) * P:(h % 4 + 1) * P],
                                           zq[i % 2][:, h * HB:(h + 1) * HB], ident)
                    ins.then_inc(S["rtq"], 1)

                def turn_k(i):
                    if i in T:
                        pe.wait_ge(*S.at("rqq", i + 1))
                    else:
                        pe.wait_ge(*S.at("rq", i + 1))
                        pe.wait_ge(*S.at("rqe", i))
                    for c in range(2):
                        pe.transpose(bank[5][:, c * P:(c + 1) * P], kdup[i % 2][:, c * P:(c + 1) * P], ident)
                    for h in range(HEADS):
                        ins = pe.transpose(bank[6 + h // 4][0:HB, (h % 4) * P:(h % 4 + 1) * P],
                                           kcat[i % 2][:, h * HB:(h + 1) * HB], ident)
                    ins.then_inc(S["rqT"], 1)

                turn_compressed(0)
                expand(0)
                turn_compressed(1)
                for i in range(NT):
                    if i + 1 < NT:
                        expand(i + 1)
                    if i in T:
                        turn_q(i)
                    if i + 2 < NT:
                        turn_compressed(i + 2)
                    turn_k(i)
                barrier("pe", pe)
                units = attention_units(l)

                def scores(u):
                    g, br, i, h, k0, nk = units[u]
                    if u >= 3:
                        pe.wait_ge(*S.at("ex", u - 2))
                    sl = slice(k0 * P, NT * P)
                    if br == 0:
                        r = slice((h % 2) * HD, (h % 2 + 1) * HD)
                        lhs, rhs = qaT[r, h // 2, i * P:(i + 1) * P], kaT[r, h // 4, sl]
                    else:
                        lhs, rhs = qbT[0:HB, h, i * P:(i + 1) * P], kbT[0:HB, h, sl]
                    pe.matmul(bank[u % 3][:, 0:nk * P], lhs, rhs, start=True, stop=True).then_inc(S["sc"], 1)

                def turn(u):
                    g, br, i, h, k0, nk = units[u]
                    pe.wait_ge(*S.at("ex", u + 1))
                    if u >= 2:
                        pe.wait_ge(*S.at("pte", u - 1))
                    for c in range(nk):
                        ins = pe.transpose(bank[3 + u % 2][:, c * P:(c + 1) * P],
                                           prob[u % 3][:, c * P:(c + 1) * P], ident)
                    ins.then_inc(S["pt"], 1)

                def values(u):
                    g, br, i, h, k0, nk = units[u]
                    pe.wait_ge(*S.at("pte", u + 1))
                    if h == 0 and g >= 2:
                        pe.wait_ge(*S.at("yev", g - 1))
                    for c in range(nk):
                        v = (z[:, k0 + c, Z_VA + (h // 4) * HD:Z_VA + (h // 4 + 1) * HD] if br == 0
                             else vb[:, k0 + c, h * HD:(h + 1) * HD])
                        ins = pe.matmul(bank[5 + g % 2][:, h * HD:(h + 1) * HD], pT[u % 2][:, c, :], v,
                                        start=c == 0, stop=c == nk - 1)
                    ins.then_inc(S["pv"], 1)

                for u in range(len(units) + 3):
                    if u < len(units):
                        scores(u)
                    if 2 <= u < len(units) + 2:
                        turn(u - 2)
                    if u >= 3:
                        values(u - 3)
                barrier("pe", pe)
                for n, i in enumerate(T):
                    if n >= 2:
                        pe.wait_ge(*S.at("yte", 2 * (n - 1)))
                    for br, o in ((0, Z_YA), (1, Z_YB)):
                        for c in range(4):
                            ins = pe.transpose(bank[2 * (n % 2) + br][:, c * P:(c + 1) * P],
                                               z[:, i, o + c * P:o + (c + 1) * P], ident)
                        ins.then_inc(S["yt"], 1)
                barrier("pe", pe)
                n = 0
                for half in range(2):
                    for i in T:
                        sa, fa = slot_of(l, B_GA[half])
                        sb_, fb = slot_of(l, B_GB[half])
                        so, fo = slot_of(l, B_O[half])
                        h_at = lambda k: hT[:, k, i * P:(i + 1) * P]
                        wa, wb, wo = w_view(sa), w_view(sb_), w_view(so)
                        q = 4 * (n % 2)
                        if n >= 2:
                            pe.wait_ge(*S.at("m", n - 1))
                        pe.wait_ge(w_full[sa], 16 * fa)
                        ins = product(bank[q][:, :], h_at, lambda k: wa[:, k, :], KD)
                        ins.then_inc(S["o"], 1)
                        pe.wait_ge(w_full[sb_], 16 * fb)
                        ins = product(bank[q + 1][:, :], h_at, lambda k: wb[:, k, :], KD)
                        ins.then_inc(S["o"], 1)
                        pe.wait_ge(w_full[so], 16 * fo)
                        pe.wait_ge(s_ob_w[l], 16 * (half + 1))
                        product(bank[q + 2][:, :], lambda k: yT[:, 0, k, i * P:(i + 1) * P],
                                lambda k: wo[:, k, :], 4)
                        ins = product(bank[q + 3][:, :], lambda k: yT[:, 1, k, i * P:(i + 1) * P],
                                      lambda k: wo[:, 4 + k, :], 4)
                        ins.then_inc(S["o"], 1)
                        n += 1
                barrier("pe", pe)
                for n, i in enumerate(T):
                    if n >= 2:
                        pe.wait_ge(*S.at("mte", 2 * (n - 1)))
                    for k in range(KD):
                        ins = pe.transpose(bank[2 * (n % 2) + k // 4][:, (k % 4) * P:(k % 4 + 1) * P],
                                           mix[:, i, k * P:(k + 1) * P], ident)
                        if k % 4 == 3:
                            ins.then_inc(S["mt"], 1)
                barrier("pe", pe)
                n = 0
                for half in range(2):
                    s, full = slot_of(l, B_OUT[half])
                    wv = w_view(s)
                    for i in T:
                        pe.wait_ge(w_full[s], 16 * full)
                        if n >= 8:
                            pe.wait_ge(*S.at("xup", n - 7))
                        ins = product(bank[n % 8][:, :], lambda k: hT[:, k, i * P:(i + 1) * P],
                                      lambda k: wv[:, k, :], KD)
                        ins.then_inc(S["wo"], 1)
                        n += 1
                pe.wait_ge(s_wr, 32)
                for j in range(len(T) + 1):
                    if j < len(T):
                        transpose_of_h(S, NT, j)
                    if j:
                        i = T[j - 1]
                        pe.wait_ge(*S.at("hev", 2 * (NT + j)))
                        ins = product(bank[4][:, (j - 1) * E:j * E], lambda k: hT[:, k, i * P:(i + 1) * P],
                                      lambda k: wr[:, k, :], KD)
                ins.then_inc(S["lg"], 1)
                pe.wait_ge(*S.at("rb", 1))
                for n, i in enumerate(T):
                    for j in range(n):
                        pe.matmul(bank[1][:, n * E:(n + 1) * E], ones_b, m_b[:, j, :], start=j == 0, stop=False)
                    ins = pe.matmul(bank[1][:, n * E:(n + 1) * E], tri_b, m_b[:, n, :], start=n == 0, stop=True)
                for n, i in enumerate(T):
                    ins = pe.matmul(bank[1][:, len(T) * E:(len(T) + 1) * E], ones_b, m_b[:, n, :], start=n == 0,
                                    stop=n == len(T) - 1)
                ins.then_inc(S["pos"], 1)
                for n, i in enumerate(T):
                    pe.wait_ge(*S.at("ohr", n + 1))
                    for e in range(E):
                        ins = pe.matmul(bank[2 + n][:, 2 * e:2 * e + 2], ohb[n % 2][:, e, :], tok_b[:, i, :],
                                        start=True, stop=True)
                    ins.then_inc(S["ix"], 1)
                barrier("pe", pe)

                base = moe_base(l)
                wg, wu = w_view(0), w_view(1)

                def turn_rows(e):
                    pe.wait_ge(*S.at("gat", (e + 1) * 16))
                    for k in range(KD):
                        ins = pe.transpose(bank[k // 4][:, (k % 4) * P:(k % 4 + 1) * P],
                                           xg[:, k * P:(k + 1) * P], ident)
                    ins.then_inc(S["xt"], 1)

                def gate_up(e):
                    pe.wait_ge(*S.at("xte", (e + 1) * 2))
                    pe.wait_ge(w_full[0], (e + base + 1) * 16)
                    product(bank[2][:, :], lambda k: xgT[:, k, :], lambda k: wg[:, k, :], KD).then_inc(w_used[0], 1)
                    pe.wait_ge(w_full[1], (e + base + 1) * 16)
                    product(bank[3][:, :], lambda k: xgT[:, k, :], lambda k: wu[:, k, :], KD).then_inc(w_used[1], 1)

                def down(e):
                    pe.wait_ge(*S.at("ate", e + 1))
                    if not isinstance(e, int) or e:
                        pe.wait_ge(*S.at("ye", e * 2))
                    pe.wait_ge(w_full[2], (e + base + 1) * 16)
                    product(bank[5][:, :], lambda k: auT[:, k, :], lambda k: wd_view[:, k, 0:BLK], KF)
                    product(bank[6][:, :], lambda k: auT[:, k, :], lambda k: wd_view[:, k, BLK:D], KF
                            ).then_inc(w_used[2], 1)

                def turn_act(e):
                    pe.wait_ge(*S.at("au", e + 1))
                    for k in range(KF):
                        ins = pe.transpose(bank[4][:, k * P:(k + 1) * P], au[:, k * P:(k + 1) * P], ident)
                    ins.then_inc(S["at"], 1)

                turn_rows(0)
                gate_up(0)
                turn_rows(1)
                turn_act(0)

                def turn(e):
                    gate_up(e)
                    down(e - 1)
                    turn_rows(e + 1)
                    turn_act(e)

                turn(1)
                with pe.Fori(2, E - 1) as e:
                    turn(e)
                gate_up(E - 1)
                down(E - 2)
                turn_act(E - 1)
                down(E - 1)
                barrier("pe", pe)
                barrier("pe", pe)
                more_rounds("pe", pe, l)
            barrier("pe", pe)

        @block.scalar
        def _(act):
            act.wait_ge(s_c, 32)
            act.activation(cth[:, :, :], cvec[:, :, :], ACT.Tanh, scale=0.5).then_inc(s_cs2, 1)

            def squares(S, base, j, i):
                if base + j:
                    act.wait_ge(*S.at("ss", base + j))
                act.activation(junk, x[:, i, :], ACT.Square, accum_out=small[:, j:j + 1]).then_inc(S["ss"], 1)

            def read_out_h(S, ts, base):
                for j, i in enumerate(ts):
                    for c in range(2):
                        act.wait_ge(*S.at("tr", 2 * (base + j) + c + 1))
                        act.copy(hT[:, 4 * c:4 * c + 4, i * P:(i + 1) * P],
                                 bank[2 * (j % 2) + c][:, :].rearrange("p (k t) -> p k t", k=4)
                                 ).then_inc(S["hev"], 1)

            for l in range(DEPTH):
                S = L[l]
                T = tiles(l)
                if l == 0:
                    act.wait_ge(s_x, 16)
                    act.wait_ge(s_x2, 16)
                    for i in range(NT):
                        squares(S, 0, i, i)
                    read_out_h(S, range(NT), 0)
                    barrier("act", act)
                else:
                    read_out_h(S, range(NT), 0)
                for n, (b, i, o, w) in enumerate(in_jobs(l)):
                    act.wait_ge(*S.at("p", n + 1))
                    act.copy(z[:, i, o:o + w], bank[(n + 4) % 8][:, 0:w]).then_inc(S["pev"], 1)
                barrier("act", act)
                for i in range(NT):
                    if i in T:
                        act.activation(lora_junk[:, i, 0:QR], z[:, i, Z_CQ:Z_CKV], ACT.Square,
                                       accum_out=lora_sum[:, i:i + 1])
                    ins = act.activation(lora_junk[:, i, QR:QR + KVR], z[:, i, Z_CKV:Z_KR], ACT.Square,
                                         accum_out=lora_sum[:, NT + i:NT + i + 1])
                ins.then_inc(S["rz"], 1)

                def read_compressed(i):
                    act.wait_ge(*S.at("rt1", i + 1))
                    if i:
                        act.wait_ge(*S.at("rp", i))
                    act.copy(cT[:, :, :], bank[0][:, 0:384].rearrange("p (c t) -> p c t", c=3)
                             ).then_inc(S["rt2"], 1)

                def read_expanded(i):
                    act.wait_ge(*S.at("rp", i + 1))
                    if i >= 2:
                        act.wait_ge(*S.at("rqT", i - 1))
                    if i in T:
                        act.copy(zq[i % 2][:, 0:512], bank[1][:, :])
                        act.copy(zq[i % 2][:, 512:768], bank[2][:, 0:256])
                    for c in range(2):
                        kv = bank[3 + c][:, :].rearrange("p (h c d) -> p h c d", h=4, c=2)
                        act.copy(kcat[i % 2].rearrange("p (h d) -> p h d", d=HB)[:, 4 * c:4 * c + 4, 0:HD],
                                 kv[:, :, 0, :])
                        ins = act.copy(vb[:, i, c * 256:(c + 1) * 256].rearrange("p (h d) -> p h d", h=4),
                                       kv[:, :, 1, :])
                    ins.then_inc(S["rpev"], 1)

                def read_turned(i, wide, heads_T, src):
                    t = slice(i * P, (i + 1) * P)
                    n = wide.shape[1]
                    act.copy(wide[:, :, t], bank[5][:, 0:n * P].rearrange("p (c t) -> p c t", c=n))
                    for c in range(2):
                        ins = act.copy(heads_T[0:HB, 4 * c:4 * c + 4, t],
                                       bank[6 + c][0:HB, :].rearrange("p (c t) -> p c t", c=4))
                    ins.then_inc(S[src], 1)

                read_compressed(0)
                read_expanded(0)
                read_compressed(1)
                for i in range(NT):
                    if i + 1 < NT:
                        read_expanded(i + 1)
                    if i in T:
                        act.wait_ge(*S.at("rtq", i + 1))
                        read_turned(i, qaT, qbT, "rqq")
                    if i + 2 < NT:
                        read_compressed(i + 2)
                    act.wait_ge(*S.at("rqT", i + 1))
                    read_turned(i, kaT, kbT, "rqe")
                barrier("act", act)
                units = attention_units(l)
                for u, (g, br, i, h, k0, nk) in enumerate(units):
                    act.wait_ge(*S.at("nm", u + 1))
                    if u >= 3:
                        act.wait_ge(*S.at("pt", u - 2))
                    act.activation(prob[u % 3][:, 0:nk * P], bank[u % 3][:, 0:nk * P], ACT.Exp,
                                   bias=small[:, nm_at(g) + h:nm_at(g) + h + 1], scale=att_scale(br),
                                   accum_out=small[:, 48 + (g % 2) * 8 + h:49 + (g % 2) * 8 + h]
                                   ).then_inc(S["ex"], 1)
                    if u >= 1:
                        read_pT(act, S, units, u - 1)
                    if h == HEADS - 1 and br == 0:
                        act.wait_ge(*S.at("nms", g + 1))
                        act.activation(small[:, 64:64 + HEADS], small[:, 64:64 + HEADS], ACT.Exp
                                       ).then_inc(S["es"], 1)
                read_pT(act, S, units, len(units) - 1)
                barrier("act", act)
                for n, i in enumerate(T):
                    for br in range(2):
                        act.wait_ge(*S.at("yt", 2 * n + br + 1))
                        act.copy(yT[:, br, :, i * P:(i + 1) * P],
                                 bank[2 * (n % 2) + br][:, :].rearrange("p (c t) -> p c t", c=4)
                                 ).then_inc(S["yte"], 1)
                barrier("act", act)
                for n in range(2 * len(T)):
                    q = 4 * (n % 2)
                    if n >= 1:
                        act.wait_ge(*S.at("m", n))
                    for c in range(2):
                        act.wait_ge(*S.at("o", 3 * n + c + 1))
                        act.activation(sg[c], bank[q + c][:, :], ACT.Tanh, scale=0.5).then_inc(S["sg"], 1)
                barrier("act", act)
                for n, i in enumerate(T):
                    for c in range(2):
                        act.wait_ge(*S.at("mt", 2 * n + c + 1))
                        act.copy(hT[:, 4 * c:4 * c + 4, i * P:(i + 1) * P],
                                 bank[2 * (n % 2) + c][:, :].rearrange("p (k t) -> p k t", k=4)
                                 ).then_inc(S["mte"], 1)
                barrier("act", act)
                for j, i in enumerate(T):
                    act.wait_ge(*S.at("xup", len(T) + j + 1))
                    squares(S, NT, j, i)
                read_out_h(S, T, NT)
                act.wait_ge(*S.at("lg", 1))
                act.activation(r_sc[:, 0:len(T) * E], bank[4][:, 0:len(T) * E], ACT.Tanh, scale=0.5
                               ).then_inc(S["lge"], 1)
                barrier("act", act)
                base = moe_base(l)

                def read_rows(e):
                    act.wait_ge(*S.at("xt", e + 1))
                    act.copy(xgT[:, 0:4, :], bank[0][:, :].rearrange("p (k t) -> p k t", k=4)).then_inc(S["xte"], 1)

                def tanh_gate(e):
                    act.wait_ge(w_used[0], e + used_base(l) + 1)
                    act.activation(tg, bank[2][:, :], ACT.Tanh, scale=0.5).then_inc(S["th"], 1)

                def read_act(e):
                    act.wait_ge(*S.at("at", e + 1))
                    act.copy(auT[:, :, :], bank[4][:, :].rearrange("p (k t) -> p k t", k=4)).then_inc(S["ate"], 1)

                def read_y(e, dst=ysb):
                    act.wait_ge(w_used[2], e + used_base(l) + 1)
                    if dst is ysb and (not isinstance(e, int) or e):
                        act.wait_ge(*S.at("yst", e * 16))
                    act.copy(dst[:, 0:BLK], bank[5][:, :]).then_inc(S["ye"], 1)

                read_rows(0)
                tanh_gate(0)
                read_rows(1)
                read_act(0)

                def turn(e):
                    tanh_gate(e)
                    read_y(e - 1)
                    read_rows(e + 1)
                    read_act(e)

                turn(1)
                with act.Fori(2, E - 1) as e:
                    turn(e)
                tanh_gate(E - 1)
                read_y(E - 2)
                read_act(E - 1)
                read_y(E - 1, ysb_last)
                barrier("act", act)
                for n in range(len(T) + 1):
                    if n < len(T):
                        act.wait_ge(*S.at(f"g0{n % 2}", 16 * (n // 2 + 1)))
                        act.mul(y1[n % 2], y1[n % 2], r_wm[:, 0, n:n + 1]).then_inc(S["ym"], 1)
                    if n:
                        act.wait_ge(*S.at("f", n))
                        if l < DEPTH - 1:
                            squares(L[l + 1], 0, n - 1, T[n - 1])
                        else:
                            if n > 1:
                                act.wait_ge(s_fin, n - 1)
                            act.activation(junk, x[:, T[n - 1], :], ACT.Square, accum_out=small[:, n - 1:n]
                                           ).then_inc(s_fin, 1)
                barrier("act", act)
                more_rounds("act", act, l)
            barrier("act", act)

        @block.vector
        def _(dve):
            def lk(ins):
                link(dve, ins)

            dve.wait_ge(s_cs2, 1)
            lk(dve.scalar_tensor_tensor(out=cth[:, :, :], in0=cth[:, :, :], scalar=1.0, in1=cvec[:, :, :],
                                        op0=ALU.add, op1=ALU.mult))
            dve.tensor_scalar(cvec[:, :, :], cth[:, :, :], 0.5, None, ALU.mult).then_inc(s_cs, 1)
            dve.wait_ge(s_const, 16)
            dve.tensor_copy(tri_b, cst("tri"))
            dve.memset(ones_b, 1.0)
            for i in range(NT):
                dve.tensor_copy(tok_b[:, i, :], cst(f"tok{i}"))
            def norm_variance(S, n, base):
                dve.wait_ge(*S.at("ss", base + n))
                dve.tensor_scalar(small[:, 8:8 + n], small[:, 0:n], 1.0 / D, EPS, ALU.mult, ALU.add
                                  ).then_inc(S["var"], 1)

            def norm_ready(S, base):
                dve.wait_ge(*S.at("rstd", 1 if base == 0 else 2))
                dve.wait_ge(*S.at("modn", 16 if base == 0 else 32))

            def norm_tile(S, base, j, i):
                if j >= 2:
                    dve.wait_ge(*S.at("tr", 2 * (base + j - 1)))
                    if base:
                        dve.wait_ge(*S.at(f"hst{j % 2}", 16 * (j // 2)))
                lk(dve.scalar_tensor_tensor(out=htok[j % 2], in0=x[:, i, :], scalar=small[:, 12 + j:13 + j],
                                            in1=modbc[:, kind(i), D:2 * D], op0=ALU.mult, op1=ALU.mult))
                dve.tensor_tensor(htok[j % 2], htok[j % 2], modbc[:, kind(i), 0:D], ALU.add
                                  ).then_inc(S["h"], 1)

            for l in range(DEPTH):
                for b in range(12):
                    c = b % 6
                    if c == 0:
                        dve.wait_ge(s_brow, l * 64 + 32 * (b // 6 + 1))
                        if l or b:
                            dve.wait_ge(s_mrow, l * 32 + 16 * (b // 6))
                    bk = bank[4 + (l * 12 + b) % 4]
                    dve.wait_ge(w_used[b % 3], l * 4 + b // 3 + 1)
                    cs = slice(c * BLK, (c + 1) * BLK)
                    if c // 2 != 1:
                        dve.tensor_tensor(mrow[:, cs], bk[0:2, :], brow[:, cs], ALU.add).then_inc(s_mevac, 1)
                    else:
                        dve.wait_ge(s_mevac, l * 12 + b)
                        dve.tensor_tensor(trow, bk[0:2, :], brow[:, cs], ALU.add).then_inc(s_mt, 1)
                        dve.wait_ge(s_mt, l * 4 + (b // 6) * 2 + c - 1)
                        dve.scalar_tensor_tensor(out=mrow[:, cs], in0=trow, scalar=1.0,
                                                 in1=grow[:, (c - 2) * BLK:(c - 1) * BLK],
                                                 op0=ALU.add, op1=ALU.mult).then_inc(s_mevac, 1)
                    if l == 0 and b == 3:
                        norm_variance(L[0], NT, 0)
                    j = first_norm_tile(l * 12 + b, 0)
                    if j is not None:
                        if j == 0:
                            norm_ready(L[0], 0)
                        norm_tile(L[0], 0, j, j)
            barrier("dve", dve)

            def rope(v, dim, heads, name, i):
                n = heads * dim
                d4 = dim // 4
                cos = cst(f"cos_{name}{i}").unsqueeze(1).to_broadcast([P, heads, dim])
                sin = cst(f"sin_{name}{i}").unsqueeze(1).to_broadcast([P, heads, dim])
                vc = rope_c[:, 0:n].rearrange("p (h d) -> p h d", d=dim)
                vs = rope_s[:, 0:n].rearrange("p (h d) -> p h d", d=dim)
                dve.tensor_tensor(vc, v, cos, ALU.mult)
                lk(dve.tensor_tensor(vs, v, sin, ALU.mult))
                for rc in range(2):
                    lo = slice(rc * dim // 2, rc * dim // 2 + d4)
                    hi = slice(rc * dim // 2 + d4, (rc + 1) * dim // 2)
                    dve.tensor_tensor(v[:, :, lo], vc[:, :, lo], vs[:, :, hi], ALU.subtract)
                    ins = dve.tensor_tensor(v[:, :, hi], vc[:, :, hi], vs[:, :, lo], ALU.add)
                return ins

            for l in range(DEPTH):
                S = L[l]
                T = tiles(l)
                if l:
                    norm_variance(S, NT, 0)
                    norm_ready(S, 0)
                    for i in range(NT):
                        norm_tile(S, 0, i, i)
                barrier("dve", dve)
                dve.wait_ge(*S.at("rz", 1))
                dve.wait_ge(*S.at("lorain", 64))
                dve.tensor_scalar(lora_var[:, 0:len(T)], lora_sum[:, 0:len(T)], 1.0 / QR, EPS, ALU.mult, ALU.add)
                if len(T) < NT:
                    dve.memset(lora_var[:, len(T):NT], 1.0)
                dve.tensor_scalar(lora_var[:, NT:], lora_sum[:, NT:], 1.0 / KVR, EPS, ALU.mult, ALU.add
                                  ).then_inc(S["rcv"], 1)
                dve.wait_ge(*S.at("rcr", 1))

                def norm_compressed(i):
                    if i:
                        dve.wait_ge(*S.at("rt1", i))
                    if i in T:
                        dve.scalar_tensor_tensor(out=cn[:, 0:QR], in0=z[:, i, Z_CQ:Z_CKV],
                                                 scalar=lora_rstd[:, i:i + 1],
                                                 in1=lora[:, 0:QR], op0=ALU.mult, op1=ALU.mult)
                    elif i == len(T):
                        dve.memset(cn[:, 0:QR], 0.0)
                    dve.scalar_tensor_tensor(out=cn[:, QR:], in0=z[:, i, Z_CKV:Z_KR],
                                             scalar=lora_rstd[:, NT + i:NT + i + 1],
                                             in1=lora[:, QR:], op0=ALU.mult, op1=ALU.mult).then_inc(S["rcn"], 1)

                norm_compressed(0)
                for i in range(NT):
                    if i < NL:
                        if i:
                            dve.wait_ge(*S.at("rq", i))
                        lk(rope(z[:, i, 0:10 * HD].rearrange("p (h d) -> p h d", d=HD), HD, 10, "a", i))
                        lk(rope(z[:, i, Z_KR:Z_END].rearrange("p (h d) -> p h d", d=RD), RD, 1, "b", i))
                    kd = kdup[i % 2].rearrange("p (g c d) -> p g c d", g=KV_A, c=2)
                    ka = z[:, i, Z_KA:Z_VA].rearrange("p (g d) -> p g d", g=KV_A)
                    if i >= 2:
                        dve.wait_ge(*S.at("rqT", i - 1))
                    for c in range(2):
                        dve.tensor_copy(kd[:, :, c, :], ka)
                    if i + 1 < NT:
                        norm_compressed(i + 1)
                    dve.wait_ge(*S.at("rpev", i + 1))
                    ins = dve.tensor_copy(kcat[i % 2].rearrange("p (h d) -> p h d", d=HB)[:, :, HD:HB],
                                          z[:, i, Z_KR:Z_END].unsqueeze(1).to_broadcast([P, HEADS, RD]))
                    if i < NL:
                        lk(ins)
                        ins = rope(zq[i % 2].rearrange("p (h d) -> p h d", d=HB)[:, :, HD:HB], RD, HEADS, "b", i)
                    ins.then_inc(S["rq"], 1)
                barrier("dve", dve)
                units = attention_units(l)

                def finish(g):
                    u_last = 8 * g + 7
                    _, br, i, _, _, _ = units[u_last]
                    dve.wait_ge(*S.at("ex", u_last + 1))
                    ls = small[:, 48 + (g % 2) * 8:56 + (g % 2) * 8]
                    if br == 0:
                        dve.wait_ge(*S.at("es", g + 1))
                        lk(dve.tensor_tensor(small[:, 72:80], ls, small[:, 64:72], ALU.add))
                        lk(dve.reciprocal(small[:, 80:88], small[:, 72:80]))
                    else:
                        lk(dve.reciprocal(small[:, 80:88], ls))
                    dve.wait_ge(*S.at("pv", u_last + 1))
                    o = Z_YA if br == 0 else Z_YB
                    dve.tensor_tensor(z[:, i, o:o + 512].rearrange("p (h d) -> p h d", d=HD),
                                      bank[5 + g % 2][:, :].rearrange("p (h d) -> p h d", d=HD),
                                      small[:, 80:88].unsqueeze(2).to_broadcast([P, HEADS, HD]), ALU.mult
                                      ).then_inc(S["yev"], 1)

                for u, (g, br, i, h, k0, nk) in enumerate(units):
                    dve.wait_ge(*S.at("sc", u + 1))
                    b = bank[u % 3]
                    if br == 0 and i < NL:
                        cut = b[:, (1 - i) * P:(2 - i) * P]
                        lk(dve.tensor_tensor(cut, cut, cst(f"mask{i}"), ALU.add))
                    lk(dve.tensor_reduce(small[:, 88 + u % 2:89 + u % 2], b[:, 0:nk * P], AX.X, ALU.max))
                    nm = small[:, nm_at(g) + h:nm_at(g) + h + 1]
                    if br == 0:
                        ins = dve.tensor_scalar(nm, small[:, 88 + u % 2:89 + u % 2], -att_scale(br), sinks[:, 8 + h:9 + h],
                                                ALU.mult, ALU.min)
                    else:
                        ins = dve.tensor_scalar(nm, small[:, 88 + u % 2:89 + u % 2], -att_scale(br), None, ALU.mult)
                    ins.then_inc(S["nm"], 1)
                    if h == HEADS - 1 and br == 0:
                        dve.wait_ge(*S.at("nm", u + 1))
                        dve.tensor_tensor(small[:, 64:72], sinks[:, 0:8], small[:, nm_at(g):nm_at(g) + 8], ALU.add
                                          ).then_inc(S["nms"], 1)
                    if h == 3 and g >= 1:
                        finish(g - 1)
                finish(units[-1][0])
                barrier("dve", dve)
                barrier("dve", dve)
                n = 0
                for half in range(2):
                    for i in T:
                        q = 4 * (n % 2)
                        dve.wait_ge(*S.at("sg", 2 * n + 2))
                        dve.wait_ge(*S.at("o", 3 * n + 3))
                        for c in range(2):
                            ins = dve.scalar_tensor_tensor(out=pg[c], in0=sg[c], scalar=1.0, in1=bank[q + 2 + c][:, :],
                                                           op0=ALU.add, op1=ALU.mult)
                        lk(ins)
                        dve.tensor_tensor(mix[:, i, half * BLK:(half + 1) * BLK], pg[0], pg[1], ALU.add
                                          ).then_inc(S["m"], 1)
                        n += 1
                barrier("dve", dve)
                barrier("dve", dve)
                dve.wait_ge(*S.at("modg", 16))
                n = 0
                for half in range(2):
                    cs = slice(half * BLK, (half + 1) * BLK)
                    for i in T:
                        dve.wait_ge(*S.at("wo", n + 1))
                        lk(dve.scalar_tensor_tensor(out=pg[n % 2], in0=bank[n % 8][:, :], scalar=0.5,
                                                    in1=modbc[:, kind(i), 2 * D + half * BLK:2 * D + (half + 1) * BLK],
                                                    op0=ALU.mult, op1=ALU.mult))
                        dve.tensor_tensor(x[:, i, cs], x[:, i, cs], pg[n % 2], ALU.add).then_inc(S["xup"], 1)
                        n += 1
                norm_variance(S, len(T), NT)
                norm_ready(S, NT)
                for j, i in enumerate(T):
                    norm_tile(S, NT, j, i)
                route(dve, lk, S, T)
                barrier("dve", dve)
                base = moe_base(l)

                def read_rows_d(e):
                    dve.wait_ge(*S.at("xt", e + 1))
                    dve.tensor_copy(xgT[:, 4:8, :], bank[1][:, :].rearrange("p (k t) -> p k t", k=4)
                                    ).then_inc(S["xte"], 1)

                def activate(e):
                    dve.wait_ge(*S.at("th", e + 1))
                    dve.scalar_tensor_tensor(out=au, in0=tg, scalar=1.0, in1=bank[2][:, :],
                                             op0=ALU.add, op1=ALU.mult).then_inc(S["aug"], 1)
                    dve.wait_ge(*S.at("aug", e + 1))
                    dve.wait_ge(w_used[1], e + used_base(l) + 1)
                    dve.tensor_tensor(au, au, bank[3][:, :], ALU.mult).then_inc(S["au"], 1)

                def read_y_d(e, dst=ysb):
                    dve.wait_ge(w_used[2], e + used_base(l) + 1)
                    if dst is ysb and (not isinstance(e, int) or e):
                        dve.wait_ge(*S.at("yst", e * 16))
                    dve.tensor_copy(dst[:, BLK:D], bank[6][:, :]).then_inc(S["ye"], 1)

                read_rows_d(0)
                activate(0)
                read_rows_d(1)

                def turn(e):
                    activate(e)
                    read_y_d(e - 1)
                    read_rows_d(e + 1)

                turn(1)
                with dve.Fori(2, E - 1) as e:
                    turn(e)
                activate(E - 1)
                read_y_d(E - 2)
                read_y_d(E - 1, ysb_last)
                barrier("dve", dve)
                dve.wait_ge(*S.at("modg", 32))
                for n, i in enumerate(T):
                    dve.wait_ge(*S.at(f"g1{n % 2}", 16 * (n // 2 + 1)))
                    dve.wait_ge(*S.at("ym", n + 1))
                    combine(dve, lk, l, n, i).then_inc(S["f"], 1)
                dve.wait_ge(*S.at("f", len(T)))
                barrier("dve", dve)
                more_rounds("dve", dve, l)
            dve.wait_ge(s_fin, NL)
            dve.tensor_scalar(small[:, 8:8 + NL], small[:, 0:NL], 1.0 / D, EPS, ALU.mult, ALU.add).then_inc(s_fvar, 1)
            dve.wait_ge(s_frs, 1)
            dve.wait_ge(s_fn, 16)
            for i in range(NL):
                dve.scalar_tensor_tensor(out=htok[i], in0=x[:, i, :], scalar=small[:, 12 + i:13 + i],
                                         in1=modbc[:, 0, 0:D], op0=ALU.mult, op1=ALU.mult).then_inc(s_fout, 1)
            barrier("dve", dve)

        @block.gpsimd
        def _(pool):
            def load_mod(sem_name, l, sub, o, n):
                pool.dma_start(modbc[:, :, o:o + n],
                               mod_dram[l, sub].rearrange("(a t) n -> a t n", a=1)[:, :, o:o + n]
                               .to_broadcast([P, 2, n])).then_inc(L[l][sem_name], 16)

            def load_shifts(l, sub):
                load_mod("modn", l, sub, 0, 2 * D)

            def load_gates(l, sub):
                load_mod("modg", l, sub, 2 * D, D)

            def load_for_layer(l):
                load_shifts(l, 0)
                for dst, w in ((lora[:, 0:QR], "mla_q_norm"), (lora[:, QR:], "mla_kv_norm"),
                               (sinks[:, 0:HEADS], "attn_sink"), (sinks[:, HEADS:], "attn_sink")):
                    pool.dma_start(dst, a[w][l:l + 1, :].to_broadcast([P, dst.shape[1]])
                                   ).then_inc(L[l]["lorain"], 16)

            def inverse_root(S, n, v):
                pool.wait_ge(*S.at("var", v))
                pool.tensor_tensor(small[:, 12:12 + n], small[:, 8:8 + n], cst("minus_half")[:, 0:n], ALU.pow
                                   ).then_inc(S["rstd"], 1)

            pool.dma_start(const[:, :], const_in).then_inc(s_const, 16)
            pool.dma_start(wr[:, :, :], a["w_router"].rearrange("(k p) e -> p k e", p=P)).then_inc(s_wr, 16)
            pool.dma_start(rbias[:, :], a["router_bias"].rearrange("(a e) -> a e", a=1).to_broadcast([P, E])
                           ).then_inc(s_wr, 16)
            pool.dma_start(x[:, 0:NL, :], a["x"].rearrange("b (i p) d -> p (b i) d", p=P)).then_inc(s_x, 16)
            pool.dma_start(x[:, NL:NT, :], a["ctx"].rearrange("b (i p) d -> p (b i) d", p=P)).then_inc(s_x2, 16)
            for l in range(DEPTH):
                for sub, g in enumerate((a["norm_mix"], a["norm_ffn"])):
                    if l or sub:
                        pool.wait_ge(s_mevac, l * 12 + sub * 6)
                    pool.dma_start(brow, a["b_mod"][l:l + 1, sub * MOD:(sub + 1) * MOD].to_broadcast([2, MOD])
                                   ).then_inc(s_brow, 16)
                    pool.dma_start(grow, g[l:l + 1, :].to_broadcast([2, D])).then_inc(s_brow, 16)
                    pool.wait_ge(s_mevac, l * 12 + sub * 6 + 6)
                    pool.dma_start(mod_dram[l, sub], mrow
                                   ).then_inc(s_mrow, 16)
                    if l == 0 and sub == 0:
                        pool.wait_ge(s_mrow, 16)
                        load_for_layer(0)
                        load_gates(0, 0)
                        inverse_root(L[0], NT, 1)
            pool.wait_ge(s_mrow, 16 * 2 * DEPTH)
            barrier("pool", pool)

            for l in range(DEPTH):
                S = L[l]
                T = tiles(l)
                if l:
                    inverse_root(S, NT, 1)
                    load_gates(l, 0)
                pool.wait_ge(*S.at("lorain", 64))
                pool.tensor_scalar(sinks[:, HEADS:], sinks[:, HEADS:], -1.0, None, ALU.mult)
                barrier("pool", pool)
                pool.wait_ge(*S.at("rcv", 1))
                for o in (0, NT):
                    ins = pool.tensor_tensor(lora_rstd[:, o:o + NT], lora_var[:, o:o + NT], cst("minus_half")[:, 0:NT],
                                             ALU.pow)
                ins.then_inc(S["rcr"], 1)
                barrier("pool", pool)
                load_shifts(l, 1)
                for _ in range(4):
                    barrier("pool", pool)
                inverse_root(S, len(T), 2)
                for n, i in enumerate(T):
                    pool.wait_ge(*S.at("h", NT + n + 1))
                    pool.dma_start(h_dram[i * P:(i + 1) * P, :], htok[n % 2]).then_inc(S[f"hst{n % 2}"], 16)
                for j in range(2):
                    pool.wait_ge(*S.at(f"hst{j}", 16 * len(T) // 2))
                barrier("pool", pool)

                def gather(e):
                    pool.indirect_dma_start(out=xg, out_offset=None, in_=h_dram,
                                            in_offset=bass.IndirectOffsetOnAxis(ap=idx[:, e:e + 1], axis=0)
                                            ).then_inc(S["gat"], 16)

                gather(0)
                for e in range(E):
                    if e + 1 < E:
                        pool.wait_ge(*S.at("xt", e + 1))
                        gather(e + 1)
                    if e == 1:
                        load_gates(l, 1)
                    elif e == 3 and l < DEPTH - 1:
                        load_for_layer(l + 1)
                    elif e == 3:
                        pool.dma_start(modbc[:, 0, 0:D], a["final_norm"].rearrange("(a d) -> a d", a=1)
                                       .to_broadcast([P, D])).then_inc(s_fn, 16)
                    if e:
                        pool.wait_ge(*S.at("ye", 2 * e))
                        pool.dma_start(y_dram[(e - 1) * CAP:e * CAP, :], ysb).then_inc(S["yst"], 16)
                pool.wait_ge(*S.at("ye", 2 * E))
                pool.dma_start(y_dram[(E - 1) * CAP:E * CAP, :], ysb_last).then_inc(S["yst"], 16)
                pool.wait_ge(*S.at("yst", 16 * E))
                barrier("pool", pool)
                for n, i in enumerate(T):
                    if n >= 2:
                        pool.wait_ge(*S.at("f", n - 1))
                    for c, (dst, s) in enumerate(((y1[n % 2], S[f"g0{n % 2}"]), (y2[n % 2], S[f"g1{n % 2}"]))):
                        pool.indirect_dma_start(out=dst, out_offset=None, in_=y_dram,
                                                in_offset=bass.IndirectOffsetOnAxis(ap=row[:, c, n:n + 1], axis=0)
                                                ).then_inc(s, 16)
                pool.wait_ge(*S.at("f", len(T)))
                barrier("pool", pool)
                more_rounds("pool", pool, l)
            pool.wait_ge(s_fvar, 1)
            pool.tensor_tensor(small[:, 12:12 + NL], small[:, 8:8 + NL], cst("minus_half")[:, 0:NL], ALU.pow
                               ).then_inc(s_frs, 1)
            for i in range(NL):
                pool.wait_ge(s_fout, i + 1)
                pool.dma_start(out[0, i * P:(i + 1) * P, :], htok[i]).then_inc(s_out, 16)
            pool.wait_ge(s_out, 16 * NL)
            barrier("pool", pool)


_INS = ['x', 'c', 'ctx', 'c_ctx', 'w_mod', 'b_mod', 'norm_mix', 'norm_ffn', 'w_in', 'attn_sink', 'mla_q_norm', 'w_uq',
        'mla_kv_norm', 'w_ukv', 'w_o_a', 'w_o_b', 'w_out', 'w_router', 'router_bias', 'w_expert_gate', 'w_expert_up',
        'w_expert_down', 'final_norm']


def kernel(**inputs):
    import concourse.bacc as bacc
    from concourse.bass_utils import run_bass_kernel_spmd

    nc = bacc.Bacc("TRN2", target_bir_lowering=False, num_devices=1)
    arrays = {f"in_{n}": np.ascontiguousarray(inputs[n]) for n in _INS}
    args = {n: nc.dram_tensor(f"in_{n}", arrays[f"in_{n}"].shape, F32, kind="ExternalInput").ap() for n in _INS}
    arrays["tables"] = CONST
    tables = nc.dram_tensor("tables", CONST.shape, F32, kind="ExternalInput").ap()
    out = nc.dram_tensor("out", (1, SEQ, D), F32, kind="ExternalOutput").ap()
    trunk(nc, args, tables, out)
    r = run_bass_kernel_spmd(nc, [arrays], core_ids=[0])
    return r.results[0]["out"]
```

```python
from contextlib import ExitStack

import numpy as np

import concourse.bass as bass
from concourse import mybir

F32 = mybir.dt.float32
F32R = mybir.dt.float32r
BF16 = mybir.dt.bfloat16
U32 = mybir.dt.uint32
I32 = mybir.dt.int32
ALU = mybir.AluOpType
ACT = mybir.ActivationFunctionType
AX = mybir.AxisListType

P = 128
D = 1024
KD = D // P
SEQ = 256
CTX = 256
NT = (SEQ + CTX) // P
NL = SEQ // P
DEPTH = 2
GRID_W = 64
ROPE_BASE = 10000.0
EPS = 1e-6
HEADS = 8
HD = 64
KV_A = 2
WINDOW = 128
QR, KVR, RD = 256, 128, 32
HB = HD + RD
E = 16
GROUPS = 4
F = 512
KF = F // P
CAP = P
ROUNDS = NT
BLK = 512
Z_QA, Z_KA, Z_VA, Z_CQ, Z_CKV, Z_KR, Z_END = 0, 512, 640, 768, 1024, 1152, 1184
Z_YA, Z_YB, Z_W = 0, 768, 1280
BIG = 1e30
MOD = 3 * D


def constants():
    cols, at = [], {}

    def put(name, a):
        at[name] = (sum(c.shape[1] for c in cols), a.shape[1])
        cols.append(np.asarray(a, np.float32))

    p = np.arange(P)
    put("ident", np.eye(P))
    put("tri", (p[:, None] < p[None, :]))
    put("iota", np.broadcast_to(p[None, :], (P, P)))
    for i in range(NL):
        q, k = i * P + p[:, None], (1 - i) * P + p[None, :]
        put(f"mask{i}", np.where(np.abs(q - k) <= WINDOW, 0.0, -BIG))
    for name, dim in (("a", HD // 2), ("b", RD // 2)):
        inv = (np.float32(ROPE_BASE) ** (-np.arange(0, dim, 2, dtype=np.float32) / np.float32(dim))).astype(np.float32)
        for i in range(NL):
            t = i * P + p
            parts_c, parts_s = [], []
            for pos in (t // GRID_W, t % GRID_W):
                ang = pos.astype(np.float32)[:, None] * inv[None, :]
                parts_c += [np.cos(ang), np.cos(ang)]
                parts_s += [np.sin(ang), np.sin(ang)]
            put(f"cos_{name}{i}", np.concatenate(parts_c, 1))
            put(f"sin_{name}{i}", np.concatenate(parts_s, 1))
    put("rank_g", np.broadcast_to(GROUPS - np.arange(GROUPS)[None], (P, GROUPS)))
    put("rank_e", np.broadcast_to(E - np.arange(E)[None], (P, E)))
    put("eid", np.broadcast_to(np.arange(E)[None] * CAP, (P, E)))
    for i in range(NT):
        put(f"tok{i}", np.stack([p, np.full(P, i * P)], 1))
    put("minus_half", np.full((P, 8), -0.5))
    return np.concatenate(cols, 1), at


CONST, AT = constants()
NCONST = CONST.shape[1]


def trunk(nc, a, const_in, out):
    with ExitStack() as ctx:
        def sb(name, shape, dt=F32):
            return ctx.enter_context(nc.sbuf_tensor(name, shape, dt))

        def sem(name):
            return ctx.enter_context(nc.semaphore(name))

        def dram(name, shape, dt=F32):
            return nc.dram_tensor(name, shape, dt).ap()

        mod_dram = dram("mod_rows", (DEPTH, 2, 2, MOD))
        h_dram = dram("h_rows", (NT * P, D))
        y_dram = dram("y_rows", (E * CAP, D))

        const = sb("const", [P, NCONST])

        def cst(name):
            o, n = AT[name]
            return const[:, o:o + n]

        ident = cst("ident")
        x = sb("x_tok", [P, NT, D])
        wslot = [sb(f"wslot{s}", [P, KD * BLK]) for s in range(3)]
        modbc = sb("modbc", [P, 2, MOD])
        z = sb("z", [P, NT, Z_W])
        SHARED = (17408, KD * NT * P, 1600)
        with ExitStack() as shared:
            arena = shared.enter_context(nc.sbuf_tensor("arena", [P, SHARED[0]], F32))
            hT = shared.enter_context(nc.sbuf_tensor("hT", [P, KD, NT * P], F32))
            rt = shared.enter_context(nc.sbuf_tensor("rt", [P, SHARED[2]], F32))
        rounded = sb("rounded", [P, sum(SHARED)], F32R)

        def carve(o, n):
            return arena[:, o:o + n]

        def carve_rounded(o, n):
            return rounded[:, o:o + n]

        qaT = [v.rearrange("p (h t) -> p h t", h=HEADS // 2) for v in (carve(0, 2048), modbc[:, 1, 0:2048])]
        kaT = carve(2048, 1024).rearrange("p (c t) -> p c t", c=2)
        vb = carve(3072, 2048).rearrange("p (i n) -> p i n", i=NT)
        qbT = carve(5120, 4096).rearrange("p (h t) -> p h t", h=HEADS)
        kbT = carve(9216, 4096).rearrange("p (h t) -> p h t", h=HEADS)
        rope_c = carve(13312, 640)
        rope_s = carve(13952, 640)
        zq = [carve(14592, 768), modbc[:, 0, 0:768]]
        kcat = [carve(15360, 768), modbc[:, 0, 768:1536]]
        kdup = [carve(16128, 256), modbc[:, 0, 1536:1792]]
        lora_sum, lora_var, lora_rstd = (rt[:, o:o + 2 * NT] for o in (1520, 1528, 1536))
        lora_junk = carve(14336, NT * (QR + KVR)).rearrange("p (i n) -> p i n", i=NT)
        cn = carve(16384, 384)
        cT = carve(16768, 384).rearrange("p (c t) -> p c t", c=3)
        prob = [carve(13312 + 512 * j, 512) for j in range(3)]
        pT = [carve(14848 + 512 * j, 512).rearrange("p (c t) -> p c t", c=4) for j in range(2)]

        def parts(o):
            return carve_rounded(o, BLK), carve_rounded(o + BLK, BLK)

        z_flat = z[:, :, :].rearrange("p i n -> p (i n)")
        in_hi, in_lo = (carve_rounded(o, KD * NT * P).rearrange("p (k t) -> p k t", k=KD) for o in (3072, 7168))
        in_ring = [parts(11264 + 2 * BLK * j) for j in range(3)]
        oh_hi = carve_rounded(0, KD * NT * P).rearrange("p (k t) -> p k t", k=KD)
        out_ring = [parts(4096), parts(15360), parts(SHARED[0] + SHARED[1])]
        y_hi, y_lo = (carve_rounded(o, 4096).rearrange("p (b c t) -> p b c t", b=2, c=4) for o in (5120, 9216))
        mix = z_flat[:, 0:4096].rearrange("p (i n) -> p i n", i=NT)
        sg = [carve(13312 + BLK * j, BLK) for j in range(NT)]
        pg = [carve(16384 + BLK * j, BLK) for j in range(2)]
        m_lo = carve_rounded(5120, KD * NT * P).rearrange("p (k t) -> p k t", k=KD)

        hT_rounded = carve_rounded(SHARED[0], SHARED[1]).rearrange("p (k t) -> p k t", k=KD)

        def exact(v):
            return v.bitcast(F32)

        htok = [carve(1024 * j, 1024) for j in range(2)]
        junk = carve(2048, 1024)
        xg = carve(4096, 1024)
        xgT = carve(5120, 1024).rearrange("p (k t) -> p k t", k=KD)
        tg = carve(6144, 512)
        au = carve(6656, 512)
        auT = carve(7168, 512).rearrange("p (k t) -> p k t", k=KF)
        auT_hi, auT_lo = (carve_rounded(o, 512).rearrange("p (k t) -> p k t", k=KF) for o in (7168, 16896))
        wd_hi, wd_lo = (carve_rounded(o, KF * D).rearrange("p (k n) -> p k n", k=KF) for o in (8704, 12800))
        ysb = carve(7680, 1024)
        ysb_last = carve(3072, 1024)
        y1 = [carve(8704 + 2048 * j, 1024) for j in range(NT)]
        y2 = [carve(9728 + 2048 * j, 1024) for j in range(NT)]
        oh = carve(13312, E * CAP).rearrange("p (j n) -> p j n", j=2)
        ohb = [oh[:, j].bitcast(BF16).rearrange("p (e s) -> p e s", e=E) for j in range(2)]
        small = sb("small", [P, 96])
        bf = sb("bf", [P, 2 * P + NT * E + 2 * NT], BF16)
        tri_b, ones_b = bf[:, 0:P], bf[:, P:2 * P]
        m_b = bf[:, 2 * P:2 * P + NT * E].rearrange("p (i e) -> p i e", e=E)
        tok_b = bf[:, 2 * P + NT * E:].rearrange("p (i c) -> p i c", c=2)
        idx = sb("idx", [P, E], U32)
        row = sb("row", [P, 2, NT], U32)
        idxc = sb("idxc", [P, 1], U32)
        more = sb("more", [1, 1], I32)
        sinks = sb("sinks", [P, 2 * HEADS])
        lora = sb("lora", [P, QR + KVR])
        wr = sb("wr", [P, KD, E])
        rbias = sb("rbias", [P, E])
        cvec = sb("cvec", [P, 2, KD])
        cth = sb("cth", [P, 2, KD])
        mrow = z[0:2, :, :].rearrange("p i n -> p (i n)")[:, 0:MOD]
        brow = arena[0:2, 14336:14336 + MOD]
        grow = arena[0:2, 11264:11264 + D]
        trow = arena[0:2, 11264 + D:11264 + D + BLK]

        bank = [ctx.enter_context(nc.psum_tensor(f"bank{j}", [P, BLK], F32)) for j in range(8)]

        s_stage = sem("stage_end")
        w_full = [sem(f"w_full{s}") for s in range(3)]
        w_used = [sem(f"w_used{s}") for s in range(3)]
        s_const = sem("const_in")
        s_c = sem("c_in")
        s_x = sem("x_in")
        s_cs = sem("silu_c")
        s_brow = sem("bias_row_in")
        s_mevac = sem("mod_evac")
        s_mrow = sem("mod_row_out")
        s_link = sem("dve_link")
        counts = dict(
            modn=32, modg=32, ss=2 * NT, var=2, rstd=2, h=2 * NT, tr=4 * NT, hev=4 * NT, lorain=64, pev=3 * NT,
            rz=1, rcv=1, rcr=2, rcn=NT, rtq=NT, rqq=NT, rt1=NT, rt2=NT, rp=NT, rpev=NT, rq=NT, rqT=NT, rqe=NT,
            sc=2 * NT * HEADS, nm=2 * NT * HEADS, ex=2 * NT * HEADS, pt=2 * NT * HEADS, pte=2 * NT * HEADS,
            pv=2 * NT * HEADS, nms=NT, es=NT, yev=2 * NT, yt=2 * NT, sg=4 * NT, m=4 * NT,
            sh=6 * NT, sl=6 * NT, wh=88, wl=88, wu=88, mt=2 * NT, xup=2 * NT, hst0=8 * NT, hst1=8 * NT, lg=1, lge=1, rb=1, pos=1,
            ohr=NT, ix=NT, gat=16 * E, xt=E, xte=2 * E, th=E, aug=E, au=E, at=E, ath=E, ate=E, dh=KF * E, dl=KF * E, ye=2 * E, yst=16 * (E - 1), ylast=16,
            g00=16, g01=16, g02=16, g03=16, g10=16, g11=16, g12=16, g13=16, f=NT, ym=NT)
        signals = {n: sem(n) for n in counts}

        class Layer:

            def __init__(self, l):
                self.l = l

            def __getitem__(self, name):
                return signals[name]

            def at(self, name, n):
                return signals[name], n + self.l * counts[name]

        L = [Layer(l) for l in range(DEPTH)]
        s_out = sem("out_dma")
        s_fin = sem("final")

        s_cs2 = sem("tanh_c")
        s_mt = sem("scale_row")
        s_wr = sem("router_in")
        s_x2 = sem("ctx_in")
        s_lora_w = [sem(f"w_ukv_in_{l}") for l in range(DEPTH)]
        s_ob_w = [sem(f"w_o_b_in_{l}") for l in range(DEPTH)]
        s_passed = sem("step_passed")
        s_more = [sem(f"more_step_{l}") for l in range(DEPTH)]
        s_xw = [sem(f"more_weights_in_{l}") for l in range(DEPTH)]
        s_xg = [sem(f"more_rows_in_{l}") for l in range(DEPTH)]
        s_xy = [sem(f"more_results_out_{l}") for l in range(DEPTH)]
        s_xc = [sem(f"more_results_in_{l}") for l in range(DEPTH)]
        s_fvar, s_frs, s_fn, s_fout = sem("final_var"), sem("final_rstd"), sem("final_norm_in"), sem("final_out")

        block = ctx.enter_context(nc.Block())
        stages = {}

        def barrier(name, eng):
            n = stages[name] = stages.get(name, 0) + 1
            eng.drain().then_inc(s_stage, 1)
            eng.wait_ge(s_stage, 4 * n)

        links = [0]

        def link(dve, ins):
            links[0] += 1
            ins.then_inc(s_link, 1)
            dve.wait_ge(s_link, links[0])

        def tiles(l):
            return range(NT) if l < DEPTH - 1 else range(NL)

        def kind(i):
            return 0 if i < NL else 1

        B_IN, B_LORA, B_GA, B_GB, B_O, B_OUT = (0, 1, 2), 3, (4, 7), (5, 8), (6, 9), (10, 11)
        IN_COLS = ((0, 512), (512, 512), (1024, 160))
        MOD_PER_SLOT = DEPTH * 12 // 3

        def first_norm_tile(b, late):
            j, odd = divmod(b - 12 - late, 2)
            return j if odd == 0 and 0 <= j < NT else None

        BLOCKS = 12

        def slot_of(l, b):
            return b % 3, MOD_PER_SLOT + l * (BLOCKS // 3 + E) + b // 3 + 1

        def moe_base(l):
            return MOD_PER_SLOT + l * (BLOCKS // 3 + E) + BLOCKS // 3

        def used_base(l):
            return MOD_PER_SLOT + l * E

        def w_view(s, n=BLK):
            return wslot[s][:, 0:KD * n].rearrange("p (k n) -> p k n", k=KD)

        wd_view = wslot[2][:, :].rearrange("p (k n) -> p k n", k=KF)

        def in_jobs(l, b):
            T = tiles(l) if b == 0 else range(NT)
            return [(i, IN_COLS[b][0], 256 if b == 1 and i not in tiles(l) else IN_COLS[b][1]) for i in T]

        def in_split(i):
            return i

        def h_split(n):
            return NT + n

        def y_split(l, n, br):
            return NT + len(tiles(l)) + 2 * n + br

        def m_split(l, n, c):
            return NT + 3 * len(tiles(l)) + 2 * n + c

        def out_blocks():
            at = 3 * KD
            for half in range(2):
                for br, gate in enumerate((B_GA, B_GB)):
                    yield gate[half], 0, KD, at, half, None
                    at += KD
                    yield B_O[half], 4 * br, 4, at, half, br
                    at += 4

        OUT_CHUNK = 3 * KD + 2 * (2 * KD + 2 * 4)

        def attention_units(l):
            groups = [(br, i) for br in range(2) for i in tiles(l)]
            return [(g, br, i, h, 0 if i < NL else NL, NT if i < NL else NT - NL)
                    for g, (br, i) in enumerate(groups) for h in range(HEADS)]

        def att_scale(br):
            return (HD if br == 0 else HB) ** -0.5

        def nm_at(g):
            return 24 + (g % 2) * 8

        def read_pT(act, S, units, u):
            g, br, i, h, k0, nk = units[u]
            act.wait_ge(*S.at("pt", u + 1))
            if u >= 2:
                act.wait_ge(*S.at("pv", u - 1))
            act.copy(pT[u % 2][:, 0:nk, :], bank[3 + u % 2][:, 0:nk * P].rearrange("p (c t) -> p c t", c=nk)
                     ).then_inc(S["pte"], 1)

        def rcol(o, n):
            return rt[:, o:o + n]

        r_sc = rcol(0, NT * E)
        r_w = rcol(1500, 2 * NT).rearrange("p (c i) -> p c i", c=2)
        r_wm = rcol(1508, 2 * NT).rearrange("p (c i) -> p c i", c=2)

        def route(dve, lk, S, T):
            n = len(T)
            ne = n * E

            def by_tile(v, m=E):
                return v.rearrange("p (i e) -> p i e", i=n)

            def over(v, m):
                return v.unsqueeze(2).to_broadcast([P, v.shape[1], m])

            sc, sel, ms, w, t = (rcol(64 * j, ne) for j in (0, 1, 2, 3, 4))
            o1, o2 = rcol(320, ne), rcol(384, ne)
            mf, posm, pos = rcol(448, ne), rcol(512, ne), rcol(576, ne)
            pair = rcol(640, n * GROUPS * 6).rearrange("p (g c) -> p g c", c=6)
            gs, w4, pen = rcol(740, n * GROUPS), rcol(756, n * GROUPS), rcol(772, n * GROUPS)
            gm = rcol(788, n)
            m1 = rcol(792, n)
            ssum = rcol(796, 2 * n)
            den = rcol(804, n)
            bE = [P, n, E]
            dve.wait_ge(*S.at("lge", 1))
            dve.wait_ge(s_wr, 32)
            lk(dve.tensor_scalar(sc, sc, 0.5, 0.5, ALU.mult, ALU.add))
            lk(dve.tensor_tensor(by_tile(sel), by_tile(sc), rbias[:, :].unsqueeze(1).to_broadcast(bE), ALU.add))
            g4 = sel.rearrange("p (g c) -> p g c", c=4)
            dve.tensor_tensor(pair[:, :, 0:3], g4[:, :, 0:3], g4[:, :, 1:4], ALU.add)
            dve.tensor_tensor(pair[:, :, 3:5], g4[:, :, 0:2], g4[:, :, 2:4], ALU.add)
            lk(dve.tensor_tensor(pair[:, :, 5:6], g4[:, :, 0:1], g4[:, :, 3:4], ALU.add))
            lk(dve.tensor_reduce(gs, pair, AX.X, ALU.max))
            lk(dve.tensor_reduce(gm, by_tile(gs), AX.X, ALU.max))
            lk(dve.tensor_tensor(by_tile(w4), by_tile(gs), over(gm, GROUPS), ALU.is_equal))
            lk(dve.tensor_tensor(by_tile(w4), by_tile(w4),
                                 cst("rank_g").unsqueeze(1).to_broadcast([P, n, GROUPS]), ALU.mult))
            lk(dve.tensor_reduce(gm, by_tile(w4), AX.X, ALU.max))
            lk(dve.tensor_tensor(by_tile(w4), by_tile(w4), over(gm, GROUPS), ALU.is_equal))
            lk(dve.tensor_scalar(pen, w4, -1.0, BIG, ALU.add, ALU.mult))
            lk(dve.tensor_tensor(ms.rearrange("p (g c) -> p g c", c=4), g4, over(pen, 4), ALU.add))
            for c, o in enumerate((o1, o2)):
                lk(dve.tensor_reduce(m1, by_tile(ms), AX.X, ALU.max))
                lk(dve.tensor_tensor(by_tile(w), by_tile(ms), over(m1, E), ALU.is_equal))
                lk(dve.tensor_tensor(by_tile(w), by_tile(w), cst("rank_e").unsqueeze(1).to_broadcast(bE), ALU.mult))
                lk(dve.tensor_reduce(m1, by_tile(w), AX.X, ALU.max))
                lk(dve.tensor_tensor(by_tile(o), by_tile(w), over(m1, E), ALU.is_equal))
                lk(dve.tensor_tensor(t, o, sc, ALU.mult))
                lk(dve.tensor_reduce(ssum[:, c * n:(c + 1) * n], by_tile(t), AX.X, ALU.add))
                if c == 0:
                    lk(dve.scalar_tensor_tensor(out=ms, in0=o, scalar=-3 * BIG, in1=ms, op0=ALU.mult, op1=ALU.add))
            lk(dve.tensor_tensor(mf, o1, o2, ALU.add))
            dve.tensor_copy(m_b[:, 0:n, :], by_tile(mf)).then_inc(S["rb"], 1)
            lk(dve.tensor_tensor(den, ssum[:, 0:n], ssum[:, n:2 * n], ALU.add))
            lk(dve.reciprocal(den, den))
            for c in range(2):
                dve.scalar_tensor_tensor(out=r_w[:, c, 0:n], in0=ssum[:, c * n:(c + 1) * n], scalar=0.5,
                                         in1=den, op0=ALU.mult, op1=ALU.mult)
            dve.wait_ge(*S.at("pos", 1))
            lk(dve.tensor_copy(pos, bank[1][:, 0:ne]))
            lk(dve.scalar_tensor_tensor(out=posm, in0=pos, scalar=1.0, in1=mf, op0=ALU.add, op1=ALU.mult))
            lk(dve.tensor_scalar(posm, posm, -1.0, None, ALU.add))
            lk(dve.tensor_copy(r_len, bank[1][:, ne:ne + E]))
            for j in range(n):
                if j >= 2:
                    dve.wait_ge(*S.at("ix", j - 1))
                one_hots(dve, n, j).then_inc(S["ohr"], 1)
            dve.wait_ge(*S.at("ix", n))
            lists(dve, lk, n)

        def route_rest(dve, lk, T):
            n = len(T)
            ne = n * E

            def by_tile(v, m=E):
                return v.rearrange("p (i e) -> p i e", i=n)

            t, pos, o1, o2 = (rcol(o, ne) for o in (256, 576, 320, 384))
            bE = [P, n, E]
            for c, o in enumerate((o1, o2)):
                lk(dve.tensor_tensor(t, o, pos, ALU.mult))
                lk(dve.tensor_reduce(r_place[:, c, 0:n], by_tile(t), AX.X, ALU.add))
                lk(dve.tensor_tensor(by_tile(t), by_tile(o), cst("eid").unsqueeze(1).to_broadcast(bE), ALU.mult))
                lk(dve.tensor_reduce(r_first[:, c, 0:n], by_tile(t), AX.X, ALU.add))
            lk(dve.tensor_reduce(r_more[:, 0:1], r_len, AX.X, ALU.max))
            lk(dve.tensor_scalar(r_more[:, 1:2], r_more[:, 0:1], CAP + 0.5, None, ALU.is_gt))
            for r in range(2, ROUNDS):
                lk(dve.scalar_tensor_tensor(out=r_more[:, 1:2], in0=r_more[:, 0:1], scalar=r * CAP + 0.5,
                                            in1=r_more[:, 1:2], op0=ALU.is_gt, op1=ALU.add))
            dve.tensor_copy(more[:, :], r_more[0:1, 1:2])
            places(dve, lk, n)

        r_posm = rcol(512, NT * E)
        r_place = rcol(900, 2 * NT).rearrange("p (c i) -> p c i", c=2)
        r_first = rcol(908, 2 * NT).rearrange("p (c i) -> p c i", c=2)
        r_more = rcol(920, 2)
        r_len = rcol(860, E)

        def one_hots(dve, n, j):
            return dve.tensor_tensor(ohb[j % 2], cst("iota").unsqueeze(1).to_broadcast([P, E, P]),
                                     r_posm[:, j * E:(j + 1) * E].unsqueeze(2).to_broadcast([P, E, P]), ALU.is_equal)

        def places(dve, lk, n):
            for c in range(2):
                place, clamped = r_place[:, c, 0:n], rcol(930, n)
                lk(dve.tensor_scalar(clamped, place, 0.0, CAP - 1.0, ALU.max, ALU.min))
                lk(dve.tensor_tensor(rcol(936, n), clamped, place, ALU.is_equal))
                lk(dve.tensor_tensor(r_wm[:, c, 0:n], r_w[:, c, 0:n], rcol(936, n), ALU.mult))
                lk(dve.tensor_tensor(clamped, clamped, r_first[:, c, 0:n], ALU.add))
                lk(dve.tensor_copy(row[:, c, 0:n], clamped))

        def lists(dve, lk, n):
            acc, acc2 = rcol(824, E), rcol(840, E)
            for j in range(n):
                lk(dve.tensor_reduce(acc2 if j else acc, bank[2 + j][:, 0:2 * E].rearrange("p (e c) -> p e c", c=2),
                                     AX.X, ALU.add))
                if j:
                    lk(dve.tensor_tensor(acc, acc, acc2, ALU.add))
            lk(dve.tensor_copy(idx[:, :], acc))

        def combine(dve, lk, l, n, i):
            a1, a2 = y1[n], y2[n]
            lk(dve.scalar_tensor_tensor(out=a1, in0=a2, scalar=r_wm[:, 1, n:n + 1], in1=a1,
                                        op0=ALU.mult, op1=ALU.add))
            lk(dve.tensor_tensor(a1, a1, modbc[:, kind(i), 2 * D:3 * D], ALU.mult))
            return dve.tensor_tensor(x[:, i, :], x[:, i, :], a1, ALU.add)

        xw_gate = hT
        xw_up = z[:, :, :].rearrange("p i n -> p (i n)")[:, 0:KD * BLK].rearrange("p (k n) -> p k n", k=KD)
        xw_down = carve(12800, KF * D).rearrange("p (k n) -> p k n", k=KF)
        EXPERT_STEPS = 12

        def more_rounds(name, eng, l):
            T = tiles(l)
            n = len(T)
            steps = 2 * n + 1 + E * EXPERT_STEPS + 2 * n + 1
            count = eng.value_load(more[0:1, 0:1], min_val=0, max_val=ROUNDS - 1)
            with eng.If(count > 0):
                with eng.Fori(0, count) as r:
                    done = [0]

                    def step(e=None):
                        done[0] += 1
                        eng.drain().then_inc(s_more[l], 1)
                        if e is None:
                            eng.wait_ge(s_more[l], r * (4 * steps) + 4 * done[0])
                        else:
                            eng.wait_ge(s_more[l], r * (4 * steps) + e * (4 * EXPERT_STEPS) + 4 * done[0])
                        eng.sem_inc(s_passed, 1)

                    for j in range(n):
                        if name == "dve":
                            if j == 0:
                                eng.tensor_scalar(r_posm[:, 0:n * E], r_posm[:, 0:n * E], -float(CAP), None, ALU.add)
                                eng.tensor_scalar(r_place[:, :, 0:n], r_place[:, :, 0:n], -float(CAP), None, ALU.add)
                                eng.drain()
                            one_hots(eng, n, j)
                        step()
                        if name == "pe":
                            for e in range(E):
                                eng.matmul(bank[2 + j][:, 2 * e:2 * e + 2], ohb[j % 2][:, e, :], tok_b[:, T[j], :],
                                           start=True, stop=True)
                        step()
                    if name == "dve":
                        drained = lambda ins: eng.drain()
                        places(eng, drained, n)
                        lists(eng, drained, n)
                    step()
                    before = done[0]
                    with eng.Fori(0, E) as e:
                        if name == "dve":
                            eng.tensor_copy(idxc[:, :], idx[:, bass.ds(e, 1)])
                        if name == "pool":
                            for dst, w in ((xw_gate, "w_expert_gate"), (xw_up, "w_expert_up"),
                                           (xw_down, "w_expert_down")):
                                eng.dma_start(dst[:, :, :], a[w][l].rearrange("e (k p) n -> e p k n", p=P)[
                                    bass.ds(e, 1)].rearrange("e p k n -> p (e k) n")).then_inc(s_xw[l], 16)
                        step(e)
                        if name == "pool":
                            eng.indirect_dma_start(out=xg, out_offset=None, in_=h_dram,
                                                   in_offset=bass.IndirectOffsetOnAxis(ap=idxc[:, :], axis=0)
                                                   ).then_inc(s_xg[l], 16)
                            eng.wait_ge(s_xg[l], r * (16 * E) + e * 16 + 16)
                            eng.wait_ge(s_xw[l], r * (48 * E) + e * 48 + 48)
                            eng.sem_inc(s_passed, 1)
                        step(e)
                        if name == "pe":
                            for k in range(KD):
                                eng.transpose(bank[k // 4][:, (k % 4) * P:(k % 4 + 1) * P],
                                              xg[:, k * P:(k + 1) * P], ident)
                        step(e)
                        for c, who in enumerate(("act", "dve")):
                            if name == who:
                                (eng.copy if c == 0 else eng.tensor_copy)(
                                    xgT[:, 4 * c:4 * c + 4, :], bank[c][:, :].rearrange("p (k t) -> p k t", k=4))
                        step(e)
                        if name == "pe":
                            for c, w in enumerate((xw_gate, xw_up)):
                                for k in range(KD):
                                    eng.matmul(bank[2 + c][:, :], xgT[:, k, :], w[:, k, :], start=k == 0,
                                               stop=k == KD - 1)
                        step(e)
                        if name == "act":
                            eng.activation(tg, bank[2][:, :], ACT.Tanh, scale=0.5)
                        step(e)
                        if name == "dve":
                            eng.scalar_tensor_tensor(out=au, in0=tg, scalar=1.0, in1=bank[2][:, :],
                                                     op0=ALU.add, op1=ALU.mult)
                            eng.drain()
                            eng.tensor_tensor(au, au, bank[3][:, :], ALU.mult)
                        step(e)
                        if name == "pe":
                            for k in range(KF):
                                eng.transpose(bank[4][:, k * P:(k + 1) * P], au[:, k * P:(k + 1) * P], ident)
                        step(e)
                        if name == "act":
                            eng.copy(auT[:, :, :], bank[4][:, :].rearrange("p (k t) -> p k t", k=4))
                        step(e)
                        if name == "pe":
                            for c in range(2):
                                for k in range(KF):
                                    eng.matmul(bank[5 + c][:, :], auT[:, k, :], xw_down[:, k, c * BLK:(c + 1) * BLK],
                                               start=k == 0, stop=k == KF - 1)
                        step(e)
                        if name == "act":
                            eng.copy(ysb[:, 0:BLK], bank[5][:, :])
                        if name == "dve":
                            eng.tensor_copy(ysb[:, BLK:D], bank[6][:, :])
                        step(e)
                        if name == "pool":
                            eng.dma_start(y_dram[bass.ds(e * CAP, CAP), :], ysb).then_inc(s_xy[l], 16)
                            eng.wait_ge(s_xy[l], r * (16 * E) + e * 16 + 16)
                            eng.sem_inc(s_passed, 1)
                        step(e)
                    assert done[0] - before == EXPERT_STEPS
                    done[0] = before + E * EXPERT_STEPS
                    for j, i in enumerate(T):
                        if name == "pool":
                            for c, dst in enumerate((y1[j], y2[j])):
                                eng.indirect_dma_start(out=dst, out_offset=None, in_=y_dram,
                                                       in_offset=bass.IndirectOffsetOnAxis(ap=row[:, c, j:j + 1],
                                                                                           axis=0)
                                                       ).then_inc(s_xc[l], 16)
                            eng.wait_ge(s_xc[l], r * (32 * n) + 32 * (j + 1))
                            eng.sem_inc(s_passed, 1)
                        step()
                        if name == "dve":
                            eng.tensor_scalar(y1[j], y1[j], r_wm[:, 0, j:j + 1], None, ALU.mult)
                            eng.drain()
                            combine(eng, lambda ins: eng.drain(), l, j, i)
                        step()
                        if name == "act":
                            eng.activation(junk, x[:, i, :], ACT.Square, accum_out=small[:, j:j + 1])
                    step()

        uq_w = wslot[0][:, 0:2 * 768].rearrange("p (k n) -> p k n", k=2)
        ukv_w = wslot[0][:, 1536:1536 + D]

        @block.sync
        def _(sp):
            sp.dma_start(cvec[:, 0, :], a["c"].rearrange("b (p k) -> p (b k)", k=KD)).then_inc(s_c, 16)
            sp.dma_start(cvec[:, 1, :], a["c_ctx"].rearrange("(p k) -> p k", k=KD)).then_inc(s_c, 16)
            for l in range(DEPTH):
                for b in range(12):
                    s = b % 3
                    if l or b >= 3:
                        sp.wait_ge(w_used[s], l * 4 + b // 3)
                    sp.dma_start(w_view(s), a["w_mod"][l].rearrange("(p k) n -> p k n", k=KD)[
                        :, :, b * BLK:(b + 1) * BLK]
                    ).then_inc(w_full[s], 16)

            def wait_block_used(l, b):
                prev, s = b - 3, b % 3
                if prev < 0:
                    sp.wait_ge(w_used[s], used_base(l))
                    return
                S = L[l]
                if prev in B_IN:
                    sp.wait_ge(*S.at("wl", KD * (prev + 1)))
                elif prev == B_LORA:
                    sp.wait_ge(*S.at("rp", NT))
                elif prev in B_OUT:
                    sp.wait_ge(*S.at("wl", OUT_CHUNK + KD * (B_OUT.index(prev) + 1)))
                else:
                    sp.wait_ge(*S.at("wl", max(at + kn for b, _, kn, at, _, _ in out_blocks() if b == prev)))

            def cols(w, o, n):
                return w.rearrange("(k p) n -> p k n", p=P)[:, :, o:o + n]

            for l in range(DEPTH):
                w_in = a["w_in"][l]
                for b in range(BLOCKS):
                    s, n = slot_of(l, b)
                    wait_block_used(l, b)
                    if b in B_IN:
                        o, w = IN_COLS[b]
                        sp.dma_start(w_view(s, w), cols(w_in, o, w)).then_inc(w_full[s], 16)
                    elif b == B_LORA:
                        sp.dma_start(uq_w, a["w_uq"][l].rearrange("(k p) n -> p k n", p=P)).then_inc(w_full[s], 16)
                        sp.dma_start(ukv_w, a["w_ukv"][l]).then_inc(s_lora_w[l], 16)
                    elif b in B_GA or b in B_GB:
                        half = 0 if b < 7 else 1
                        o = Z_END + (0 if b in B_GA else D) + half * BLK
                        sp.dma_start(w_view(s), cols(w_in, o, BLK)).then_inc(w_full[s], 16)
                    elif b in B_O:
                        half = B_O.index(b)
                        v = w_view(s)
                        sp.dma_start(v[:, 0:4], cols(a["w_o_a"][l], half * BLK, BLK)).then_inc(w_full[s], 16)
                        sp.dma_start(v[:, 4:8], cols(a["w_o_b"][l], half * BLK, BLK)).then_inc(s_ob_w[l], 16)
                    else:
                        sp.dma_start(w_view(s), cols(a["w_out"][l], B_OUT.index(b) * BLK, BLK)).then_inc(w_full[s], 16)

                def load_expert(s, e):
                    w = a[("w_expert_gate", "w_expert_up", "w_expert_down")[s]][l]
                    src = w.rearrange("e (k p) n -> e p k n", p=P)[bass.ds(e, 1)].rearrange("e p k n -> p (e k) n")
                    sp.dma_start(w_view(s) if s < 2 else wd_view, src).then_inc(w_full[s], 16)

                def next_expert(s, e):
                    if s < 2:
                        sp.wait_ge(w_used[s], e + used_base(l))
                    else:
                        sp.wait_ge(*S.at("dl", KF * e))
                    load_expert(s, e)

                S = L[l]
                for s in range(3):
                    wait_block_used(l, BLOCKS + s)
                    load_expert(s, 0)
                next_expert(0, 1)
                next_expert(1, 1)
                with sp.Fori(2, E) as e:
                    next_expert(0, e)
                    next_expert(1, e)
                    next_expert(2, e - 1)
                next_expert(2, E - 1)
            for i in range(NL):
                sp.wait_ge(s_fout, i + 1)
                sp.dma_start(out[0, i * P:(i + 1) * P, :], htok[i]).then_inc(s_out, 16)
            sp.wait_ge(s_out, 16 * NL)

        @block.tensor
        def _(pe):
            def product(dst, lhs, rhs, n, first=True, last=True):
                for k in range(n):
                    ins = pe.matmul(dst, lhs(k), rhs(k), start=first and k == 0, stop=last and k == n - 1)
                return ins

            def split_products(S, ring, c, k, kn, dsts, hi, lo):
                pe.wait_ge(*S.at("wl", c + 1))
                w_hi, w_lo = ring[c % 3]
                for i, dst in dsts:
                    n = dst.shape[1]
                    pe.matmul(dst, hi(k, i), w_hi[:, 0:n], start=k == 0, stop=False)
                    pe.matmul(dst, lo(k, i), w_hi[:, 0:n], start=False, stop=False)
                    ins = pe.matmul(dst, hi(k, i), w_lo[:, 0:n], start=False, stop=k == kn - 1)
                ins.then_inc(S["wu"], 1)

            def of_tile(v):
                return lambda k, i: v[:, k, i * P:(i + 1) * P]

            def transpose_of_h(S, base, j):
                pe.wait_ge(*S.at("h", base + j + 1))
                if base + j >= 2:
                    pe.wait_ge(*S.at("hev", 2 * (base + j - 1)))
                for k in range(KD):
                    ins = pe.transpose(bank[2 * (j % 2) + k // 4][:, (k % 4) * P:(k % 4 + 1) * P],
                                       htok[j % 2][:, k * P:(k + 1) * P], ident)
                    if k % 4 == 3:
                        ins.then_inc(S["tr"], 1)

            pe.wait_ge(s_const, 16)
            pe.wait_ge(s_cs, 1)
            for l in range(DEPTH):
                for b in range(12):
                    s = b % 3
                    pe.wait_ge(w_full[s], (l * 4 + b // 3 + 1) * 16)
                    g = l * 12 + b
                    if g >= 4:
                        pe.wait_ge(s_mevac, g - 3)
                    w = w_view(s)
                    product(bank[4 + g % 4][0:2, :], lambda k: cvec[:, :, k], lambda k: w[:, k, :], KD
                            ).then_inc(w_used[s], 1)
                    j = first_norm_tile(g, 1)
                    if j is not None:
                        transpose_of_h(L[0], 0, j)
            barrier("pe", pe)

            for l in range(DEPTH):
                S = L[l]
                T = tiles(l)
                if l:
                    for j in range(NT):
                        transpose_of_h(S, 0, j)
                for b in B_IN:
                    if b == 0:
                        pe.wait_ge(*S.at("sl", in_split(NT - 1) + 1))
                    if b == 2:
                        pe.wait_ge(*S.at("pev", len(T)))
                    dsts = [(i, bank[4 * ((b + 1) % 2) + n][:, 0:w]) for n, (i, _, w) in enumerate(in_jobs(l, b))]
                    for k in range(KD):
                        split_products(S, in_ring, b * KD + k, k, KD, dsts, of_tile(in_hi), of_tile(in_lo))
                barrier("pe", pe)
                s, full = slot_of(l, B_LORA)

                def turn_compressed(i):
                    pe.wait_ge(*S.at("rcn", i + 1))
                    if i:
                        pe.wait_ge(*S.at("rt2", i))
                    for c in range(3):
                        ins = pe.transpose(bank[0][:, c * P:(c + 1) * P], cn[:, c * P:(c + 1) * P], ident)
                    ins.then_inc(S["rt1"], 1)

                def expand(i):
                    pe.wait_ge(*S.at("rt2", i + 1))
                    if i == 0:
                        pe.wait_ge(w_full[s], 16 * full)
                        pe.wait_ge(s_lora_w[l], 16)
                    else:
                        pe.wait_ge(*S.at("rpev", i))
                    if i in T:
                        product(bank[1][:, :], lambda k: cT[:, k, :], lambda k: uq_w[:, k, 0:512], 2)
                        product(bank[2][:, 0:256], lambda k: cT[:, k, :], lambda k: uq_w[:, k, 512:768], 2)
                    product(bank[3][:, :], lambda k: cT[:, 2, :], lambda k: ukv_w[:, 0:512], 1)
                    ins = product(bank[4][:, :], lambda k: cT[:, 2, :], lambda k: ukv_w[:, 512:1024], 1)
                    ins.then_inc(S["rp"], 1)

                def turn_q(i):
                    pe.wait_ge(*S.at("rq", i + 1))
                    if i:
                        pe.wait_ge(*S.at("rqe", i))
                    for c in range(4):
                        pe.transpose(bank[5][:, c * P:(c + 1) * P], z[:, i, c * P:(c + 1) * P], ident)
                    for h in range(HEADS):
                        ins = pe.transpose(bank[6 + h // 4][0:HB, (h % 4) * P:(h % 4 + 1) * P],
                                           zq[i % 2][:, h * HB:(h + 1) * HB], ident)
                    ins.then_inc(S["rtq"], 1)

                def turn_k(i):
                    if i in T:
                        pe.wait_ge(*S.at("rqq", i + 1))
                    else:
                        pe.wait_ge(*S.at("rq", i + 1))
                        pe.wait_ge(*S.at("rqe", i))
                    for c in range(2):
                        pe.transpose(bank[5][:, c * P:(c + 1) * P], kdup[i % 2][:, c * P:(c + 1) * P], ident)
                    for h in range(HEADS):
                        ins = pe.transpose(bank[6 + h // 4][0:HB, (h % 4) * P:(h % 4 + 1) * P],
                                           kcat[i % 2][:, h * HB:(h + 1) * HB], ident)
                    ins.then_inc(S["rqT"], 1)

                turn_compressed(0)
                expand(0)
                turn_compressed(1)
                for i in range(NT):
                    if i + 1 < NT:
                        expand(i + 1)
                    if i in T:
                        turn_q(i)
                    if i + 2 < NT:
                        turn_compressed(i + 2)
                    turn_k(i)
                barrier("pe", pe)
                units = attention_units(l)

                def scores(u):
                    g, br, i, h, k0, nk = units[u]
                    if u >= 3:
                        pe.wait_ge(*S.at("ex", u - 2))
                    sl = slice(k0 * P, NT * P)
                    if br == 0:
                        lhs, rhs = qaT[h // 4][:, h % 4, i * P:(i + 1) * P], kaT[:, h // 4, sl]
                    else:
                        lhs, rhs = qbT[0:HB, h, i * P:(i + 1) * P], kbT[0:HB, h, sl]
                    pe.matmul(bank[u % 3][:, 0:nk * P], lhs, rhs, start=True, stop=True).then_inc(S["sc"], 1)

                def turn(u):
                    g, br, i, h, k0, nk = units[u]
                    pe.wait_ge(*S.at("ex", u + 1))
                    if u >= 2:
                        pe.wait_ge(*S.at("pte", u - 1))
                    for c in range(nk):
                        ins = pe.transpose(bank[3 + u % 2][:, c * P:(c + 1) * P],
                                           prob[u % 3][:, c * P:(c + 1) * P], ident)
                    ins.then_inc(S["pt"], 1)

                def values(u):
                    g, br, i, h, k0, nk = units[u]
                    pe.wait_ge(*S.at("pte", u + 1))
                    if h == 0 and g >= 2:
                        pe.wait_ge(*S.at("yev", g - 1))
                    for c in range(nk):
                        v = (z[:, k0 + c, Z_VA + (h // 4) * HD:Z_VA + (h // 4 + 1) * HD] if br == 0
                             else vb[:, k0 + c, h * HD:(h + 1) * HD])
                        ins = pe.matmul(bank[5 + g % 2][:, h * HD:(h + 1) * HD], pT[u % 2][:, c, :], v,
                                        start=c == 0, stop=c == nk - 1)
                    ins.then_inc(S["pv"], 1)

                for u in range(len(units) + 3):
                    if u < len(units):
                        scores(u)
                    if 2 <= u < len(units) + 2:
                        turn(u - 2)
                    if u >= 3:
                        values(u - 3)
                barrier("pe", pe)
                def turn_y(n):
                    i = T[n]
                    if n >= 2:
                        pe.wait_ge(*S.at("sl", y_split(l, n - 2, 1) + 1))
                    for br, o in ((0, Z_YA), (1, Z_YB)):
                        for c in range(4):
                            ins = pe.transpose(bank[2 * (n % 2) + br][:, c * P:(c + 1) * P],
                                               z[:, i, o + c * P:o + (c + 1) * P], ident)
                        ins.then_inc(S["yt"], 1)

                for n in range(2):
                    turn_y(n)
                pe.wait_ge(*S.at("sl", h_split(len(T) - 1) + 1))
                for q, (b, k0, kn, at, half, br) in enumerate(out_blocks()):
                    if br is None:
                        if q:
                            pe.wait_ge(*S.at("sg", len(T) * q // 2))
                        hi, lo, banks = of_tile(oh_hi), of_tile(hT_rounded), bank[4:]
                    else:
                        if q == 1:
                            for n in range(2, len(T)):
                                turn_y(n)
                            pe.wait_ge(*S.at("sl", y_split(l, len(T) - 1, 1) + 1))
                        else:
                            pe.wait_ge(*S.at("m", len(T) * (q - 1) // 2))
                        hi, lo, banks = of_tile(y_hi[:, br]), of_tile(y_lo[:, br]), bank
                    dsts = [(i, banks[n][:, :]) for n, i in enumerate(T)]
                    for k in range(kn):
                        split_products(S, out_ring, at + k, k, kn, dsts, hi, lo)
                barrier("pe", pe)
                for n, i in enumerate(T):
                    if n >= 2:
                        pe.wait_ge(*S.at("sl", m_split(l, n - 2, 1) + 1))
                    for k in range(KD):
                        ins = pe.transpose(bank[2 * (n % 2) + k // 4][:, (k % 4) * P:(k % 4 + 1) * P],
                                           mix[:, i, k * P:(k + 1) * P], ident)
                        if k % 4 == 3:
                            ins.then_inc(S["mt"], 1)
                barrier("pe", pe)
                for half in range(2):
                    dsts = [(i, bank[4 * half + n][:, :]) for n, i in enumerate(T)]
                    for k in range(KD):
                        split_products(S, out_ring, OUT_CHUNK + half * KD + k, k, KD, dsts,
                                       of_tile(hT_rounded), of_tile(m_lo))
                pe.wait_ge(*S.at("xup", 2 * len(T)))
                pe.wait_ge(s_wr, 32)
                for j in range(len(T) + 1):
                    if j < len(T):
                        transpose_of_h(S, NT, j)
                    if j:
                        i = T[j - 1]
                        pe.wait_ge(*S.at("hev", 2 * (NT + j)))
                        ins = product(bank[4][:, (j - 1) * E:j * E], lambda k: hT[:, k, i * P:(i + 1) * P],
                                      lambda k: wr[:, k, :], KD)
                ins.then_inc(S["lg"], 1)
                pe.wait_ge(*S.at("rb", 1))
                for n, i in enumerate(T):
                    for j in range(n):
                        pe.matmul(bank[1][:, n * E:(n + 1) * E], ones_b, m_b[:, j, :], start=j == 0, stop=False)
                    ins = pe.matmul(bank[1][:, n * E:(n + 1) * E], tri_b, m_b[:, n, :], start=n == 0, stop=True)
                for n, i in enumerate(T):
                    ins = pe.matmul(bank[1][:, len(T) * E:(len(T) + 1) * E], ones_b, m_b[:, n, :], start=n == 0,
                                    stop=n == len(T) - 1)
                ins.then_inc(S["pos"], 1)
                for n, i in enumerate(T):
                    pe.wait_ge(*S.at("ohr", n + 1))
                    for e in range(E):
                        ins = pe.matmul(bank[2 + n][:, 2 * e:2 * e + 2], ohb[n % 2][:, e, :], tok_b[:, i, :],
                                        start=True, stop=True)
                    ins.then_inc(S["ix"], 1)
                barrier("pe", pe)

                base = moe_base(l)
                wg, wu = w_view(0), w_view(1)

                def turn_rows(e):
                    pe.wait_ge(*S.at("gat", (e + 1) * 16))
                    for k in range(KD):
                        ins = pe.transpose(bank[k // 4][:, (k % 4) * P:(k % 4 + 1) * P],
                                           xg[:, k * P:(k + 1) * P], ident)
                    ins.then_inc(S["xt"], 1)

                def gate_up(e):
                    pe.wait_ge(*S.at("xte", (e + 1) * 2))
                    pe.wait_ge(w_full[0], (e + base + 1) * 16)
                    product(bank[2][:, :], lambda k: xgT[:, k, :], lambda k: wg[:, k, :], KD).then_inc(w_used[0], 1)
                    pe.wait_ge(w_full[1], (e + base + 1) * 16)
                    product(bank[3][:, :], lambda k: xgT[:, k, :], lambda k: wu[:, k, :], KD).then_inc(w_used[1], 1)

                def down(e):
                    pe.wait_ge(*S.at("ate", e + 1))
                    if not isinstance(e, int) or e:
                        pe.wait_ge(*S.at("ye", e * 2))
                    for k in range(KF):
                        pe.wait_ge(*S.at("dl", e * KF + k + 1))
                        for c in range(2):
                            w_hi, w_lo = wd_hi[:, k, c * BLK:(c + 1) * BLK], wd_lo[:, k, c * BLK:(c + 1) * BLK]
                            pe.matmul(bank[5 + c][:, :], auT_hi[:, k, :], w_hi, start=k == 0, stop=False)
                            pe.matmul(bank[5 + c][:, :], auT_lo[:, k, :], w_hi, start=False, stop=False)
                            ins = pe.matmul(bank[5 + c][:, :], auT_hi[:, k, :], w_lo, start=False, stop=k == KF - 1)
                    ins.then_inc(w_used[2], 1)

                def turn_act(e):
                    pe.wait_ge(*S.at("au", e + 1))
                    for k in range(KF):
                        ins = pe.transpose(bank[4][:, k * P:(k + 1) * P], au[:, k * P:(k + 1) * P], ident)
                    ins.then_inc(S["at"], 1)

                turn_rows(0)
                gate_up(0)
                turn_rows(1)
                turn_act(0)

                def turn(e):
                    gate_up(e)
                    down(e - 1)
                    turn_rows(e + 1)
                    turn_act(e)

                turn(1)
                with pe.Fori(2, E - 1) as e:
                    turn(e)
                gate_up(E - 1)
                down(E - 2)
                turn_act(E - 1)
                down(E - 1)
                barrier("pe", pe)
                barrier("pe", pe)
                more_rounds("pe", pe, l)
            barrier("pe", pe)

        @block.scalar
        def _(act):
            act.wait_ge(s_c, 32)
            act.activation(cth[:, :, :], cvec[:, :, :], ACT.Tanh, scale=0.5).then_inc(s_cs2, 1)

            def part_hi(S, dst, src, waits=()):
                for w in waits:
                    act.wait_ge(*w)
                act.copy(dst, src).then_inc(S["sh"], 1)

            def w_hi(S, l, ring, c, b, k, n=BLK):
                if k % 4 == 0:
                    s, full = slot_of(l, b)
                    act.wait_ge(w_full[s], 16 * full)
                    if b in B_O and k == 4:
                        act.wait_ge(s_ob_w[l], 16 * (B_O.index(b) + 1))
                if c >= 3:
                    act.wait_ge(*S.at("wu", c - 2))
                act.copy(ring[c % 3][0][:, 0:n], w_view(b % 3, n)[:, k, :]).then_inc(S["wh"], 1)

            def squares(S, base, j, i):
                if base + j:
                    act.wait_ge(*S.at("ss", base + j))
                act.activation(junk, x[:, i, :], ACT.Square, accum_out=small[:, j:j + 1]).then_inc(S["ss"], 1)

            def read_out_h(S, base, j, i):
                for c in range(2):
                    act.wait_ge(*S.at("tr", 2 * (base + j) + c + 1))
                    act.copy(hT[:, 4 * c:4 * c + 4, i * P:(i + 1) * P],
                             bank[2 * (j % 2) + c][:, :].rearrange("p (k t) -> p k t", k=4)).then_inc(S["hev"], 1)

            for l in range(DEPTH):
                S = L[l]
                T = tiles(l)
                if l == 0:
                    act.wait_ge(s_x, 16)
                    act.wait_ge(s_x2, 16)
                    for i in range(NT):
                        squares(S, 0, i, i)
                for i in range(NT):
                    read_out_h(S, 0, i, i)
                    part_hi(S, in_hi[:, :, i * P:(i + 1) * P], hT[:, :, i * P:(i + 1) * P],
                            [S.at("hev", 2 * (i + 1))])
                if l == 0:
                    barrier("act", act)

                def read_in(b):
                    act.wait_ge(*S.at("wu", KD * (b + 1)))
                    for n, (i, o, w) in enumerate(in_jobs(l, b)):
                        act.copy(z[:, i, o:o + w], bank[4 * ((b + 1) % 2) + n][:, 0:w]).then_inc(S["pev"], 1)

                for b in B_IN:
                    for k in range(KD):
                        w_hi(S, l, in_ring, b * KD + k, b, k, IN_COLS[b][1])
                        if b and k == 2:
                            read_in(b - 1)
                act.wait_ge(*S.at("pev", len(T) + NT))
                for i in T:
                    act.activation(lora_junk[:, i, 0:QR], z[:, i, Z_CQ:Z_CKV], ACT.Square,
                                   accum_out=lora_sum[:, i:i + 1])
                read_in(2)
                barrier("act", act)
                for i in range(NT):
                    ins = act.activation(lora_junk[:, i, QR:QR + KVR], z[:, i, Z_CKV:Z_KR], ACT.Square,
                                         accum_out=lora_sum[:, NT + i:NT + i + 1])
                ins.then_inc(S["rz"], 1)

                def read_compressed(i):
                    act.wait_ge(*S.at("rt1", i + 1))
                    if i:
                        act.wait_ge(*S.at("rp", i))
                    act.copy(cT[:, :, :], bank[0][:, 0:384].rearrange("p (c t) -> p c t", c=3)
                             ).then_inc(S["rt2"], 1)

                def read_expanded(i):
                    act.wait_ge(*S.at("rp", i + 1))
                    if i >= 2:
                        act.wait_ge(*S.at("rqT", i - 1))
                    if i in T:
                        act.copy(zq[i % 2][:, 0:512], bank[1][:, :])
                        act.copy(zq[i % 2][:, 512:768], bank[2][:, 0:256])
                    for c in range(2):
                        kv = bank[3 + c][:, :].rearrange("p (h c d) -> p h c d", h=4, c=2)
                        act.copy(kcat[i % 2].rearrange("p (h d) -> p h d", d=HB)[:, 4 * c:4 * c + 4, 0:HD],
                                 kv[:, :, 0, :])
                        ins = act.copy(vb[:, i, c * 256:(c + 1) * 256].rearrange("p (h d) -> p h d", h=4),
                                       kv[:, :, 1, :])
                    ins.then_inc(S["rpev"], 1)

                def read_q(i):
                    act.wait_ge(*S.at("rtq", i + 1))
                    t = slice(i * P, (i + 1) * P)
                    if i == 0:
                        act.wait_ge(*S.at("rcr", 2))
                    for odd in range(2):
                        rows = slice(odd * HD, (odd + 1) * HD)
                        for g in range(2):
                            act.copy(qaT[g][rows, :, :].rearrange("p (c o) t -> p c o t", o=2)[:, :, odd, t],
                                     bank[5][rows, 2 * g * P:2 * (g + 1) * P].rearrange("p (c t) -> p c t", c=2))
                    for c in range(2):
                        ins = act.copy(qbT[0:HB, 4 * c:4 * c + 4, t],
                                       bank[6 + c][0:HB, :].rearrange("p (c t) -> p c t", c=4))
                    ins.then_inc(S["rqq"], 1)

                read_compressed(0)
                read_expanded(0)
                read_compressed(1)
                for i in range(NT):
                    if i + 1 < NT:
                        read_expanded(i + 1)
                    if i in T:
                        read_q(i)
                    if i + 2 < NT:
                        read_compressed(i + 2)
                barrier("act", act)
                units = attention_units(l)
                for u, (g, br, i, h, k0, nk) in enumerate(units):
                    act.wait_ge(*S.at("nm", u + 1))
                    if u >= 3:
                        act.wait_ge(*S.at("pt", u - 2))
                    act.activation(prob[u % 3][:, 0:nk * P], bank[u % 3][:, 0:nk * P], ACT.Exp,
                                   bias=small[:, nm_at(g) + h:nm_at(g) + h + 1], scale=att_scale(br),
                                   accum_out=small[:, 48 + (g % 2) * 8 + h:49 + (g % 2) * 8 + h]
                                   ).then_inc(S["ex"], 1)
                    if u >= 1:
                        read_pT(act, S, units, u - 1)
                    if h == HEADS - 1 and br == 0:
                        act.wait_ge(*S.at("nms", g + 1))
                        act.activation(small[:, 64:64 + HEADS], small[:, 64:64 + HEADS], ACT.Exp
                                       ).then_inc(S["es"], 1)
                read_pT(act, S, units, len(units) - 1)
                barrier("act", act)
                for n, i in enumerate(T):
                    part_hi(S, oh_hi[:, :, i * P:(i + 1) * P], hT[:, :, i * P:(i + 1) * P])

                def y_part(n):
                    i = T[n]
                    for br in range(2):
                        part_hi(S, y_hi[:, br, :, i * P:(i + 1) * P],
                                bank[2 * (n % 2) + br][:, :].rearrange("p (c t) -> p c t", c=4),
                                [S.at("yt", 2 * n + br + 1)])

                def gates(q, last):
                    act.wait_ge(*S.at("wu", last + 1))
                    for n in range(len(T)):
                        if q:
                            act.wait_ge(*S.at("m", len(T) * (q // 2 - 1) + n + 1))
                        act.activation(sg[n], bank[4 + n][:, :], ACT.Tanh, scale=0.5).then_inc(S["sg"], 1)

                for n in range(2):
                    y_part(n)
                before = None
                for q, (b, k0, kn, at, half, br) in enumerate(out_blocks()):
                    for k in range(kn):
                        w_hi(S, l, out_ring, at + k, b, k0 + k)
                        if k == 2 and before is not None:
                            gates(*before)
                    before = (q, at + kn - 1) if br is None else None
                    if q == 0:
                        for n in range(2, len(T)):
                            y_part(n)
                barrier("act", act)
                for k in range(2):
                    w_hi(S, l, out_ring, OUT_CHUNK + k, B_OUT[0], k)
                for n, i in enumerate(T):
                    for c in range(2):
                        part_hi(S, hT_rounded[:, 4 * c:4 * c + 4, i * P:(i + 1) * P],
                                bank[2 * (n % 2) + c][:, :].rearrange("p (k t) -> p k t", k=4),
                                [S.at("mt", 2 * n + c + 1)])
                barrier("act", act)
                for half in range(2):
                    for k in range(KD):
                        if half or k >= 2:
                            w_hi(S, l, out_ring, OUT_CHUNK + half * KD + k, B_OUT[half], k)
                for j, i in enumerate(T):
                    act.wait_ge(*S.at("xup", len(T) + j + 1))
                    squares(S, NT, j, i)
                for j, i in enumerate(T):
                    read_out_h(S, NT, j, i)
                act.wait_ge(*S.at("lg", 1))
                act.activation(r_sc[:, 0:len(T) * E], bank[4][:, 0:len(T) * E], ACT.Tanh, scale=0.5
                               ).then_inc(S["lge"], 1)
                barrier("act", act)
                base = moe_base(l)

                def read_rows(e):
                    act.wait_ge(*S.at("xt", e + 1))
                    act.copy(xgT[:, 0:4, :], bank[0][:, :].rearrange("p (k t) -> p k t", k=4)).then_inc(S["xte"], 1)

                def tanh_gate(e):
                    act.wait_ge(w_used[0], e + used_base(l) + 1)
                    act.activation(tg, bank[2][:, :], ACT.Tanh, scale=0.5).then_inc(S["th"], 1)

                def read_act(e):
                    act.wait_ge(*S.at("at", e + 1))
                    act.copy(auT_hi[:, :, :], bank[4][:, :].rearrange("p (k t) -> p k t", k=4)).then_inc(S["ath"], 1)

                def split_down(e):
                    act.wait_ge(w_full[2], (e + base + 1) * 16)
                    act.wait_ge(w_used[2], e + used_base(l))
                    for k in range(KF):
                        act.copy(wd_hi[:, k, :], wd_view[:, k, :]).then_inc(S["dh"], 1)

                def read_y(e, dst=ysb):
                    act.wait_ge(w_used[2], e + used_base(l) + 1)
                    if dst is ysb and (not isinstance(e, int) or e):
                        act.wait_ge(*S.at("yst", e * 16))
                    act.copy(dst[:, 0:BLK], bank[5][:, :]).then_inc(S["ye"], 1)

                read_rows(0)
                tanh_gate(0)
                read_rows(1)
                read_act(0)

                def turn(e):
                    tanh_gate(e)
                    split_down(e - 1)
                    read_y(e - 1)
                    read_rows(e + 1)
                    read_act(e)

                turn(1)
                with act.Fori(2, E - 1) as e:
                    turn(e)
                tanh_gate(E - 1)
                split_down(E - 2)
                read_y(E - 2)
                split_down(E - 1)
                read_act(E - 1)
                read_y(E - 1, ysb_last)
                act.wait_ge(*S.at("ye", 2 * E))
                act.dma_start(y_dram[(E - 1) * CAP:E * CAP, :], ysb_last).then_inc(S["ylast"], 16)
                barrier("act", act)
                for n in range(len(T) + 1):
                    if n < len(T):
                        act.wait_ge(*S.at(f"g0{n}", 16))
                        act.mul(y1[n], y1[n], r_wm[:, 0, n:n + 1]).then_inc(S["ym"], 1)
                    if n:
                        act.wait_ge(*S.at("f", n))
                        if l < DEPTH - 1:
                            squares(L[l + 1], 0, n - 1, T[n - 1])
                        else:
                            if n > 1:
                                act.wait_ge(s_fin, n - 1)
                            act.activation(junk, x[:, T[n - 1], :], ACT.Square, accum_out=small[:, n - 1:n]
                                           ).then_inc(s_fin, 1)
                barrier("act", act)
                more_rounds("act", act, l)
            barrier("act", act)

        @block.vector
        def _(dve):
            def lk(ins):
                link(dve, ins)

            dve.wait_ge(s_cs2, 1)
            lk(dve.scalar_tensor_tensor(out=cth[:, :, :], in0=cth[:, :, :], scalar=1.0, in1=cvec[:, :, :],
                                        op0=ALU.add, op1=ALU.mult))
            dve.tensor_scalar(cvec[:, :, :], cth[:, :, :], 0.5, None, ALU.mult).then_inc(s_cs, 1)
            dve.wait_ge(s_const, 16)
            dve.tensor_copy(tri_b, cst("tri"))
            dve.memset(ones_b, 1.0)
            for i in range(NT):
                dve.tensor_copy(tok_b[:, i, :], cst(f"tok{i}"))
            def part_lo(S, n, dst, src, hi):
                dve.wait_ge(*S.at("sh", n + 1))
                dve.tensor_tensor(dst, src, exact(hi), ALU.subtract).then_inc(S["sl"], 1)

            def w_lo(S, ring, c, b, k, n=BLK):
                dve.wait_ge(*S.at("wh", c + 1))
                hi, lo = ring[c % 3]
                dve.tensor_tensor(lo[:, 0:n], w_view(b % 3, n)[:, k, :], exact(hi[:, 0:n]), ALU.subtract
                                  ).then_inc(S["wl"], 1)

            def in_part(S, i):
                t = slice(i * P, (i + 1) * P)
                part_lo(S, in_split(i), in_lo[:, :, t], hT[:, :, t], in_hi[:, :, t])

            def norm_variance(S, n, base):
                dve.wait_ge(*S.at("ss", base + n))
                dve.tensor_scalar(small[:, 8:8 + n], small[:, 0:n], 1.0 / D, EPS, ALU.mult, ALU.add
                                  ).then_inc(S["var"], 1)

            def norm_ready(S, base):
                dve.wait_ge(*S.at("rstd", 1 if base == 0 else 2))
                dve.wait_ge(*S.at("modn", 16 if base == 0 else 32))

            def norm_tile(S, base, j, i):
                if j >= 2:
                    dve.wait_ge(*S.at("tr", 2 * (base + j - 1)))
                    if base:
                        dve.wait_ge(*S.at(f"hst{j % 2}", 16 * (j // 2)))
                lk(dve.scalar_tensor_tensor(out=htok[j % 2], in0=x[:, i, :], scalar=small[:, 12 + j:13 + j],
                                            in1=modbc[:, kind(i), D:2 * D], op0=ALU.mult, op1=ALU.mult))
                dve.tensor_tensor(htok[j % 2], htok[j % 2], modbc[:, kind(i), 0:D], ALU.add
                                  ).then_inc(S["h"], 1)

            for l in range(DEPTH):
                for b in range(12):
                    c = b % 6
                    if c == 0:
                        dve.wait_ge(s_brow, l * 64 + 32 * (b // 6 + 1))
                        if l or b:
                            dve.wait_ge(s_mrow, l * 32 + 16 * (b // 6))
                    bk = bank[4 + (l * 12 + b) % 4]
                    dve.wait_ge(w_used[b % 3], l * 4 + b // 3 + 1)
                    cs = slice(c * BLK, (c + 1) * BLK)
                    if c // 2 != 1:
                        dve.tensor_tensor(mrow[:, cs], bk[0:2, :], brow[:, cs], ALU.add).then_inc(s_mevac, 1)
                    else:
                        dve.wait_ge(s_mevac, l * 12 + b)
                        dve.tensor_tensor(trow, bk[0:2, :], brow[:, cs], ALU.add).then_inc(s_mt, 1)
                        dve.wait_ge(s_mt, l * 4 + (b // 6) * 2 + c - 1)
                        dve.scalar_tensor_tensor(out=mrow[:, cs], in0=trow, scalar=1.0,
                                                 in1=grow[:, (c - 2) * BLK:(c - 1) * BLK],
                                                 op0=ALU.add, op1=ALU.mult).then_inc(s_mevac, 1)
                    if l == 0 and b == 3:
                        norm_variance(L[0], NT, 0)
                    j = first_norm_tile(l * 12 + b, 0)
                    if j is not None:
                        if j == 0:
                            norm_ready(L[0], 0)
                        norm_tile(L[0], 0, j, j)
                    j = first_norm_tile(l * 12 + b, 3)
                    if j is not None:
                        in_part(L[0], j)
            barrier("dve", dve)

            def rope(v, dim, heads, name, i):
                n = heads * dim
                d4 = dim // 4
                cos = cst(f"cos_{name}{i}").unsqueeze(1).to_broadcast([P, heads, dim])
                sin = cst(f"sin_{name}{i}").unsqueeze(1).to_broadcast([P, heads, dim])
                vc = rope_c[:, 0:n].rearrange("p (h d) -> p h d", d=dim)
                vs = rope_s[:, 0:n].rearrange("p (h d) -> p h d", d=dim)
                dve.tensor_tensor(vc, v, cos, ALU.mult)
                lk(dve.tensor_tensor(vs, v, sin, ALU.mult))
                for rc in range(2):
                    lo = slice(rc * dim // 2, rc * dim // 2 + d4)
                    hi = slice(rc * dim // 2 + d4, (rc + 1) * dim // 2)
                    dve.tensor_tensor(v[:, :, lo], vc[:, :, lo], vs[:, :, hi], ALU.subtract)
                    ins = dve.tensor_tensor(v[:, :, hi], vc[:, :, hi], vs[:, :, lo], ALU.add)
                return ins

            for l in range(DEPTH):
                S = L[l]
                T = tiles(l)
                if l:
                    norm_variance(S, NT, 0)
                    norm_ready(S, 0)
                    for i in range(NT):
                        norm_tile(S, 0, i, i)
                        if i >= 2:
                            in_part(S, i - 2)
                    in_part(S, NT - 2)
                    in_part(S, NT - 1)
                for b in B_IN:
                    for k in range(KD):
                        w_lo(S, in_ring, b * KD + k, b, k, IN_COLS[b][1])
                barrier("dve", dve)
                dve.wait_ge(*S.at("rz", 1))
                dve.wait_ge(*S.at("lorain", 64))
                dve.tensor_scalar(lora_var[:, 0:len(T)], lora_sum[:, 0:len(T)], 1.0 / QR, EPS, ALU.mult, ALU.add)
                if len(T) < NT:
                    dve.memset(lora_var[:, len(T):NT], 1.0)
                dve.tensor_scalar(lora_var[:, NT:], lora_sum[:, NT:], 1.0 / KVR, EPS, ALU.mult, ALU.add
                                  ).then_inc(S["rcv"], 1)
                dve.wait_ge(*S.at("rcr", 1))

                def norm_compressed(i):
                    if i:
                        dve.wait_ge(*S.at("rt1", i))
                    if i in T:
                        dve.scalar_tensor_tensor(out=cn[:, 0:QR], in0=z[:, i, Z_CQ:Z_CKV],
                                                 scalar=lora_rstd[:, i:i + 1],
                                                 in1=lora[:, 0:QR], op0=ALU.mult, op1=ALU.mult)
                    elif i == len(T):
                        dve.memset(cn[:, 0:QR], 0.0)
                    dve.scalar_tensor_tensor(out=cn[:, QR:], in0=z[:, i, Z_CKV:Z_KR],
                                             scalar=lora_rstd[:, NT + i:NT + i + 1],
                                             in1=lora[:, QR:], op0=ALU.mult, op1=ALU.mult).then_inc(S["rcn"], 1)

                def read_k(i):
                    dve.wait_ge(*S.at("rqT", i + 1))
                    t = slice(i * P, (i + 1) * P)
                    dve.tensor_copy(kaT[:, :, t], bank[5][:, 0:2 * P].rearrange("p (c t) -> p c t", c=2))
                    for c in range(2):
                        ins = dve.tensor_copy(kbT[0:HB, 4 * c:4 * c + 4, t],
                                              bank[6 + c][0:HB, :].rearrange("p (c t) -> p c t", c=4))
                    ins.then_inc(S["rqe"], 1)

                norm_compressed(0)
                for i in range(NT):
                    if i < NL:
                        if i:
                            dve.wait_ge(*S.at("rq", i))
                        lk(rope(z[:, i, 0:10 * HD].rearrange("p (h d) -> p h d", d=HD), HD, 10, "a", i))
                        lk(rope(z[:, i, Z_KR:Z_END].rearrange("p (h d) -> p h d", d=RD), RD, 1, "b", i))
                    kd = kdup[i % 2].rearrange("p (g c d) -> p g c d", g=KV_A, c=2)
                    ka = z[:, i, Z_KA:Z_VA].rearrange("p (g d) -> p g d", g=KV_A)
                    if i >= 2:
                        dve.wait_ge(*S.at("rqT", i - 1))
                    for c in range(2):
                        dve.tensor_copy(kd[:, :, c, :], ka)
                    if i + 1 < NT:
                        norm_compressed(i + 1)
                    if i:
                        read_k(i - 1)
                    dve.wait_ge(*S.at("rpev", i + 1))
                    ins = dve.tensor_copy(kcat[i % 2].rearrange("p (h d) -> p h d", d=HB)[:, :, HD:HB],
                                          z[:, i, Z_KR:Z_END].unsqueeze(1).to_broadcast([P, HEADS, RD]))
                    if i < NL:
                        lk(ins)
                        ins = rope(zq[i % 2].rearrange("p (h d) -> p h d", d=HB)[:, :, HD:HB], RD, HEADS, "b", i)
                    ins.then_inc(S["rq"], 1)
                read_k(NT - 1)
                barrier("dve", dve)
                units = attention_units(l)

                def finish(g):
                    u_last = 8 * g + 7
                    _, br, i, _, _, _ = units[u_last]
                    dve.wait_ge(*S.at("ex", u_last + 1))
                    ls = small[:, 48 + (g % 2) * 8:56 + (g % 2) * 8]
                    if br == 0:
                        dve.wait_ge(*S.at("es", g + 1))
                        lk(dve.tensor_tensor(small[:, 72:80], ls, small[:, 64:72], ALU.add))
                        lk(dve.reciprocal(small[:, 80:88], small[:, 72:80]))
                    else:
                        lk(dve.reciprocal(small[:, 80:88], ls))
                    dve.wait_ge(*S.at("pv", u_last + 1))
                    o = Z_YA if br == 0 else Z_YB
                    dve.tensor_tensor(z[:, i, o:o + 512].rearrange("p (h d) -> p h d", d=HD),
                                      bank[5 + g % 2][:, :].rearrange("p (h d) -> p h d", d=HD),
                                      small[:, 80:88].unsqueeze(2).to_broadcast([P, HEADS, HD]), ALU.mult
                                      ).then_inc(S["yev"], 1)

                for u, (g, br, i, h, k0, nk) in enumerate(units):
                    dve.wait_ge(*S.at("sc", u + 1))
                    b = bank[u % 3]
                    if br == 0 and i < NL:
                        cut = b[:, (1 - i) * P:(2 - i) * P]
                        lk(dve.tensor_tensor(cut, cut, cst(f"mask{i}"), ALU.add))
                    lk(dve.tensor_reduce(small[:, 88 + u % 2:89 + u % 2], b[:, 0:nk * P], AX.X, ALU.max))
                    nm = small[:, nm_at(g) + h:nm_at(g) + h + 1]
                    if br == 0:
                        ins = dve.tensor_scalar(nm, small[:, 88 + u % 2:89 + u % 2], -att_scale(br), sinks[:, 8 + h:9 + h],
                                                ALU.mult, ALU.min)
                    else:
                        ins = dve.tensor_scalar(nm, small[:, 88 + u % 2:89 + u % 2], -att_scale(br), None, ALU.mult)
                    ins.then_inc(S["nm"], 1)
                    if h == HEADS - 1 and br == 0:
                        dve.wait_ge(*S.at("nm", u + 1))
                        dve.tensor_tensor(small[:, 64:72], sinks[:, 0:8], small[:, nm_at(g):nm_at(g) + 8], ALU.add
                                          ).then_inc(S["nms"], 1)
                    if h == 3 and g >= 1:
                        finish(g - 1)
                finish(units[-1][0])
                barrier("dve", dve)
                for n, i in enumerate(T):
                    t = slice(i * P, (i + 1) * P)
                    part_lo(S, h_split(n), hT_rounded[:, :, t], hT[:, :, t], oh_hi[:, :, t])

                def y_part(n):
                    t = slice(T[n] * P, (T[n] + 1) * P)
                    for br in range(2):
                        part_lo(S, y_split(l, n, br), y_lo[:, br, :, t],
                                bank[2 * (n % 2) + br][:, :].rearrange("p (c t) -> p c t", c=4), y_hi[:, br, :, t])

                def branch(q, half, br, last):
                    dve.wait_ge(*S.at("wu", last + 1))
                    cs = slice(half * BLK, (half + 1) * BLK)
                    for n, i in enumerate(T):
                        done = len(T) * (q // 2) + n
                        dve.wait_ge(*S.at("sg", done + 1))
                        if br == 0:
                            dve.scalar_tensor_tensor(out=mix[:, i, cs], in0=sg[n], scalar=1.0, in1=bank[n][:, :],
                                                     op0=ALU.add, op1=ALU.mult).then_inc(S["m"], 1)
                        else:
                            dve.wait_ge(*S.at("m", done))
                            lk(dve.scalar_tensor_tensor(out=pg[0], in0=sg[n], scalar=1.0, in1=bank[n][:, :],
                                                        op0=ALU.add, op1=ALU.mult))
                            dve.tensor_tensor(mix[:, i, cs], mix[:, i, cs], pg[0], ALU.add).then_inc(S["m"], 1)

                for n in range(2):
                    y_part(n)
                before = None
                for q, (b, k0, kn, at, half, br) in enumerate(out_blocks()):
                    for k in range(kn):
                        w_lo(S, out_ring, at + k, b, k0 + k)
                        if k == 2 and before is not None:
                            branch(*before)
                    before = (q, half, br, at + kn - 1) if br is not None else None
                    if q == 0:
                        for n in range(2, len(T)):
                            y_part(n)
                branch(*before)
                barrier("dve", dve)
                for k in range(2):
                    w_lo(S, out_ring, OUT_CHUNK + k, B_OUT[0], k)
                for n, i in enumerate(T):
                    t = slice(i * P, (i + 1) * P)
                    for c in range(2):
                        part_lo(S, m_split(l, n, c), m_lo[:, 4 * c:4 * c + 4, t],
                                bank[2 * (n % 2) + c][:, :].rearrange("p (k t) -> p k t", k=4),
                                hT_rounded[:, 4 * c:4 * c + 4, t])
                barrier("dve", dve)
                dve.wait_ge(*S.at("modg", 16))

                def update(half):
                    dve.wait_ge(*S.at("wu", OUT_CHUNK + KD * (half + 1)))
                    cs = slice(half * BLK, (half + 1) * BLK)
                    for n, i in enumerate(T):
                        lk(dve.scalar_tensor_tensor(out=pg[n % 2], in0=bank[4 * half + n][:, :], scalar=0.5,
                                                    in1=modbc[:, kind(i), 2 * D + half * BLK:2 * D + (half + 1) * BLK],
                                                    op0=ALU.mult, op1=ALU.mult))
                        dve.tensor_tensor(x[:, i, cs], x[:, i, cs], pg[n % 2], ALU.add).then_inc(S["xup"], 1)

                for half in range(2):
                    for k in range(KD):
                        if half or k >= 2:
                            w_lo(S, out_ring, OUT_CHUNK + half * KD + k, B_OUT[half], k)
                        if half and k == 2:
                            update(0)
                update(1)
                norm_variance(S, len(T), NT)
                norm_ready(S, NT)
                for j, i in enumerate(T):
                    norm_tile(S, NT, j, i)
                route(dve, lk, S, T)
                barrier("dve", dve)
                base = moe_base(l)

                def read_rows_d(e):
                    dve.wait_ge(*S.at("xt", e + 1))
                    dve.tensor_copy(xgT[:, 4:8, :], bank[1][:, :].rearrange("p (k t) -> p k t", k=4)
                                    ).then_inc(S["xte"], 1)

                def split_down(e):
                    for k in range(KF):
                        dve.wait_ge(*S.at("dh", e * KF + k + 1))
                        dve.tensor_tensor(wd_lo[:, k, :], wd_view[:, k, :], exact(wd_hi[:, k, :]), ALU.subtract
                                          ).then_inc(S["dl"], 1)

                def read_act_d(e):
                    dve.wait_ge(*S.at("ath", e + 1))
                    dve.tensor_tensor(auT_lo[:, :, :], bank[4][:, :].rearrange("p (k t) -> p k t", k=4),
                                      exact(auT_hi[:, :, :]), ALU.subtract).then_inc(S["ate"], 1)

                def activate(e):
                    dve.wait_ge(*S.at("th", e + 1))
                    dve.scalar_tensor_tensor(out=au, in0=tg, scalar=1.0, in1=bank[2][:, :],
                                             op0=ALU.add, op1=ALU.mult).then_inc(S["aug"], 1)
                    if not isinstance(e, int) or e:
                        split_down(e - 1)
                    dve.wait_ge(*S.at("aug", e + 1))
                    dve.wait_ge(w_used[1], e + used_base(l) + 1)
                    dve.tensor_tensor(au, au, bank[3][:, :], ALU.mult).then_inc(S["au"], 1)

                def read_y_d(e, dst=ysb):
                    dve.wait_ge(w_used[2], e + used_base(l) + 1)
                    if dst is ysb and (not isinstance(e, int) or e):
                        dve.wait_ge(*S.at("yst", e * 16))
                    dve.tensor_copy(dst[:, BLK:D], bank[6][:, :]).then_inc(S["ye"], 1)

                read_rows_d(0)
                route_rest(dve, lk, T)
                activate(0)
                read_rows_d(1)
                read_act_d(0)

                def turn(e):
                    activate(e)
                    read_y_d(e - 1)
                    read_rows_d(e + 1)
                    read_act_d(e)

                turn(1)
                with dve.Fori(2, E - 1) as e:
                    turn(e)
                activate(E - 1)
                read_y_d(E - 2)
                split_down(E - 1)
                read_act_d(E - 1)
                read_y_d(E - 1, ysb_last)
                barrier("dve", dve)
                dve.wait_ge(*S.at("modg", 32))
                for n, i in enumerate(T):
                    dve.wait_ge(*S.at(f"g1{n}", 16))
                    dve.wait_ge(*S.at("ym", n + 1))
                    combine(dve, lk, l, n, i).then_inc(S["f"], 1)
                dve.wait_ge(*S.at("f", len(T)))
                barrier("dve", dve)
                more_rounds("dve", dve, l)
            dve.wait_ge(s_fin, NL)
            dve.tensor_scalar(small[:, 8:8 + NL], small[:, 0:NL], 1.0 / D, EPS, ALU.mult, ALU.add).then_inc(s_fvar, 1)
            dve.wait_ge(s_frs, 1)
            dve.wait_ge(s_fn, 16)
            for i in range(NL):
                dve.scalar_tensor_tensor(out=htok[i], in0=x[:, i, :], scalar=small[:, 12 + i:13 + i],
                                         in1=modbc[:, 0, 0:D], op0=ALU.mult, op1=ALU.mult).then_inc(s_fout, 1)
            barrier("dve", dve)

        @block.gpsimd
        def _(pool):
            def load_mod(sem_name, l, sub, o, n):
                pool.dma_start(modbc[:, :, o:o + n],
                               mod_dram[l, sub].rearrange("(a t) n -> a t n", a=1)[:, :, o:o + n]
                               .to_broadcast([P, 2, n])).then_inc(L[l][sem_name], 16)

            def load_shifts(l, sub):
                load_mod("modn", l, sub, 0, 2 * D)

            def load_gates(l, sub):
                load_mod("modg", l, sub, 2 * D, D)

            def load_for_layer(l):
                load_shifts(l, 0)
                for dst, w in ((lora[:, 0:QR], "mla_q_norm"), (lora[:, QR:], "mla_kv_norm"),
                               (sinks[:, 0:HEADS], "attn_sink"), (sinks[:, HEADS:], "attn_sink")):
                    pool.dma_start(dst, a[w][l:l + 1, :].to_broadcast([P, dst.shape[1]])
                                   ).then_inc(L[l]["lorain"], 16)

            def inverse_root(S, n, v):
                pool.wait_ge(*S.at("var", v))
                pool.tensor_tensor(small[:, 12:12 + n], small[:, 8:8 + n], cst("minus_half")[:, 0:n], ALU.pow
                                   ).then_inc(S["rstd"], 1)

            pool.dma_start(const[:, :], const_in).then_inc(s_const, 16)
            pool.dma_start(wr[:, :, :], a["w_router"].rearrange("(k p) e -> p k e", p=P)).then_inc(s_wr, 16)
            pool.dma_start(rbias[:, :], a["router_bias"].rearrange("(a e) -> a e", a=1).to_broadcast([P, E])
                           ).then_inc(s_wr, 16)
            pool.dma_start(x[:, 0:NL, :], a["x"].rearrange("b (i p) d -> p (b i) d", p=P)).then_inc(s_x, 16)
            pool.dma_start(x[:, NL:NT, :], a["ctx"].rearrange("b (i p) d -> p (b i) d", p=P)).then_inc(s_x2, 16)
            for l in range(DEPTH):
                for sub, g in enumerate((a["norm_mix"], a["norm_ffn"])):
                    if l or sub:
                        pool.wait_ge(s_mevac, l * 12 + sub * 6)
                    pool.dma_start(brow, a["b_mod"][l:l + 1, sub * MOD:(sub + 1) * MOD].to_broadcast([2, MOD])
                                   ).then_inc(s_brow, 16)
                    pool.dma_start(grow, g[l:l + 1, :].to_broadcast([2, D])).then_inc(s_brow, 16)
                    pool.wait_ge(s_mevac, l * 12 + sub * 6 + 6)
                    pool.dma_start(mod_dram[l, sub], mrow
                                   ).then_inc(s_mrow, 16)
                    if l == 0 and sub == 0:
                        pool.wait_ge(s_mrow, 16)
                        load_for_layer(0)
                        load_gates(0, 0)
                        inverse_root(L[0], NT, 1)
            pool.wait_ge(s_mrow, 16 * 2 * DEPTH)
            barrier("pool", pool)

            for l in range(DEPTH):
                S = L[l]
                T = tiles(l)
                if l:
                    inverse_root(S, NT, 1)
                    load_gates(l, 0)
                pool.wait_ge(*S.at("lorain", 64))
                pool.tensor_scalar(sinks[:, HEADS:], sinks[:, HEADS:], -1.0, None, ALU.mult)
                barrier("pool", pool)
                pool.wait_ge(*S.at("rcv", 1))
                pool.tensor_tensor(lora_rstd, lora_var, cst("minus_half")[:, 0:2 * NT], ALU.pow).then_inc(S["rcr"], 1)
                for v in qaT:
                    ins = pool.memset(v, 0.0)
                ins.then_inc(S["rcr"], 1)
                barrier("pool", pool)
                barrier("pool", pool)
                load_shifts(l, 1)
                for _ in range(2):
                    barrier("pool", pool)
                inverse_root(S, len(T), 2)
                for n, i in enumerate(T):
                    pool.wait_ge(*S.at("h", NT + n + 1))
                    pool.dma_start(h_dram[i * P:(i + 1) * P, :], htok[n % 2]).then_inc(S[f"hst{n % 2}"], 16)
                for j in range(2):
                    pool.wait_ge(*S.at(f"hst{j}", 16 * len(T) // 2))
                barrier("pool", pool)

                def gather(e):
                    pool.indirect_dma_start(out=xg, out_offset=None, in_=h_dram,
                                            in_offset=bass.IndirectOffsetOnAxis(ap=idx[:, e:e + 1], axis=0)
                                            ).then_inc(S["gat"], 16)

                gather(0)
                for e in range(E):
                    if e + 1 < E:
                        pool.wait_ge(*S.at("xt", e + 1))
                        gather(e + 1)
                    if e == 1:
                        load_gates(l, 1)
                    elif e == 3 and l < DEPTH - 1:
                        load_for_layer(l + 1)
                    elif e == 3:
                        pool.dma_start(modbc[:, 0, 0:D], a["final_norm"].rearrange("(a d) -> a d", a=1)
                                       .to_broadcast([P, D])).then_inc(s_fn, 16)
                    if e:
                        pool.wait_ge(*S.at("ye", 2 * e))
                        pool.dma_start(y_dram[(e - 1) * CAP:e * CAP, :], ysb).then_inc(S["yst"], 16)
                pool.wait_ge(*S.at("yst", 16 * (E - 1)))
                pool.wait_ge(*S.at("ylast", 16))
                barrier("pool", pool)
                for n, i in enumerate(T):
                    for c, (dst, s) in enumerate(((y1[n], S[f"g0{n}"]), (y2[n], S[f"g1{n}"]))):
                        pool.indirect_dma_start(out=dst, out_offset=None, in_=y_dram,
                                                in_offset=bass.IndirectOffsetOnAxis(ap=row[:, c, n:n + 1], axis=0)
                                                ).then_inc(s, 16)
                pool.wait_ge(*S.at("f", len(T)))
                barrier("pool", pool)
                more_rounds("pool", pool, l)
            pool.wait_ge(s_fvar, 1)
            pool.tensor_tensor(small[:, 12:12 + NL], small[:, 8:8 + NL], cst("minus_half")[:, 0:NL], ALU.pow
                               ).then_inc(s_frs, 1)
            pool.wait_ge(s_out, 16 * NL)
            barrier("pool", pool)


_INS = ['x', 'c', 'ctx', 'c_ctx', 'w_mod', 'b_mod', 'norm_mix', 'norm_ffn', 'w_in', 'attn_sink', 'mla_q_norm', 'w_uq',
        'mla_kv_norm', 'w_ukv', 'w_o_a', 'w_o_b', 'w_out', 'w_router', 'router_bias', 'w_expert_gate', 'w_expert_up',
        'w_expert_down', 'final_norm']


def kernel(**inputs):
    import concourse.bacc as bacc
    from concourse.bass_utils import run_bass_kernel_spmd

    nc = bacc.Bacc("TRN2", target_bir_lowering=False, num_devices=1)
    arrays = {f"in_{n}": np.ascontiguousarray(inputs[n]) for n in _INS}
    args = {n: nc.dram_tensor(f"in_{n}", arrays[f"in_{n}"].shape, F32, kind="ExternalInput").ap() for n in _INS}
    arrays["tables"] = CONST
    tables = nc.dram_tensor("tables", CONST.shape, F32, kind="ExternalInput").ap()
    out = nc.dram_tensor("out", (1, SEQ, D), F32, kind="ExternalOutput").ap()
    trunk(nc, args, tables, out)
    r = run_bass_kernel_spmd(nc, [arrays], core_ids=[0])
    return r.results[0]["out"]
```
